# Optimizing a Trainium2 kernel written in Bass

```python
import jax, jax.numpy as jnp
from jax import lax
import numpy as np

D_MODEL = 1024
BATCH = 1
SEQ = 1024
DEPTH = 1

CHUNK = 64
MIX_WIDTH = D_MODEL
POOL_WIDTH = MIX_WIDTH // 2
POOL_WINDOWS = (2, 4, 8, 16)
POOL_GROUPS = len(POOL_WINDOWS)
POOL_GROUP_DIM = POOL_WIDTH // POOL_GROUPS
HGRN_WIDTH = MIX_WIDTH - POOL_WIDTH
HGRN_EXPAND = 128
HGRN_HEADS = HGRN_WIDTH // HGRN_EXPAND
HGRN_DK = HGRN_EXPAND
HGRN_DV = HGRN_WIDTH // HGRN_HEADS
IN_COLS = POOL_WIDTH + 4 * HGRN_WIDTH
D_FF = 2816
CONV_WIDTH = 3
LN_EPS = 1e-5
RMS_EPS = 1e-6
ALPHA = (2.0 * DEPTH) ** 0.25
BETA = (8.0 * DEPTH) ** -0.25


def layer_norm(x, g, b):
    xf = x.astype(jnp.float32)
    mu = jnp.mean(xf, axis=-1, keepdims=True)
    var = jnp.mean(jnp.square(xf - mu), axis=-1, keepdims=True)
    y = (xf - mu) * lax.rsqrt(var + LN_EPS)
    return (y * g + b).astype(x.dtype)

def pool_mixer(xp, pool_w, pool_scale):
    B, T, _ = xp.shape
    xf = xp.astype(jnp.float32)
    cs0 = jnp.pad(jnp.cumsum(xf, axis=1), ((0, 0), (1, 0), (0, 0)))
    pos = jnp.arange(1, T + 1, dtype=jnp.float32)
    outs = []
    for gi, w in enumerate(POOL_WINDOWS):
        sl = slice(gi * POOL_GROUP_DIM, (gi + 1) * POOL_GROUP_DIM)
        c = cs0[..., sl]
        lagged = jnp.pad(c, ((0, 0), (w - 1, 0), (0, 0)))[:, :T]
        mean = (c[:, 1:] - lagged) / jnp.minimum(pos, float(w))[None, :, None]
        d = (mean - xf[..., sl]).astype(xp.dtype)
        outs.append(jnp.einsum('btc,cd->btd', d, pool_w[gi]))
    return jnp.concatenate(outs, axis=-1) * pool_scale

def hgrn2_mixer(q, f_pre, i, g, lb, gnorm_w):
    B, T, _ = q.shape
    nC = T // CHUNK
    H = HGRN_HEADS
    lbf = lb.astype(jnp.float32)
    forget = lbf + (1.0 - lbf) * jax.nn.sigmoid(f_pre.astype(jnp.float32))
    log_f = jnp.log(forget)
    k = 1.0 - forget
    qf = jax.nn.silu(q.astype(jnp.float32))

    def to_chunks(t, d):
        return t.astype(jnp.float32).reshape(B, nC, CHUNK, H, d).transpose(1, 0, 3, 2, 4)

    qh, lfh, kh = to_chunks(qf, HGRN_DK), to_chunks(log_f, HGRN_DK), to_chunks(k, HGRN_DK)
    vh = to_chunks(i, HGRN_DV)
    causal = jnp.tril(jnp.ones((CHUNK, CHUNK), dtype=bool))

    def step(S, inp):
        qc, lfc, kc, vc = inp
        b = jnp.cumsum(lfc, axis=2)
        diff = b[:, :, :, None, :] - b[:, :, None, :, :]
        decay = jnp.exp(jnp.where(causal[:, :, None], diff, -jnp.inf))
        scores = jnp.einsum('bhtd,bhsd,bhtsd->bhts', qc, kc, decay)
        o = jnp.einsum('bhts,bhse->bhte', scores, vc) \
            + jnp.einsum('bhtd,bhde->bhte', qc * jnp.exp(b), S)
        b_last = b[:, :, -1:, :]
        S = jnp.exp(b_last)[:, :, 0, :, None] * S \
            + jnp.einsum('bhsd,bhse->bhde', kc * jnp.exp(b_last - b), vc)
        return S, o

    S0 = jnp.zeros((B, H, HGRN_DK, HGRN_DV), jnp.float32)
    _, o = lax.scan(step, S0, (qh, lfh, kh, vh))
    o = o.transpose(1, 0, 3, 2, 4).reshape(B, T, H, HGRN_DV)
    o = o * lax.rsqrt(jnp.mean(jnp.square(o), axis=-1, keepdims=True) + RMS_EPS) * gnorm_w
    o = o * jax.nn.silu(g.astype(jnp.float32).reshape(B, T, H, HGRN_DV))
    return o.reshape(B, T, HGRN_WIDTH).astype(q.dtype)

def conv_gated_mlp(h, w_up, conv_w, conv_b, w_down):
    u = jnp.einsum('btd,df->btf', h, w_up)
    T = u.shape[1]
    up = jnp.pad(u, ((0, 0), (CONV_WIDTH - 1, 0), (0, 0)))
    uc = conv_b + sum(conv_w[j] * up[:, j:j + T] for j in range(CONV_WIDTH))
    a, v = jnp.split(uc, 2, axis=-1)
    return jnp.einsum('btf,fd->btd', jax.nn.gelu(a) * v, w_down)

def first_inputs(seed: int = 0) -> dict:
    key = jax.random.key(seed)
    ks = jax.random.split(key, 16)
    n = jax.random.normal
    f32 = jnp.float32
    return {
        "x": n(ks[0], (BATCH, SEQ, D_MODEL), f32),
        "w_in": n(ks[1], (DEPTH, D_MODEL, IN_COLS), f32) * D_MODEL ** -0.5,
        "pool_w": n(ks[2], (DEPTH, POOL_GROUPS, POOL_GROUP_DIM, POOL_GROUP_DIM), f32) * POOL_GROUP_DIM ** -0.5,
        "pool_scale": 1.0 + 0.02 * n(ks[3], (DEPTH, POOL_WIDTH), f32),
        "hgrn_lb": n(ks[4], (DEPTH + 1, HGRN_WIDTH), f32),
        "hgrn_gnorm": 1.0 + 0.02 * n(ks[5], (DEPTH, HGRN_DV), f32),
        "w_out": n(ks[6], (DEPTH, MIX_WIDTH, D_MODEL), f32) * (MIX_WIDTH ** -0.5 * BETA),
        "ln1_g": 1.0 + 0.02 * n(ks[7], (DEPTH, D_MODEL), f32),
        "ln1_b": 0.02 * n(ks[8], (DEPTH, D_MODEL), f32),
        "w_up": n(ks[9], (DEPTH, D_MODEL, 2 * D_FF), f32) * D_MODEL ** -0.5,
        "conv_w": n(ks[10], (DEPTH, CONV_WIDTH, 2 * D_FF), f32) * CONV_WIDTH ** -0.5,
        "conv_b": 0.02 * n(ks[11], (DEPTH, 2 * D_FF), f32),
        "w_down": n(ks[12], (DEPTH, D_FF, D_MODEL), f32) * (D_FF ** -0.5 * BETA),
        "ln2_g": 1.0 + 0.02 * n(ks[13], (DEPTH, D_MODEL), f32),
        "ln2_b": 0.02 * n(ks[14], (DEPTH, D_MODEL), f32),
    }

def first_block(x, w_in, pool_w, pool_scale, hgrn_lb, hgrn_gnorm, w_out, ln1_g, ln1_b,
              w_up, conv_w, conv_b, w_down, ln2_g, ln2_b):
    lb_all = jnp.cumsum(jax.nn.softmax(hgrn_lb.astype(jnp.float32), axis=0), axis=0)
    splits = [POOL_WIDTH, POOL_WIDTH + HGRN_WIDTH, POOL_WIDTH + 2 * HGRN_WIDTH,
              POOL_WIDTH + 3 * HGRN_WIDTH]
    h = x
    for l in range(DEPTH):
        proj = jnp.einsum('btd,dc->btc', h, w_in[l])
        xp, q, f_pre, i, g = jnp.split(proj, splits, axis=-1)
        y_a = pool_mixer(xp, pool_w[l], pool_scale[l])
        y_b = hgrn2_mixer(q, f_pre, i, g, lb_all[l], hgrn_gnorm[l])
        mix = jnp.einsum('btc,cd->btd', jnp.concatenate([y_a, y_b], axis=-1), w_out[l])
        h = layer_norm(ALPHA * h + mix, ln1_g[l], ln1_b[l])
        ffn = conv_gated_mlp(h, w_up[l], conv_w[l], conv_b[l], w_down[l])
        h = layer_norm(ALPHA * h + ffn, ln2_g[l], ln2_b[l])
    return h


_first_inputs = first_inputs


def first_inputs(seed=0):
    import zlib

    import numpy as np

    out = dict(_first_inputs(seed))
    spreads = {}
    factors = {'pool_scale': 8.0,
     'hgrn_lb': 2.865,
     'hgrn_gnorm': 8.0,
     'ln1_g': 2.728,
     'ln1_b': 2.846,
     'conv_b': 6.511,
     'ln2_g': 2.739,
     'ln2_b': 2.874}
    for name, (base, spread) in spreads.items():
        noise = np.random.default_rng([zlib.crc32(name.encode()), seed]).standard_normal(out[name].shape)
        drawn = base * np.exp(spread * noise) if base else spread * noise
        out[name] = __import__('jax').numpy.asarray(drawn.astype(out[name].dtype))
    for name, factor in factors.items():
        out[name] = (out[name] * factor).astype(out[name].dtype)
    return out


_narrow_inputs = first_inputs


def first_inputs(seed=0):

    out = dict(_narrow_inputs(seed))
    wider = {'pool_scale': 3.52, 'hgrn_gnorm': 4.19, 'ln2_g': 3.08, 'ln2_b': 3.08}
    for name, times in wider.items():
        mean = out[name].mean()
        out[name] = (mean + times * (out[name] - mean)).astype(out[name].dtype)
    return out


MIX_WIDTH_2 = D_MODEL
ATTN_WIDTH = MIX_WIDTH_2 // 2
CONV_WIDTH_2 = MIX_WIDTH_2 - ATTN_WIDTH
HEAD_DIM = 64
N_ATTN_HEADS = ATTN_WIDTH // HEAD_DIM
N_CONV_GROUPS = CONV_WIDTH_2 // HEAD_DIM
CONV_KERNEL = 31
D_FF_2 = 4 * D_MODEL
Q_BLOCK = 128
EPS = 1e-6
IN_COLS_2 = 3 * ATTN_WIDTH + 2 * CONV_WIDTH_2 + N_ATTN_HEADS
SPLITS = (ATTN_WIDTH, 2 * ATTN_WIDTH, 3 * ATTN_WIDTH,
          3 * ATTN_WIDTH + CONV_WIDTH_2, 3 * ATTN_WIDTH + 2 * CONV_WIDTH_2)


def rmsnorm(x, g):
    xf = x.astype(jnp.float32)
    y = xf * lax.rsqrt(jnp.mean(xf * xf, axis=-1, keepdims=True) + EPS)
    return (y * g.astype(jnp.float32)).astype(x.dtype)

def layernorm(x, g, b):
    xf = x.astype(jnp.float32)
    mu = jnp.mean(xf, axis=-1, keepdims=True)
    xc = xf - mu
    y = xc * lax.rsqrt(jnp.mean(xc * xc, axis=-1, keepdims=True) + EPS)
    return (y * g.astype(jnp.float32) + b.astype(jnp.float32)).astype(x.dtype)

def headwise_rmsnorm(y, g, n_groups):
    B, S, _ = y.shape
    yh = y.reshape(B, S, n_groups, HEAD_DIM)
    out = rmsnorm(yh, g.reshape(n_groups, HEAD_DIM))
    return out.reshape(B, S, n_groups * HEAD_DIM)

def fox_attention(q, k, v, log_f):
    B, S, H, Dh = q.shape
    scale = Dh ** -0.5
    qh = jnp.transpose(q, (0, 2, 1, 3))
    kh = jnp.transpose(k, (0, 2, 1, 3))
    vh = jnp.transpose(v, (0, 2, 1, 3))
    c = jnp.transpose(jnp.cumsum(log_f.astype(jnp.float32), axis=1), (0, 2, 1))
    outs = []
    for blk in range(S // Q_BLOCK):
        q0 = blk * Q_BLOCK
        q1 = q0 + Q_BLOCK
        qb = qh[:, :, q0:q1]
        kb = kh[:, :, :q1]
        vb = vh[:, :, :q1]
        s = jnp.einsum('bhqd,bhkd->bhqk', qb, kb, preferred_element_type=jnp.float32) * scale
        s = s + c[:, :, q0:q1, None] - c[:, :, None, :q1]
        qpos = q0 + jnp.arange(Q_BLOCK)
        kpos = jnp.arange(q1)
        s = jnp.where(kpos[None, :] <= qpos[:, None], s, -jnp.inf)
        p = jax.nn.softmax(s, axis=-1)
        outs.append(jnp.einsum('bhqk,bhkd->bhqd', p.astype(vb.dtype), vb))
    o = jnp.concatenate(outs, axis=2)
    return jnp.transpose(o, (0, 2, 1, 3))

def causal_depthwise_conv(u, w, b):
    K, C = w.shape
    y = lax.conv_general_dilated(
        u, w[:, None, :].astype(u.dtype), window_strides=(1,), padding=[(K - 1, 0)],
        dimension_numbers=('NWC', 'WIO', 'NWC'), feature_group_count=C)
    return y + b.astype(u.dtype)

def second_inputs(seed: int = 0) -> dict:
    key = jax.random.key(seed)
    ks = jax.random.split(key, 20)
    f32 = jnp.float32
    L = DEPTH
    nrm = lambda k, shape, s: jax.random.normal(k, shape, f32) * s
    x = jax.random.normal(ks[0], (BATCH, SEQ, D_MODEL), f32)
    norm_mix_g = 1.0 + nrm(ks[1], (L, D_MODEL), 0.02)
    w_in = nrm(ks[2], (L, D_MODEL, IN_COLS_2), D_MODEL ** -0.5)
    b_forget = jnp.linspace(1.0, 4.0, N_ATTN_HEADS, dtype=f32)[None, :] + nrm(ks[3], (L, N_ATTN_HEADS), 0.1)
    conv_dw_w = nrm(ks[4], (L, CONV_KERNEL, CONV_WIDTH_2), CONV_KERNEL ** -0.5)
    conv_dw_b = nrm(ks[5], (L, CONV_WIDTH_2), 0.02)
    conv_ln_g = 1.0 + nrm(ks[6], (L, CONV_WIDTH_2), 0.02)
    conv_ln_b = nrm(ks[7], (L, CONV_WIDTH_2), 0.02)
    w_conv_pw = nrm(ks[8], (L, CONV_WIDTH_2, CONV_WIDTH_2), CONV_WIDTH_2 ** -0.5)
    b_conv_pw = nrm(ks[9], (L, CONV_WIDTH_2), 0.02)
    attn_out_g = 1.0 + nrm(ks[10], (L, ATTN_WIDTH), 0.02)
    conv_out_g = 1.0 + nrm(ks[11], (L, CONV_WIDTH_2), 0.02)
    w_out = nrm(ks[12], (L, MIX_WIDTH_2, D_MODEL), MIX_WIDTH_2 ** -0.5)
    norm_ffn_g = 1.0 + nrm(ks[13], (L, D_MODEL), 0.02)
    w_ffn_up = nrm(ks[14], (L, D_MODEL, D_FF_2), D_MODEL ** -0.5)
    w_ffn_down = nrm(ks[15], (L, D_FF_2, D_MODEL), D_FF_2 ** -0.5)
    norm_final_g = 1.0 + nrm(ks[16], (D_MODEL,), 0.02)
    return {"x": x, "norm_mix_g": norm_mix_g, "w_in": w_in, "b_forget": b_forget,
            "conv_dw_w": conv_dw_w, "conv_dw_b": conv_dw_b, "conv_ln_g": conv_ln_g,
            "conv_ln_b": conv_ln_b, "w_conv_pw": w_conv_pw, "b_conv_pw": b_conv_pw,
            "attn_out_g": attn_out_g, "conv_out_g": conv_out_g, "w_out": w_out,
            "norm_ffn_g": norm_ffn_g, "w_ffn_up": w_ffn_up, "w_ffn_down": w_ffn_down,
            "norm_final_g": norm_final_g}

def second_block(x, norm_mix_g, w_in, b_forget, conv_dw_w, conv_dw_b, conv_ln_g, conv_ln_b,
              w_conv_pw, b_conv_pw, attn_out_g, conv_out_g, w_out, norm_ffn_g,
              w_ffn_up, w_ffn_down, norm_final_g):
    B, S, _ = x.shape
    for l in range(DEPTH):
        h = rmsnorm(x, norm_mix_g[l])
        proj = h @ w_in[l]
        q, k, v, ga, gb, f_logit = jnp.split(proj, SPLITS, axis=-1)
        log_f = jax.nn.log_sigmoid(f_logit.astype(jnp.float32) + b_forget[l].astype(jnp.float32))
        hs = (B, S, N_ATTN_HEADS, HEAD_DIM)
        attn = fox_attention(q.reshape(hs), k.reshape(hs), v.reshape(hs), log_f)
        attn = headwise_rmsnorm(attn.reshape(B, S, ATTN_WIDTH), attn_out_g[l], N_ATTN_HEADS)
        u = ga * jax.nn.sigmoid(gb)
        u = causal_depthwise_conv(u, conv_dw_w[l], conv_dw_b[l])
        u = jax.nn.silu(layernorm(u, conv_ln_g[l], conv_ln_b[l]))
        u = u @ w_conv_pw[l] + b_conv_pw[l]
        conv = headwise_rmsnorm(u, conv_out_g[l], N_CONV_GROUPS)
        x = x + jnp.concatenate([attn, conv], axis=-1) @ w_out[l]
        h = rmsnorm(x, norm_ffn_g[l])
        x = x + jnp.square(jax.nn.relu(h @ w_ffn_up[l])) @ w_ffn_down[l]
    return rmsnorm(x, norm_final_g)


_first_inputs_2 = second_inputs


def second_inputs(seed=0):
    import zlib

    import numpy as np

    out = dict(_first_inputs_2(seed))
    spreads = {}
    factors = {'conv_ln_g': 4.359,
     'conv_ln_b': 5.491,
     'b_conv_pw': 3.215,
     'attn_out_g': 5.107,
     'conv_out_g': 5.098,
     'norm_ffn_g': 3.626,
     'norm_final_g': 2.868}
    for name, (base, spread) in spreads.items():
        noise = np.random.default_rng([zlib.crc32(name.encode()), seed]).standard_normal(out[name].shape)
        drawn = base * np.exp(spread * noise) if base else spread * noise
        out[name] = __import__('jax').numpy.asarray(drawn.astype(out[name].dtype))
    for name, factor in factors.items():
        out[name] = (out[name] * factor).astype(out[name].dtype)
    return out


_narrow_inputs_2 = second_inputs


def second_inputs(seed=0):

    out = dict(_narrow_inputs_2(seed))
    wider = {'conv_ln_g': 3.89,
     'conv_ln_b': 3.31,
     'b_conv_pw': 3.9,
     'attn_out_g': 3.88,
     'conv_out_g': 3.87,
     'norm_final_g': 3.23}
    for name, times in wider.items():
        mean = out[name].mean()
        out[name] = (mean + times * (out[name] - mean)).astype(out[name].dtype)
    return out


CTX_LEN = 256
GRID_W = 64
D_MIX = D_MODEL
D_GMLP = D_MIX // 2
G_A = 4
GA_DIM = D_GMLP // G_A
CHUNK_A = 2 * GRID_W
D_MLSTM = D_MIX - D_GMLP
H_B = 4
HV = D_MLSTM // H_B
HK = HV // 2
D_QK = H_B * HK
CONV_W = 3
CHUNK_B = 128
N_GATES = 4 * H_B
D_IN = 2 * D_GMLP + 2 * D_QK + 2 * D_MLSTM + N_GATES
D_FF_3 = 4 * D_MODEL
ALPHA_3 = (2 * DEPTH) ** 0.25
BETA_3 = (8 * DEPTH) ** -0.25


def _ln_stats(x):
    xf = x.astype(jnp.float32)
    mu = jnp.mean(xf, axis=-1, keepdims=True)
    var = jnp.mean(jnp.square(xf - mu), axis=-1, keepdims=True)
    return (xf - mu) * lax.rsqrt(var + LN_EPS)

def layer_norm_3(x, g, b):
    return (_ln_stats(x) * g + b).astype(x.dtype)

def modulate(x, shift, scale):
    return _ln_stats(x).astype(x.dtype) * (1 + scale) + shift

def ada_split(cond, w_ada, b_ada):
    return jnp.split(jax.nn.silu(cond) @ w_ada + b_ada, 6, axis=-1)

def split_proj(p):
    bounds = [D_GMLP, 2 * D_GMLP, 2 * D_GMLP + D_QK, 2 * D_GMLP + 2 * D_QK,
              2 * D_GMLP + 2 * D_QK + D_MLSTM, 2 * D_GMLP + 2 * D_QK + 2 * D_MLSTM]
    return jnp.split(p, bounds, axis=-1)

def spatial_gating(u, v, w_s, b_s, g_v, b_v):
    bsz, s, _ = v.shape
    vc = layer_norm_3(v, g_v, b_v).reshape(bsz, s // CHUNK_A, CHUNK_A, G_A, GA_DIM)
    mixed = jnp.einsum('gts,bnsgd->bntgd', w_s, vc) + b_s.T[:, :, None]
    return u * mixed.reshape(bsz, s, D_GMLP)

def short_conv(x, w):
    pad = CONV_W // 2
    return lax.conv_general_dilated(
        x, w[:, None, :], window_strides=(1,), padding=[(pad, pad)],
        dimension_numbers=('NWC', 'WIO', 'NWC'), feature_group_count=x.shape[-1])

def mlstm_inputs(q, k, vv, gates, conv_w, b_gates):
    bsz, s, _ = q.shape
    qk = jax.nn.silu(short_conv(jnp.concatenate([q, k], axis=-1), conv_w))
    q, k = jnp.split(qk, 2, axis=-1)
    heads = lambda a, d: a.reshape(bsz, s, H_B, d).transpose(0, 2, 1, 3)
    g = (gates + b_gates).reshape(bsz, s, 4, H_B).transpose(2, 0, 3, 1)
    return heads(q, HK), heads(k, HK), heads(vv, HV), g

def mlstm_chunkwise(q, k, v, ig, fg, state):
    bsz, nh, s, _ = q.shape
    nc = s // CHUNK_B
    f32 = jnp.float32
    q = q.astype(f32) * (HK ** -0.5)
    k = k.astype(f32)
    v = v.astype(f32)
    ig = ig.astype(f32)
    logf = jax.nn.log_sigmoid(fg.astype(f32))

    def to_chunks(a):
        return jnp.moveaxis(a.reshape(bsz, nh, nc, CHUNK_B, *a.shape[3:]), 2, 0)

    tri = jnp.tril(jnp.ones((CHUNK_B, CHUNK_B), dtype=bool))

    def step(carry, xs_c):
        c0, n0, m0 = carry
        qc, kc, vc, ic, lfc = xs_c
        b = jnp.cumsum(lfc, axis=-1)
        dmat = jnp.where(tri, b[..., :, None] - b[..., None, :] + ic[..., None, :], -jnp.inf)
        inter = b + m0[..., None]
        m = jnp.maximum(inter, jnp.max(dmat, axis=-1))
        w_intra = jnp.exp(dmat - m[..., None])
        w_inter = jnp.exp(inter - m)
        scores = jnp.einsum('bhtk,bhsk->bhts', qc, kc) * w_intra
        num = (jnp.einsum('bhts,bhsv->bhtv', scores, vc)
               + w_inter[..., None] * jnp.einsum('bhtk,bhkv->bhtv', qc, c0))
        den = jnp.sum(scores, axis=-1) + w_inter * jnp.einsum('bhtk,bhk->bht', qc, n0)
        h = num / jnp.maximum(jnp.abs(den), jnp.exp(-m))[..., None]
        b_last = b[..., -1]
        dec = b_last[..., None] - b + ic
        m_new = jnp.maximum(b_last + m0, jnp.max(dec, axis=-1))
        w_s = jnp.exp(dec - m_new[..., None])
        carry_w = jnp.exp(b_last + m0 - m_new)
        c_new = carry_w[..., None, None] * c0 + jnp.einsum('bhs,bhsk,bhsv->bhkv', w_s, kc, vc)
        n_new = carry_w[..., None] * n0 + jnp.einsum('bhs,bhsk->bhk', w_s, kc)
        return (c_new, n_new, m_new), h

    xs = (to_chunks(q), to_chunks(k), to_chunks(v), to_chunks(ig), to_chunks(logf))
    state, hs = lax.scan(step, state, xs)
    h = jnp.moveaxis(hs, 0, 2).reshape(bsz, nh, s, HV)
    return h, state

def mlstm_bidirectional(ctx_in, lat_in):
    qc, kc, vc, gc = ctx_in
    ql, kl, vl, gl = lat_in
    bsz = ql.shape[0]
    f32 = jnp.float32
    zero = (jnp.zeros((bsz, H_B, HK, HV), f32), jnp.zeros((bsz, H_B, HK), f32), jnp.zeros((bsz, H_B), f32))
    flip = lambda a: jnp.flip(a, axis=2)
    hc_f, st_f = mlstm_chunkwise(qc, kc, vc, gc[0], gc[1], zero)
    hl_f, _ = mlstm_chunkwise(ql, kl, vl, gl[0], gl[1], st_f)
    hc_b, st_b = mlstm_chunkwise(flip(qc), flip(kc), flip(vc), flip(gc[2]), flip(gc[3]), zero)
    hl_b, _ = mlstm_chunkwise(flip(ql), flip(kl), flip(vl), flip(gl[2]), flip(gl[3]), st_b)
    return hc_f + flip(hc_b), hl_f + flip(hl_b)

def head_norm(h, g):
    bsz, nh, s, dv = h.shape
    y = _ln_stats(h).transpose(0, 2, 1, 3).reshape(bsz, s, nh * dv)
    return y * g

def mixer_output(u, v, h_b, o, w_s, b_s, ln_v_g, ln_v_b, hn_g, w_out):
    y_a = spatial_gating(u, v, w_s, b_s, ln_v_g, ln_v_b)
    y_b = head_norm(h_b, hn_g).astype(o.dtype) * jax.nn.sigmoid(o)
    return jnp.concatenate([y_a, y_b], axis=-1) @ w_out

def channel_mlp(h, w1, b1, w2, b2):
    return jnp.square(jax.nn.relu(h @ w1 + b1)) @ w2 + b2

def deepnorm_update(x, y, gate, g, b):
    return layer_norm_3(ALPHA_3 * x + gate * y, g, b)

def third_inputs(seed: int = 0) -> dict:
    key = jax.random.key(seed)
    ks = jax.random.split(key, 28)
    nrm = lambda k, shape, s: jax.random.normal(k, shape, jnp.float32) * s
    L = DEPTH
    f_bias = jnp.linspace(3.0, 6.0, H_B, dtype=jnp.float32)
    b_gates = jnp.concatenate([
        nrm(ks[10], (L, H_B), 0.1), f_bias + nrm(ks[11], (L, H_B), 0.1),
        nrm(ks[12], (L, H_B), 0.1), f_bias + nrm(ks[13], (L, H_B), 0.1)], axis=-1)
    return {
        "x": nrm(ks[0], (BATCH, SEQ, D_MODEL), 1.0),
        "c": nrm(ks[1], (BATCH, D_MODEL), 1.0),
        "ctx": nrm(ks[2], (BATCH, CTX_LEN, D_MODEL), 1.0),
        "c_ctx": nrm(ks[3], (D_MODEL,), 1.0),
        "w_ada": nrm(ks[4], (L, D_MODEL, 6 * D_MODEL), D_MODEL ** -0.5),
        "b_ada": nrm(ks[5], (L, 6 * D_MODEL), 0.01),
        "w_in": nrm(ks[6], (L, D_MODEL, D_IN), D_MODEL ** -0.5),
        "w_s": nrm(ks[7], (L, G_A, CHUNK_A, CHUNK_A), CHUNK_A ** -0.5),
        "b_s": 1.0 + nrm(ks[8], (L, G_A, CHUNK_A), 0.01),
        "ln_v_g": 1.0 + nrm(ks[9], (L, D_GMLP), 0.01),
        "ln_v_b": nrm(ks[14], (L, D_GMLP), 0.01),
        "conv_qk": nrm(ks[15], (L, CONV_W, 2 * D_QK), CONV_W ** -0.5),
        "b_gates": b_gates,
        "hn_g": 1.0 + nrm(ks[16], (L, D_MLSTM), 0.01),
        "w_out": nrm(ks[17], (L, D_MIX, D_MODEL), BETA_3 * D_MIX ** -0.5),
        "ln1_g": 1.0 + nrm(ks[18], (L, D_MODEL), 0.01),
        "ln1_b": nrm(ks[19], (L, D_MODEL), 0.01),
        "w1": nrm(ks[20], (L, D_MODEL, D_FF_3), D_MODEL ** -0.5),
        "b1": nrm(ks[21], (L, D_FF_3), 0.01),
        "w2": nrm(ks[22], (L, D_FF_3, D_MODEL), BETA_3 * D_FF_3 ** -0.5),
        "b2": nrm(ks[23], (L, D_MODEL), 0.01),
        "ln2_g": 1.0 + nrm(ks[24], (L, D_MODEL), 0.01),
        "ln2_b": nrm(ks[25], (L, D_MODEL), 0.01),
    }

def third_block(x, c, ctx, c_ctx, w_ada, b_ada, w_in, w_s, b_s, ln_v_g, ln_v_b, conv_qk, b_gates, hn_g,
              w_out, ln1_g, ln1_b, w1, b1, w2, b2, ln2_g, ln2_b):
    xc = ctx
    for l in range(DEPTH):
        sh1, sc1, g1, sh2, sc2, g2 = [m[:, None, :] for m in ada_split(c, w_ada[l], b_ada[l])]
        csh1, csc1, cg1, csh2, csc2, cg2 = ada_split(c_ctx, w_ada[l], b_ada[l])

        u_l, v_l, q_l, k_l, vv_l, o_l, gt_l = split_proj(modulate(x, sh1, sc1) @ w_in[l])
        u_c, v_c, q_c, k_c, vv_c, o_c, gt_c = split_proj(modulate(xc, csh1, csc1) @ w_in[l])

        hb_c, hb_l = mlstm_bidirectional(
            mlstm_inputs(q_c, k_c, vv_c, gt_c, conv_qk[l], b_gates[l]),
            mlstm_inputs(q_l, k_l, vv_l, gt_l, conv_qk[l], b_gates[l]))

        y_l = mixer_output(u_l, v_l, hb_l, o_l, w_s[l], b_s[l], ln_v_g[l], ln_v_b[l], hn_g[l], w_out[l])
        x_new = deepnorm_update(x, y_l, g1, ln1_g[l], ln1_b[l])
        x_new = deepnorm_update(x_new, channel_mlp(modulate(x_new, sh2, sc2), w1[l], b1[l], w2[l], b2[l]),
                                g2, ln2_g[l], ln2_b[l])

        if l < DEPTH - 1:
            y_c = mixer_output(u_c, v_c, hb_c, o_c, w_s[l], b_s[l], ln_v_g[l], ln_v_b[l], hn_g[l], w_out[l])
            xc = deepnorm_update(xc, y_c, cg1, ln1_g[l], ln1_b[l])
            xc = deepnorm_update(xc, channel_mlp(modulate(xc, csh2, csc2), w1[l], b1[l], w2[l], b2[l]),
                                 cg2, ln2_g[l], ln2_b[l])
        x = x_new
    return x


_first_inputs_3 = third_inputs


def third_inputs(seed=0):
    import zlib

    import numpy as np

    out = dict(_first_inputs_3(seed))
    spreads = {}
    factors = {'ctx': 5.289,
     'b_ada': 3.928,
     'b_s': 8.0,
     'ln_v_g': 8.0,
     'ln_v_b': 8.0,
     'hn_g': 8.0,
     'ln1_g': 5.768,
     'ln1_b': 5.735,
     'b1': 8.0,
     'b2': 8.0,
     'ln2_g': 5.662,
     'ln2_b': 5.61}
    for name, (base, spread) in spreads.items():
        noise = np.random.default_rng([zlib.crc32(name.encode()), seed]).standard_normal(out[name].shape)
        drawn = base * np.exp(spread * noise) if base else spread * noise
        out[name] = __import__('jax').numpy.asarray(drawn.astype(out[name].dtype))
    for name, factor in factors.items():
        out[name] = (out[name] * factor).astype(out[name].dtype)
    return out


_narrow_inputs_3 = third_inputs


def third_inputs(seed=0):

    out = dict(_narrow_inputs_3(seed))
    wider = {'b_s': 10.87,
     'ln_v_g': 9.87,
     'ln_v_b': 10.3,
     'hn_g': 12.0,
     'ln1_g': 6.68,
     'ln1_b': 6.46,
     'b1': 7.36,
     'b2': 8.34,
     'ln2_g': 6.3,
     'ln2_b': 6.37}
    for name, times in wider.items():
        mean = out[name].mean()
        out[name] = (mean + times * (out[name] - mean)).astype(out[name].dtype)
    return out


def setup_inputs(seed=0):
    out = dict(first_inputs(seed))
    for name, value in second_inputs(seed + 1).items():
        if name != "x":
            out[name + "_2"] = value
    for name, value in third_inputs(seed + 2).items():
        if name != "x":
            out[name + "_3"] = value
    return out


def reference(
    x, w_in, pool_w, pool_scale, hgrn_lb, hgrn_gnorm, w_out, ln1_g, ln1_b, w_up, conv_w, conv_b,
    w_down, ln2_g, ln2_b, norm_mix_g_2, w_in_2, b_forget_2, conv_dw_w_2, conv_dw_b_2,
    conv_ln_g_2, conv_ln_b_2, w_conv_pw_2, b_conv_pw_2, attn_out_g_2, conv_out_g_2, w_out_2,
    norm_ffn_g_2, w_ffn_up_2, w_ffn_down_2, norm_final_g_2, c_3, ctx_3, c_ctx_3, w_ada_3,
    b_ada_3, w_in_3, w_s_3, b_s_3, ln_v_g_3, ln_v_b_3, conv_qk_3, b_gates_3, hn_g_3, w_out_3,
    ln1_g_3, ln1_b_3, w1_3, b1_3, w2_3, b2_3, ln2_g_3, ln2_b_3,
):
    x = first_block(
        x, w_in, pool_w, pool_scale, hgrn_lb, hgrn_gnorm, w_out, ln1_g, ln1_b, w_up, conv_w,
        conv_b, w_down, ln2_g, ln2_b,
    )
    x = second_block(
        x, norm_mix_g_2, w_in_2, b_forget_2, conv_dw_w_2, conv_dw_b_2, conv_ln_g_2, conv_ln_b_2,
        w_conv_pw_2, b_conv_pw_2, attn_out_g_2, conv_out_g_2, w_out_2, norm_ffn_g_2, w_ffn_up_2,
        w_ffn_down_2, norm_final_g_2,
    )
    return third_block(
        x, c_3, ctx_3, c_ctx_3, w_ada_3, b_ada_3, w_in_3, w_s_3, b_s_3, ln_v_g_3, ln_v_b_3,
        conv_qk_3, b_gates_3, hn_g_3, w_out_3, ln1_g_3, ln1_b_3, w1_3, b1_3, w2_3, b2_3,
        ln2_g_3, ln2_b_3,
    )


_drawn_inputs = setup_inputs


def setup_inputs(seed=0):
    import zlib

    import numpy as np

    out = dict(_drawn_inputs(seed))
    spreads = {}
    factors = {}
    for name, (base, spread) in spreads.items():
        noise = np.random.default_rng([zlib.crc32(name.encode()), seed]).standard_normal(out[name].shape)
        drawn = base * np.exp(spread * noise) if base else spread * noise
        out[name] = __import__('jax').numpy.asarray(drawn.astype(out[name].dtype))
    for name, factor in factors.items():
        out[name] = (out[name] * factor).astype(out[name].dtype)
    return out
```

```python
from contextlib import ExitStack, contextmanager

import numpy as np

import concourse.bass as bass
from concourse import mybir
from concourse.alu_op_type import AluOpType as ALU

ACT = mybir.ActivationFunctionType
F32 = mybir.dt.float32
F32R = mybir.dt.float32r
AX_X = mybir.AxisListType.X
ds = bass.ds

P = 128
D = 1024
T = 1024
KT = D // P
HALF = 512
SLAB = 2048
ALPHA = 2.0 ** 0.25
LN_EPS, RMS_EPS = 1e-5, 1e-6
LEVELS = 7
CH = 128
NC_ = T // CH
CTX = 256
TT = T + CTX


def param_spec():
    return [
        ("pool_scale", 4), ("hgrn_lb", 8), ("hgrn_gnorm", 1), ("ln1_g", 8), ("ln1_b", 8),
        ("conv_w", 3 * 44), ("conv_b", 44), ("ln2_g", 8), ("ln2_b", 8),
        ("norm_mix_g_2", 8), ("conv_dw_w_2", 31 * 4), ("conv_dw_b_2", 4), ("conv_ln_g_2", 4),
        ("conv_ln_b_2", 4), ("b_conv_pw_2", 4), ("attn_out_g_2", 4), ("conv_out_g_2", 4),
        ("norm_ffn_g_2", 8), ("norm_final_g_2", 8),
        ("c_3", 8), ("c_ctx_3", 8), ("b_ada_3", 48), ("ln_v_g_3", 4), ("ln_v_b_3", 4),
        ("conv_qk_3", 3 * 4), ("hn_g_3", 4), ("ln1_g_3", 8), ("ln1_b_3", 8), ("b1_3", 32),
        ("b2_3", 8), ("ln2_g_3", 8), ("ln2_b_3", 8),
    ]


def param_columns():
    at, n = {}, 0
    for name, width in param_spec():
        at[name] = (n, width)
        n += width
    return at, n


class Core:

    def __init__(self, nc, ctx, inputs, out):
        self.nc, self.inp, self.out = nc, inputs, out

        def sb(name, shape, dt=F32):
            return ctx.enter_context(nc.sbuf_tensor(name, shape, dt))

        base = nc.sbuf_base + -nc.sbuf_base % 32
        sb("arena", [P, 48, T])

        def over(name, first, shape, dt=F32):
            return nc.alloc_sbuf_tensor_at(name, shape, dt, offset=base + first * T * 4)

        self.X = over("residual", 0, [P, KT, T])
        self.H = over("gemm_input", 8, [P, KT, T])
        self.M = over("mixer", 16, [P, 20, T])
        self.T = over("scratch", 36, [P, 4, T])
        self.W = over("weight_slots", 40, [P, 4, SLAB])
        self.XR = over("residual_r", 0, [P, KT, T], F32R)
        self.HR = over("gemm_input_r", 8, [P, KT, T], F32R)
        self.MR = over("mixer_r", 28, [P, KT, T], F32R)
        self.hidR = over("hidden_r", 16, [P, 8, T], F32R)
        self.WR = over("weights_r", 44, [P, 4, T], F32R)
        self.downR = over("down_r", 36, [P, 4, T], F32R)
        self.down1R = over("down1_r", 26, [P, 2, T], F32R)
        self.spill = nc.dram_tensor("residual_spill", (P, KT, T), F32, kind="Internal").ap()
        self.par = sb("params", [P, param_columns()[1]])
        self.ident = sb("ident", [P, P])
        self.masks = sb("masks", [P, LEVELS + 2, P])
        self.ones_d = sb("ones_d", [P, P])
        self.ones = sb("ones", [P, P])
        self.small = sb("small", [P, 64])
        self.group_ones = sb("group_ones", [P, P])
        self.from_below, self.from_above = self.masks[:, LEVELS, :], self.masks[:, LEVELS + 1, :]
        self.rows = sb("rows", [P, TT])
        self.ada = sb("ada", [P, 96])
        self.gate_bias = sb("gate_bias", [P, 8])
        self.gate_tmp = sb("v_rstd", [P, 8])
        self.row_par = sb("row_params", [P, 4])
        self.ones_h = sb("ones_half", [P, P])
        self.PS = ctx.enter_context(nc.psum_tensor("psum", [P, 8, 512], F32))
        self.landed = [ctx.enter_context(nc.semaphore(f"slab_landed_{i}")) for i in range(4)]
        self.loads = [0] * 4
        self.retired, self.stages = [], 0

    def vec(self, name, j=0, n=1):
        at = param_columns()[0][name][0]
        return self.par[:, at + j:at + j + n]

    def mask(self, level):
        return self.masks[:, level:level + 1, :].to_broadcast([P, NC_, P])

    @contextmanager
    def stage(self, *names):
        nc = self.nc
        self.stages += 1
        sems = [nc.alloc_semaphore(name=f"{n}_{self.stages}") for n in names]
        retired, self.retired = self.retired, sems
        with nc.Block() as block:
            if retired:
                @block.gpsimd
                def _(pool):
                    for s in retired:
                        pool.sem_clear(s)

            yield (block, *sems)
        for s in retired:
            nc.release_semaphore(s)

    def slab(self, name, i, n=1):
        w = self.inp[name]
        if n == 1:
            return w[ds(i * P, P), :]
        return w[ds(i * P, P), :]

    def load(self, sp, slot, name, i):
        w = self.inp[name]
        width = w.shape[1]
        dst = self.W[:, slot, 0:width] if width <= SLAB else self.W[:, slot:slot + 2, :].rearrange("p a b -> p (a b)")
        sp.dma_start(dst, w[ds(i * P, P), :]).then_inc(self.landed[slot], 16)


def plain_project_pe(c, pe, products, drained, loops, rhs, g0=0, tokens=T):
    n_half = max(1, tokens // HALF)
    width = min(tokens, HALF)
    per = 4 * n_half
    base = list(c.loads)
    with pe.Fori(0, loops) as i:
        for slot in range(2):
            pe.wait_ge(c.landed[slot], base[slot] + 16 + i * 16)
            for m in range(2):
                for n in range(n_half):
                    j = (slot * 2 + m) * n_half + n
                    pe.wait_ge(drained, g0 + j + 1 + i * per)
                    for k in range(KT):
                        mm = pe.matmul(c.PS[:, (g0 + j) % 8, 0:width], c.W[:, slot, k * 256 + m * P:k * 256 + (m + 1) * P],
                                       rhs[:, k, n * HALF:n * HALF + width], start=k == 0, stop=k == KT - 1)
                    mm.then_inc(products, 1)
    for slot in range(2):
        c.loads[slot] += 16 * loops


def plain_token_major_pe(c, pe, products, drained, slot, rhs, g0, tiles=NC_):
    pe.wait_ge(c.landed[slot], c.loads[slot] + 16)
    w = c.W[:, slot:slot + 2, :].rearrange("p a (k n) -> p (a k) n", n=HALF)
    for t in range(tiles):
        pe.wait_ge(drained, g0 + t + 1)
        for k in range(KT):
            mm = pe.matmul(c.PS[:, (g0 + t) % 8, :], rhs[:, k, t * P:(t + 1) * P], w[:, k, :], start=k == 0,
                           stop=k == KT - 1)
        mm.then_inc(products, 1)
    c.loads[slot] += 16


def refill(c, sp, products, name, first, loops, g0=0):
    if loops > 1:
        with sp.Fori(1, loops) as i:
            for slot in range(2):
                sp.wait_ge(products, g0 + 4 * (slot + 1) - 8 + i * 8)
                c.load(sp, slot, name, first + slot + i * 2)


def project_pe(c, pe, products, drained, w_ready, loops, hi, lo, g0=0, h0=0):
    with pe.Fori(0, loops) as i:
        for j in range(4):
            pe.wait_ge(w_ready, h0 + j + 1 + i * 4)
            for n in range(2):
                pe.wait_ge(drained, g0 + 2 * j + n + 1 + i * 8)
                half_slab_pe(c, pe, (g0 + 2 * j + n) % 8, j % 2, n, hi, lo).then_inc(products, 1)


def half_slab_pe(c, pe, bank, buf, n, hi, lo):
    half = slice(n * HALF, (n + 1) * HALF)
    for k in range(KT):
        w_hi, w_lo = c.WR[:, 2 * buf, k * P:(k + 1) * P], c.WR[:, 2 * buf + 1, k * P:(k + 1) * P]
        pe.matmul(c.PS[:, bank, :], w_hi, hi[:, k, half], start=k == 0, stop=False)
        pe.matmul(c.PS[:, bank, :], w_hi, lo[:, k, half], start=False, stop=False)
        mm = pe.matmul(c.PS[:, bank, :], w_lo, hi[:, k, half], start=False, stop=k == KT - 1)
    return mm


def token_major_pe(c, pe, products, drained, w_ready, hi, lo, g0, h0, slabs_=2):
    w = c.WR[:, :, :].rearrange("p (s a) (k n) -> p s (a k) n", s=2, n=256)
    for s_ in range(slabs_):
        pe.wait_ge(w_ready, h0 + 2 * s_ + 2)
        for t in range(NC_):
            g, at = g0 + 8 * s_ + t, slice(t * P, (t + 1) * P)
            pe.wait_ge(drained, g + 1)
            for k in range(KT):
                out = c.PS[:, g % 8, 0:256]
                pe.matmul(out, hi[:, k, at], w[:, 0, k, :], start=k == 0, stop=False)
                pe.matmul(out, hi[:, k, at], w[:, 1, k, :], start=False, stop=False)
                mm = pe.matmul(out, lo[:, k, at], w[:, 0, k, :], start=False, stop=k == KT - 1)
            mm.then_inc(products, 1)


def pool_round(c, pool, out, x):
    one = c.ones[:, 0:1].unsqueeze(2).to_broadcast(list(x.shape))
    return pool.tensor_tensor(out, x, one, ALU.mult)


class Split:

    def __init__(self, c, pool, products, w_step, w_ready):
        self.c, self.pool, self.products, self.w_step, self.w_ready = c, pool, products, w_step, w_ready
        self.base, self.slab, self.steps = list(c.loads), 0, 0

    def halves(self, loops, g0):
        c, pool = self.c, self.pool
        assert self.slab % 2 == 0
        if g0:
            pool.wait_ge(self.products, PRE + g0)
        with pool.Fori(0, loops) as i:
            for j in range(4):
                slot, m = j // 2, j % 2
                if m == 0:
                    pool.wait_ge(c.landed[slot], self.base[slot] + 16 * (self.slab // 2 + 1) + i * 16)
                pool.wait_ge(self.products, PRE + g0 + 2 * j - 2 + i * 8)
                raw = c.W[:, slot, :].rearrange("p (k n) -> p k n", n=256)[:, :, m * P:(m + 1) * P]
                parts = [c.WR[:, 2 * m + x, :].rearrange("p (k n) -> p k n", n=P) for x in range(2)]
                pool_round(c, pool, parts[0], raw).then_inc(self.w_step, 1)
                pool.wait_ge(self.w_step, self.steps + j + 1 + i * 4)
                pool.tensor_tensor(parts[1], raw, parts[0].bitcast(F32), ALU.subtract).then_inc(self.w_ready, 1)
        self.slab += 2 * loops
        self.steps += 4 * loops

    def whole(self, g0, half=False):
        c, pool, slot = self.c, self.pool, self.slab % 2
        pool.wait_ge(c.landed[slot], self.base[slot] + 16 * (self.slab // 2 + 1))
        if g0:
            pool.wait_ge(self.products, PRE + g0)
        if half:
            raw = c.W[:, slot, :].rearrange("p (k n) -> p k n", n=256)[:, :, 0:P]
            parts = [c.WR[:, x, :].rearrange("p (k n) -> p k n", n=P) for x in range(2)]
        else:
            raw = c.W[:, slot, :].rearrange("p (a n) -> p a n", a=2)
            parts = [c.WR[:, 0:2, :], c.WR[:, 2:4, :]]
        pool_round(c, pool, parts[0], raw).then_inc(self.w_step, 1)
        self.steps += 1
        pool.wait_ge(self.w_step, self.steps)
        pool.tensor_tensor(parts[1], raw, parts[0].bitcast(F32), ALU.subtract).then_inc(self.w_ready, 2)
        self.slab += 1


PRE = 4


def stream(c, sp, w_ready, name, slabs_):
    with sp.Fori(1, slabs_ // 2) as i:
        for slot in range(2):
            sp.wait_ge(w_ready, 2 * slot - 2 + i * 4)
            c.load(sp, slot, name, slot + i * 2)
    if slabs_ % 2:
        sp.wait_ge(w_ready, 2 * (slabs_ - 2))
        c.load(sp, 0, name, slabs_ - 1)


def stream_done(c, slabs_):
    c.loads[0] += 16 * ((slabs_ + 1) // 2)
    c.loads[1] += 16 * (slabs_ // 2)


def w_out_stage(c, name, w, prefetch, scale, gate=None):
    with c.stage("products", "drained", "w_step", "w_ready", "hi_ready", "lo_ready") as (
            block, products, drained, w_step, w_ready, hi_ready, lo_ready):
        @block.sync
        def _(sp):
            stream(c, sp, w_ready, w, 4)
            prefetch_after(c, sp, products, PRE + 16, prefetch)

        @block.gpsimd
        def _(pool):
            Split(c, pool, products, w_step, w_ready).halves(2, 0)

        @block.tensor
        def _(pe):
            pe.sem_inc(products, PRE)
            pe.wait_ge(lo_ready, 16)
            project_pe(c, pe, products, drained, w_ready, 2, c.MR, c.HR)

        @block.scalar
        def _(act):
            for n in range(2):
                for k in range(KT):
                    half = slice(n * HALF, (n + 1) * HALF)
                    act.activation(c.MR[:, k, half], c.H[:, k, half], ACT.Copy).then_inc(hi_ready, 1)

        @block.vector
        def _(dve):
            dve.sem_inc(drained, 8)
            for n in range(2):
                for k in range(KT):
                    half = slice(n * HALF, (n + 1) * HALF)
                    dve.wait_ge(hi_ready, n * KT + k + 1)
                    dve.tensor_tensor(c.HR[:, k, half], c.H[:, k, half], c.MR[:, k, half].bitcast(F32),
                                      ALU.subtract).then_inc(lo_ready, 1)
            with dve.Fori(0, 2) as i:
                for j in range(8):
                    dve.wait_ge(products, PRE + j + 1 + i * 8)
                    x = c.X[:, ds(i * 4 + j // 2, 1), (j % 2) * HALF:(j % 2 + 1) * HALF]
                    ps = c.PS[:, j:j + 1, :]
                    if gate is None:
                        dve.scalar_tensor_tensor(out=x, in0=x, scalar=scale, in1=ps, op0=ALU.mult,
                                                 op1=ALU.add).then_inc(drained, 1)
                    else:
                        dve.scalar_tensor_tensor(out=x, in0=ps, scalar=c.ada[:, ds(i * 8 + gate + j // 2 * 2, 1)],
                                                 in1=x, op0=ALU.mult, op1=ALU.add).then_inc(drained, 1)
    stream_done(c, 4)


def prefetch_after(c, sp, sem, value, loads):
    if loads:
        if sem is not None:
            sp.wait_ge(sem, value)
        for slot, w, i in loads:
            c.load(sp, slot, w, i)


def layer_norm_stage(c, name, src, dst, tiles, ones, eps, g, b=None, centre=True, copies=None, prefetch=(),
                     func=ACT.Identity, halves=2, width=HALF, arrive=None, scratch=True,
                     hi=None, lo=None, spill=False):
    R = 4
    sq = (c.M[:, 1:3, :] if arrive else c.T[:, 0:2, :]).rearrange("p a b -> p (a b)")
    sq = sq.rearrange("p (a n) -> p a n", n=HALF)[:, :, 0:width]
    rstd = (c.T[:, 2, :] if scratch else c.M[:, 0, :]).rearrange("p (a n) -> p a n", n=HALF)[:, :, 0:width]
    with c.stage("spilled", "hi_ready", "lo_ready", "mean_done", "centred", "squared", "squares_used", "var_done", "std_ready", "rstd_ready", "scaled",
                 "written", "copied") as (block, spilled, hi_ready, lo_ready, mean_done, centred, squared, squares_used, var_done, std_ready,
                                          rstd_ready, scaled, written, copied):
        @block.sync
        def _(sp):
            if spill:
                sp.dma_start(c.spill, c.X[:, :, :]).then_inc(spilled, 16)
                sp.wait_ge(spilled, 16)
            prefetch_after(c, sp, None, 0, prefetch)

        @block.tensor
        def _(pe):
            if arrive:
                pe.wait_ge(arrive, 16)
            if centre:
                for n in range(halves):
                    for k in range(tiles):
                        mm = pe.matmul(c.PS[:, n, 0:width], ones, src(k, n), start=k == 0, stop=k == tiles - 1)
                    mm.then_inc(mean_done, 1)
            for n in range(halves):
                for k in range(tiles):
                    pe.wait_ge(squared, n * tiles + k + 1)
                    pe.matmul(c.PS[:, 2 + n, 0:width], ones, sq[:, (n * tiles + k) % R, :], start=k == 0,
                              stop=k == tiles - 1).then_inc(squares_used, 1)

        @block.scalar
        def _(act):
            for n in range(halves):
                for k in range(tiles):
                    i = n * tiles + k
                    if centre:
                        act.wait_ge(centred, i + 1)
                    if i >= R:
                        act.wait_ge(squares_used, i - R + 1)
                    act.activation(sq[:, i % R, :], (dst if centre else src)(k, n), ACT.Square).then_inc(squared, 1)
            for n in range(halves):
                act.wait_ge(squares_used, (n + 1) * tiles)
                act.activation(rstd[:, n, :], c.PS[:, 2 + n, 0:width], ACT.Ln, bias=eps).then_inc(std_ready, 1)
                act.wait_ge(std_ready, n + 1)
                act.activation(rstd[:, n, :], rstd[:, n, :], ACT.Exp, scale=-0.5).then_inc(rstd_ready, 1)
            for n in range(halves):
                for k in range(tiles):
                    act.wait_ge(scaled, n * tiles + k + 1)
                    if hi:
                        if spill and n == 0 and k == 0:
                            act.wait_ge(spilled, 16)
                        act.activation(hi(k, n), dst(k, n), func, scale=g(k), bias=b(k) if b else 0.0).then_inc(hi_ready, 1)
                        act.wait_ge(hi_ready, n * tiles + k + 1)
                    act.activation(dst(k, n), dst(k, n), func, scale=g(k),
                                   bias=b(k) if b else 0.0).then_inc(written, 1)

        @block.vector
        def _(dve):
            if centre:
                for n in range(halves):
                    dve.wait_ge(mean_done, n + 1)
                    for k in range(tiles):
                        dve.tensor_tensor(dst(k, n), src(k, n), c.PS[:, n, 0:width], ALU.subtract).then_inc(centred, 1)
            for n in range(halves):
                dve.wait_ge(rstd_ready, n + 1)
                for k in range(tiles):
                    dve.tensor_tensor(dst(k, n), (dst if centre else src)(k, n), rstd[:, n, :],
                                      ALU.mult).then_inc(scaled, 1)
            if copies is not None:
                for n in range(halves):
                    for k in range(tiles):
                        dve.wait_ge(written, n * tiles + k + 1)
                        copies(dve, k, n).then_inc(copied, 1)
            if hi:
                for n in range(halves):
                    for k in range(tiles):
                        dve.wait_ge(copied if copies else written, n * tiles + k + 1)
                        dve.tensor_tensor(lo(k, n), dst(k, n), hi(k, n).bitcast(F32), ALU.subtract).then_inc(lo_ready, 1)


def tile_of(buf, first=0):
    return lambda k, n: buf[:, first + k, n * HALF:(n + 1) * HALF]


def block1_project(c):
    M, H, S = c.M, c.H, c.small
    V = M[:, 12:16, :].rearrange("p a (b n) -> p (a b) n", n=HALF)
    reset = c.T[:, 0, :]
    sums = [c.T[:, 1, :], c.T[:, 2, :]]
    fix = S[:, 32:48]
    with c.stage("products", "drained", "sig", "forget", "logf", "bounds", "exps", "pooled", "d_ready", "consts", "pw",
                 "gates", "chain") as (
            block, products, drained, sig, forget, logf, bounds, exps, pooled, d_ready, consts, pw_landed, gates, chain):
        pool_w = c.T[:, 3, 0:512]
        inv = c.T[:, 3, 512:576]

        @block.sync
        def _(sp):
            sp.dma_start(pool_w, c.inp["pool_w"]).then_inc(pw_landed, 16)
            refill(c, sp, products, "w_in_cm", 0, 3)
            sp.wait_ge(products, 20)
            c.load(sp, 0, "w_in_cm", 6)
            sp.wait_ge(products, 24)
            c.load(sp, 1, "w_in_cm", 7)
            sp.dma_start(inv, c.inp["inv_count"]).then_inc(gates, 16)

        @block.tensor
        def _(pe):
            pe.wait_ge(c.x_landed, 16)
            plain_project_pe(c, pe, products, drained, 3, c.X)
            plain_token_major_pe(c, pe, products, drained, 2, c.X, 24)
            plain_project_pe(c, pe, products, drained, 1, c.X, g0=32)
            pe.wait_ge(pw_landed, 16)
            for g in range(4):
                pe.wait_ge(d_ready, g + 1)
                for n in range(2):
                    pe.wait_ge(drained, 40 + 2 * g + n + 1)
                    pe.matmul(c.PS[:, 2 * g + n, :], pool_w[:, g * P:(g + 1) * P], M[:, g, n * HALF:(n + 1) * HALF],
                              start=True, stop=True).then_inc(products, 1)

        @block.scalar
        def _(act):
            act.sem_inc(drained, 8)
            act.wait_ge(bounds, 1)
            act.activation(S[:, 8:12], S[:, 0:4], ACT.Exp).then_inc(exps, 1)
            act.activation(S[:, 12:16], S[:, 4:8], ACT.Exp).then_inc(exps, 1)
            with act.Fori(0, 3) as i:
                for j in range(8):
                    act.wait_ge(products, j + 1 + i * 8)
                    act.activation(M[:, ds(i * 4 + j // 2, 1), (j % 2) * HALF:(j % 2 + 1) * HALF], c.PS[:, j:j + 1, :],
                                   ACT.Copy).then_inc(drained, 1)
            act.wait_ge(drained, 32)
            for h in range(4):
                act.activation(M[:, 8 + h, :], M[:, 8 + h, :], ACT.Sigmoid).then_inc(sig, 1)
            for t in range(8):
                act.wait_ge(products, 24 + t + 1)
                act.activation(V[:, t, :], c.PS[:, t, :], ACT.Copy).then_inc(drained, 1)
            for h in range(4):
                act.wait_ge(forget, 2 * h + 2)
                act.activation(M[:, 8 + h, :], M[:, 8 + h, :], ACT.Ln).then_inc(logf, 1)
            for j in range(8):
                act.wait_ge(products, 32 + j + 1)
                act.activation(M[:, 16 + j // 2, (j % 2) * HALF:(j % 2 + 1) * HALF], c.PS[:, j, :],
                               ACT.Silu).then_inc(drained, 1)
            for h in range(4):
                act.activation(M[:, 4 + h, :], M[:, 4 + h, :], ACT.Silu)
            for g in range(4):
                for n in range(2):
                    act.wait_ge(products, 40 + 2 * g + n + 1)
                    act.activation(H[:, g, n * HALF:(n + 1) * HALF], c.PS[:, 2 * g + n, :], ACT.Identity,
                                   scale=c.vec("pool_scale", g)).then_inc(drained, 1)

        @block.gpsimd
        def _(pool):
            pool.memset(reset, 1.0).then_inc(consts, 1)
            pool.wait_ge(consts, 1)
            pool.memset(c.T[:, 0, :].rearrange("p (a b) -> p a b", b=CH)[:, :, 0:1], 0.0).then_inc(consts, 1)

        @block.vector
        def _(dve):
            step = [0]

            def then(ins):
                step[0] += 1
                ins.then_inc(chain, 1)
                dve.wait_ge(chain, step[0])

            dve.wait_ge(c.par_landed, 16)
            lb = c.vec("hgrn_lb", 0, 8)
            then(dve.tensor_tensor(S[:, 16:20], lb[:, 0:4], lb[:, 4:8], ALU.max))
            dve.tensor_tensor(S[:, 0:4], lb[:, 0:4], S[:, 16:20], ALU.subtract)
            dve.tensor_tensor(S[:, 4:8], lb[:, 4:8], S[:, 16:20], ALU.subtract).then_inc(bounds, 1)
            dve.wait_ge(exps, 2)
            then(dve.tensor_tensor(S[:, 16:20], S[:, 8:12], S[:, 12:16], ALU.add))
            then(dve.reciprocal(S[:, 16:20], S[:, 16:20]))
            then(dve.tensor_tensor(S[:, 20:24], S[:, 8:12], S[:, 16:20], ALU.mult))
            then(dve.tensor_scalar(S[:, 24:28], S[:, 20:24], -1.0, 1.0, ALU.mult, ALU.add))
            dve.wait_ge(drained, 32)
            dve.wait_ge(gates, 16)
            for g in range(4):
                a, turn = M[:, g, :], 0
                for lag in [2 ** j for j in range(g + 1)]:
                    s = sums[turn]
                    dve.tensor_copy(s[:, 0:lag], a[:, 0:lag])
                    then(dve.tensor_tensor(s[:, lag:T], a[:, lag:T], a[:, 0:T - lag], ALU.add))
                    a, turn = s, 1 - turn
                then(dve.tensor_tensor(fix, a[:, 0:16], inv[:, g * 16:(g + 1) * 16], ALU.mult))
                then(dve.tensor_tensor(fix, fix, M[:, g, 0:16], ALU.subtract))
                then(dve.scalar_tensor_tensor(out=M[:, g, :], in0=a, scalar=1.0 / 2 ** (g + 1), in1=M[:, g, :],
                                              op0=ALU.mult, op1=ALU.subtract))
                dve.tensor_copy(M[:, g, 0:16], fix).then_inc(d_ready, 1)
            for h in range(4):
                dve.wait_ge(sig, h + 1)
                dve.tensor_scalar(M[:, 8 + h, :], M[:, 8 + h, :], S[:, 24 + h:25 + h], S[:, 20 + h:21 + h], ALU.mult,
                                  ALU.add).then_inc(forget, 1)
                dve.wait_ge(forget, 2 * h + 1)
                dve.tensor_scalar(H[:, 4 + h, :], M[:, 8 + h, :], -1.0, 1.0, ALU.mult, ALU.add).then_inc(forget, 1)
            dve.wait_ge(consts, 2)
            for h in range(4):
                dve.wait_ge(logf, h + 1)
                then(dve.tensor_tensor_scan(sums[h % 2], reset, M[:, 8 + h, :], 0.0, ALU.mult, ALU.add))
                dve.tensor_copy(M[:, 8 + h, :], sums[h % 2])


def block1_hgrn(c, prefetch):
    M, H, PS = c.M, c.H, c.PS
    Wl = [c.T[:, 0, :], c.T[:, 1, :]]
    E = [c.T[:, 2, :], c.T[:, 3, :]]
    Sm = [M[:, 0, :], M[:, 1, :]]
    Vh, St = M[:, 2, :], M[:, 3, :]
    V = M[:, 12:16, :].rearrange("p a (b n) -> p (a b) n", n=HALF)
    OUT, MEAN = PS[:, 4:6, :], PS[:, 6:8, :]
    ch = lambda a, i: a[:, i * CH:(i + 1) * CH]
    with c.stage("v_ready", "d_ready", "e_ready", "w_ready", "scores_done", "masked", "o_done", "squared", "mean_done",
                 "std_ready", "o_consumed", "chain", "written", "step") as (
            block, v_ready, d_ready, e_ready, w_ready, scores_done, masked, o_done, squared, mean_done, std_ready,
            o_consumed, chain, written, stepped):

        def score_bank(r, i):
            return PS[:, 2 * (r % 2) + i // 4, (i % 4) * CH:(i % 4 + 1) * CH]

        @block.sync
        def _(sp):
            prefetch_after(c, sp, None, 0, prefetch)

        @block.gpsimd
        def _(pool):
            with pool.Fori(0, 4) as h:
                pool.wait_ge(o_done, h * 9 + 1)
                pool.tensor_copy(Vh.rearrange("p (a b) -> p a b", b=CH), V[:, :, ds(h * CH, CH)]).then_inc(v_ready, 1)

        @block.tensor
        def _(pe):
            pe.sem_inc(o_done, 1)
            with pe.Fori(0, 4) as h:
                def scores(r):
                    pe.wait_ge(w_ready, h * 10 + r + 1)
                    if r >= 2:
                        pe.wait_ge(masked, h * 10 + r - 1)
                    for i in range(NC_):
                        rhs = c.M[:, ds(h + 4, 1), i * CH:(i + 1) * CH] if r == 7 else ch(Wl[r % 2], i)
                        mm = pe.matmul(score_bank(r, i), ch(Wl[r % 2], i), rhs, start=i % 4 == 0, stop=i % 4 == 3,
                                       skip_group_check=True)
                    mm.then_inc(scores_done, 1)

                def outputs(r):
                    pe.wait_ge(masked, h * 10 + r + 1)
                    for i in range(NC_):
                        mm = pe.matmul(OUT[:, i // 4, (i % 4) * CH:(i % 4 + 1) * CH], ch(Vh, i), ch(Sm[r % 2], i),
                                       start=r == 0 and i % 4 == 0, stop=False, skip_group_check=True)
                    mm.then_inc(o_done, 1)

                for r in range(8):
                    scores(r)
                    if r == 1:
                        pe.wait_ge(v_ready, h + 1)
                        pe.wait_ge(o_consumed, h + 1)
                    if r >= 1:
                        outputs(r - 1)
                pe.wait_ge(w_ready, h * 10 + 9)
                pe.wait_ge(masked, h * 10 + 7)
                for i in range(NC_):
                    mm = pe.transpose(score_bank(8, i), ch(Wl[0], i), c.ident[:, :])
                mm.then_inc(scores_done, 1)
                outputs(7)
                pe.wait_ge(masked, h * 10 + 9)
                for i in range(NC_):
                    mm = pe.matmul(score_bank(9, i), ch(Sm[0], i), ch(Vh, i), start=i % 4 == 0, stop=i % 4 == 3,
                                   skip_group_check=True)
                mm.then_inc(scores_done, 1)
                pe.wait_ge(masked, h * 10 + 10)
                pe.wait_ge(w_ready, h * 10 + 10)
                for i in range(1, NC_):
                    mm = pe.matmul(OUT[:, i // 4, (i % 4) * CH:(i % 4 + 1) * CH], ch(St, i), ch(Wl[1], i), start=False,
                                   stop=i % 4 == 3, skip_group_check=True)
                mm.then_inc(o_done, 1)
                pe.wait_ge(squared, h + 1)
                for n in range(2):
                    mm = pe.matmul(MEAN[:, n, :], c.ones[:, :], E[0][:, n * HALF:(n + 1) * HALF], start=True, stop=True)
                mm.then_inc(mean_done, 1)

        @block.scalar
        def _(act):
            with act.Fori(0, 4) as h:
                for q in range(8):
                    act.wait_ge(d_ready, h * 8 + q + 1)
                    act.activation(E[q % 2], E[q % 2], ACT.Exp).then_inc(e_ready, 1)
                act.wait_ge(w_ready, h * 10 + 7)
                act.activation(c.T[:, 2:3, :], M[:, ds(h + 8, 1), :], ACT.Exp).then_inc(e_ready, 1)
                act.wait_ge(o_done, h * 9 + 10)
                act.activation(c.T[:, 2, :].rearrange("p (a n) -> p a n", n=HALF), OUT, ACT.Square).then_inc(squared, 1)
                act.wait_ge(mean_done, h + 1)
                act.activation(c.T[:, 3, :].rearrange("p (a n) -> p a n", n=HALF), MEAN, ACT.Ln,
                               scale=1.0 / P, bias=c.rms_eps[:, :]).then_inc(std_ready, 1)
                act.wait_ge(std_ready, h * 2 + 1)
                act.activation(c.T[:, 3, :], c.T[:, 3, :], ACT.Exp, scale=-0.5).then_inc(std_ready, 1)

        @block.vector
        def _(dve):
            dve.sem_inc(o_consumed, 1)
            with dve.Fori(0, 4) as h:
                b = lambda m: M[:, ds(h + 8, 1), :].rearrange("p a (n m) -> p (a n) m", m=m)
                kk = lambda m: H[:, ds(h + 4, 1), :].rearrange("p a (n m) -> p (a n) m", m=m)
                qq = lambda m: M[:, ds(h + 4, 1), :].rearrange("p a (n m) -> p (a n) m", m=m)
                blocks = lambda a, m: a.rearrange("p (n m) -> p n m", m=m)

                def exponents(r):
                    m = 64 >> r
                    bv, e = b(2 * m), blocks(E[r % 2], 2 * m)
                    ref = bv[:, :, m - 1:m].to_broadcast([P, T // (2 * m), m])
                    if r >= 2:
                        dve.wait_ge(w_ready, h * 10 + r - 1)
                    dve.tensor_tensor(e[:, :, 0:m], ref, bv[:, :, 0:m], ALU.subtract)
                    dve.tensor_tensor(e[:, :, m:2 * m], bv[:, :, m:2 * m], ref, ALU.subtract).then_inc(d_ready, 1)

                def decayed(r):
                    m = 64 >> r
                    e, w = blocks(E[r % 2], 2 * m), blocks(Wl[r % 2], 2 * m)
                    dve.wait_ge(e_ready, h * 9 + r + 1)
                    if r >= 2:
                        dve.wait_ge(scores_done, h * 10 + r - 1)
                    dve.tensor_tensor(w[:, :, 0:m], kk(2 * m)[:, :, 0:m], e[:, :, 0:m], ALU.mult)
                    dve.tensor_tensor(w[:, :, m:2 * m], qq(2 * m)[:, :, m:2 * m], e[:, :, m:2 * m],
                                      ALU.mult).then_inc(w_ready, 1)

                def masks(r):
                    dve.wait_ge(scores_done, h * 10 + r + 1)
                    if r >= 2:
                        dve.wait_ge(o_done, h * 9 + r)
                    s = PS[:, 2 * (r % 2):2 * (r % 2) + 2, :].rearrange("p a (b n) -> p (a b) n", n=CH)
                    mask = c.ident[:, :].unsqueeze(1).to_broadcast([P, NC_, P]) if r == 7 else c.mask(r)
                    dve.tensor_tensor(blocks(Sm[r % 2], CH), s, mask, ALU.mult).then_inc(masked, 1)

                exponents(0)
                for r in range(LEVELS):
                    if r + 1 < LEVELS:
                        exponents(r + 1)
                    decayed(r)
                    if r >= 1:
                        masks(r - 1)
                dve.wait_ge(scores_done, h * 10 + 6)
                dve.tensor_scalar(blocks(Wl[1], T), kk(T), 1.0, None, ALU.mult).then_inc(w_ready, 1)
                bv = b(CH)
                dve.wait_ge(w_ready, h * 10 + 6)
                dve.tensor_tensor(blocks(E[1], CH), bv[:, :, CH - 1:CH].to_broadcast([P, NC_, CH]), bv,
                                  ALU.subtract).then_inc(d_ready, 1)
                masks(6)
                dve.wait_ge(e_ready, h * 9 + 8)
                dve.wait_ge(scores_done, h * 10 + 7)
                dve.tensor_tensor(blocks(Wl[0], CH), kk(CH), blocks(E[1], CH), ALU.mult).then_inc(w_ready, 1)
                masks(7)
                dve.wait_ge(e_ready, h * 9 + 9)
                dve.wait_ge(scores_done, h * 10 + 8)
                dve.tensor_tensor(blocks(Wl[1], CH), qq(CH), blocks(E[0], CH), ALU.mult).then_inc(w_ready, 1)
                dve.wait_ge(scores_done, h * 10 + 9)
                dve.wait_ge(o_done, h * 9 + 8)
                dve.tensor_copy(Sm[0].rearrange("p (a n) -> p a n", n=HALF), PS[:, 0:2, :]).then_inc(masked, 1)
                dve.wait_ge(scores_done, h * 10 + 10)
                dve.tensor_copy(ch(St, 1), score_bank(9, 0)).then_inc(stepped, 1)
                for i in range(2, NC_):
                    dve.wait_ge(stepped, h * 7 + i - 1)
                    ins = dve.scalar_tensor_tensor(out=ch(St, i), in0=ch(St, i - 1), scalar=E[0][:, i * CH - 1:i * CH],
                                                   in1=score_bank(9, i - 1), op0=ALU.mult, op1=ALU.add)
                    ins.then_inc(stepped, 1)
                dve.wait_ge(stepped, h * 7 + 7)
                dve.tensor_copy(c.small[:, 60:61], ch(St, 7)[:, 0:1]).then_inc(masked, 1)
                dve.wait_ge(std_ready, h * 2 + 2)
                dve.tensor_tensor(E[1].rearrange("p (a n) -> p a n", n=HALF), OUT,
                                  E[1].rearrange("p (a n) -> p a n", n=HALF), ALU.mult).then_inc(o_consumed, 1)
                dve.wait_ge(o_consumed, h + 2)
                dve.scalar_tensor_tensor(out=H[:, ds(h + 4, 1), :], in0=c.T[:, 3:4, :], scalar=c.vec("hgrn_gnorm"),
                                         in1=M[:, ds(h + 16, 1), :], op0=ALU.mult, op1=ALU.mult).then_inc(chain, 1)
                dve.wait_ge(chain, h + 1)


def ffn_stage(c, name, up, down, chunks, conv=False, bias=None, gate=None, prefetch=()):
    KD = 1 if conv else 2
    M, X, PS = c.M, c.X, c.PS
    hid_hi = [c.hidR[:, 4 * b:4 * b + KD, :] for b in range(2)]
    hid_lo = [c.hidR[:, 4 * b + 2:4 * b + 2 + KD, :] for b in range(2)]
    down_parts = c.down1R if conv else c.downR
    w_down = [down_parts[:, x * KD:(x + 1) * KD, :] for x in range(2)]
    mixed = M[:, 8:10, :]
    PAD = 2
    raw = c.T[:, :, :].rearrange("p a b -> p (a b)")[:, 0:2 * (T + PAD)].rearrange("p (a b) -> p a b", b=T + PAD)
    at = lambda i, per, const: const if i is None else i * (2 * per) + const
    base = list(c.loads)
    with c.stage("up_done", "up_drained", "conv_done", "tap_done", "gelu_done", "hi_done", "sq_done", "hid_ready",
                 "down_done", "down_drained", "padded", "bias_ready", "up_step", "up_ready", "down_step",
                 "down_ready") as (
            block, up_done, up_drained, conv_done, tap_done, gelu_done, hi_done, sq_done, hid_ready, down_done,
            down_drained, padded, bias_ready, up_step, up_ready, down_step, down_ready):
        def schedule(eng, first, body):
            n = (chunks - 1) // 2
            first(None, 0)
            with eng.Fori(0, n) as i:
                for off in (0, 1):
                    body(i, off, True)
            for o in range(2 * n, chunks):
                body(None, o, o + 1 < chunks)

        @block.sync
        def _(sp):
            with sp.Fori(0, chunks - 1) as j:
                sp.wait_ge(up_ready, j * 2 + 2)
                c.load(sp, 0, up, j + 1)
                sp.wait_ge(down_ready, j + 1)
                c.load(sp, 1, down, j + 1)
            prefetch_after(c, sp, down_done, chunks * 16, prefetch)

        @block.gpsimd
        def _(pool):
            def split_up(ch, used):
                pool.wait_ge(c.landed[0], ch * 16 + base[0] + 16)
                for m in range(2):
                    if used:
                        pool.wait_ge(up_done, ch * 4 + 2 * m - 2)
                    src = c.W[:, 0, :].rearrange("p (k n) -> p k n", n=256)[:, :, m * P:(m + 1) * P]
                    hi, lo = [c.WR[:, 2 * m + x, :].rearrange("p (k n) -> p k n", n=P) for x in range(2)]
                    pool_round(c, pool, hi, src).then_inc(up_step, 1)
                    pool.wait_ge(up_step, ch * 2 + m + 1)
                    pool.tensor_tensor(lo, src, hi.bitcast(F32), ALU.subtract).then_inc(up_ready, 1)

            def split_down(ch, used):
                pool.wait_ge(c.landed[1], ch * 16 + base[1] + 16)
                if used:
                    pool.wait_ge(down_done, ch * 16)
                src = c.W[:, 1, 0:KD * D].rearrange("p (k n) -> p k n", k=KD)
                pool_round(c, pool, w_down[0], src).then_inc(down_step, 1)
                pool.wait_ge(down_step, ch + 1)
                pool.tensor_tensor(w_down[1], src, w_down[0].bitcast(F32), ALU.subtract).then_inc(down_ready, 1)

            split_up(0, False)
            split_down(0, False)
            split_up(1, True)
            with pool.Fori(2, chunks) as j:
                split_up(j, True)
                split_down(j - 1, True)
            split_down(chunks - 1, True)

        @block.tensor
        def _(pe):
            def up_part(i, o):
                for g in range(4):
                    m, n = g // 2, g % 2
                    if n == 0:
                        pe.wait_ge(up_ready, at(i, 2, 2 * o + m + 1))
                    pe.wait_ge(up_drained, at(i, 4, 4 * o + g + 1))
                    half_slab_pe(c, pe, g, m, n, c.MR, c.HR).then_inc(up_done, 1)

            def down_part(i, o):
                pe.wait_ge(down_ready, at(i, 1, o + 1))
                pe.wait_ge(hid_ready, at(i, KD, KD * (o + 1)))
                h_hi, h_lo = hid_hi[o % 2], hid_lo[o % 2]
                for g in range(16):
                    m, n = g // 2, g % 2
                    half, bank = slice(n * HALF, (n + 1) * HALF), PS[:, 4 + g % 4, :]
                    pe.wait_ge(down_drained, at(i, 16, 16 * o + g + 1 + 16))
                    for k in range(KD):
                        w_hi, w_lo = [w[:, k, m * P:(m + 1) * P] for w in w_down]
                        pe.matmul(bank, w_hi, h_hi[:, k, half], start=k == 0, stop=False)
                        pe.matmul(bank, w_lo, h_hi[:, k, half], start=False, stop=False)
                        mm = pe.matmul(bank, w_hi, h_lo[:, k, half], start=False, stop=k == KD - 1)
                    mm.then_inc(down_done, 1)

            def body(i, o, more):
                if more:
                    up_part(i, o + 1)
                down_part(i, o)

            schedule(pe, up_part, body)

        bias_cols = [c.small[:, 0:2], c.small[:, 2:4]]

        def stage_bias(act, i, o):
            col = param_columns()[0][bias][0] + 2 * o
            src = c.par[:, col:col + 2] if i is None else c.par[:, ds(i * 4 + col, 2)]
            act.copy(bias_cols[o % 2], src).then_inc(bias_ready, 1)

        @block.scalar
        def _(act):
            def up_part(i, o):
                if bias is not None:
                    act.wait_ge(bias_ready, at(i, 1, o + 1))
                for m in range(2):
                    if i is not None or o > 0:
                        used = conv_done if conv else hid_ready
                        act.wait_ge(used, at(i, 2, 2 * (o - 1) + m + 1))
                    for n in range(2):
                        act.wait_ge(up_done, at(i, 4, 4 * o + 2 * m + n + 1))
                        ps = PS[:, 2 * m + n, :]
                        if conv:
                            act.activation(raw[:, m, PAD + n * HALF:PAD + (n + 1) * HALF], ps,
                                           ACT.Copy).then_inc(up_drained, 1)
                        else:
                            b = 0.0 if bias is None else bias_cols[o % 2][:, m:m + 1]
                            act.activation(mixed[:, m, n * HALF:(n + 1) * HALF], ps, ACT.Relu,
                                           bias=b).then_inc(up_drained, 1)
                    if not conv:
                        act.wait_ge(up_drained, at(i, 4, 4 + 4 * o + 2 * m + 2))
                        act.activation(hid_hi[o % 2][:, m, :], mixed[:, m, :], ACT.Square).then_inc(hi_done, 1)
                if conv:
                    act.wait_ge(conv_done, at(i, 2, 2 * o + 1))
                    act.activation(mixed[:, 0, :], mixed[:, 0, :], ACT.Gelu_apprx_tanh).then_inc(gelu_done, 1)
                if bias is not None and (i is not None or o + 1 < chunks):
                    stage_bias(act, i, o + 1)

            act.sem_inc(up_drained, 4)
            if bias is not None:
                stage_bias(act, None, 0)
            schedule(act, up_part, lambda i, o, more: up_part(i, o + 1) if more else None)

        @block.vector
        def _(dve):
            def conv_tile(i, o, tile):
                at_w = param_columns()[0]["conv_w"][0] + tile * 22 + o
                at_b = param_columns()[0]["conv_b"][0] + tile * 22 + o
                col = lambda n: c.par[:, n:n + 1] if i is None else c.par[:, ds(i * 2 + n, 1)]
                out = mixed[:, tile, :]
                if i is not None or o > 0:
                    dve.wait_ge(hid_ready, at(i, 1, o))
                dve.wait_ge(up_drained, at(i, 4, 4 * o + 2 * tile + 2 + 4))
                dve.tensor_scalar(out, raw[:, tile, 2:2 + T], col(at_w + 88), col(at_b), ALU.mult,
                                  ALU.add).then_inc(tap_done, 1)
                dve.wait_ge(tap_done, at(i, 4, 4 * o + 2 * tile + 1))
                dve.scalar_tensor_tensor(out=out, in0=raw[:, tile, 1:1 + T], scalar=col(at_w + 44), in1=out,
                                         op0=ALU.mult, op1=ALU.add).then_inc(tap_done, 1)
                dve.wait_ge(tap_done, at(i, 4, 4 * o + 2 * tile + 2))
                dve.scalar_tensor_tensor(out=out, in0=raw[:, tile, 0:T], scalar=col(at_w), in1=out,
                                         op0=ALU.mult, op1=ALU.add).then_inc(conv_done, 1)

            def low_part(i, o, m, n):
                dve.wait_ge(sq_done, at(i, n, n * o + m + 1))
                dve.tensor_tensor(hid_lo[o % 2][:, m, :], mixed[:, m, :], hid_hi[o % 2][:, m, :].bitcast(F32),
                                  ALU.subtract).then_inc(hid_ready, 1)

            def square(i, o, m):
                dve.wait_ge(hi_done, at(i, 2, 2 * o + m + 1))
                dve.tensor_tensor(mixed[:, m, :], mixed[:, m, :], mixed[:, m, :], ALU.mult).then_inc(sq_done, 1)
                low_part(i, o, m, 2)

            def gated(i, o):
                a, v = mixed[:, 0, :], mixed[:, 1, :]
                dve.wait_ge(gelu_done, at(i, 1, o + 1))
                dve.wait_ge(conv_done, at(i, 2, 2 * o + 2))
                dve.tensor_tensor(hid_hi[o % 2][:, 0, :], a, v, ALU.mult).then_inc(hi_done, 1)
                dve.wait_ge(hi_done, at(i, 1, o + 1))
                dve.tensor_tensor(a, a, v, ALU.mult).then_inc(sq_done, 1)
                low_part(i, o, 0, 1)

            def drain(i, o):
                for g in range(16):
                    m, n = g // 2, g % 2
                    x, ps = X[:, m, n * HALF:(n + 1) * HALF], PS[:, 4 + g % 4, :]
                    dve.wait_ge(down_drained, at(i, 16, 16 * o + g + 1 + 4))
                    dve.wait_ge(down_done, at(i, 16, 16 * o + g + 1))
                    if gate is None:
                        dve.tensor_tensor(x, x, ps, ALU.add).then_inc(down_drained, 1)
                    else:
                        dve.scalar_tensor_tensor(out=x, in0=ps, scalar=gate(m), in1=x, op0=ALU.mult,
                                                 op1=ALU.add).then_inc(down_drained, 1)

            def early(i, o):
                conv_tile(i, o, 0) if conv else square(i, o, 0)

            def late(i, o):
                if conv:
                    conv_tile(i, o, 1)
                    gated(i, o)
                else:
                    square(i, o, 1)

            def first(i, o):
                early(i, o)
                late(i, o)

            def body(i, o, more):
                if more:
                    early(i, o + 1)
                drain(i, o)
                if more:
                    late(i, o + 1)

            dve.sem_inc(down_drained, 20)
            if conv:
                dve.memset(raw[:, :, 0:PAD], 0.0).then_inc(padded, 1)
                dve.wait_ge(padded, 1)
            schedule(dve, first, body)
    c.loads[0] += 16 * chunks
    c.loads[1] += 16 * chunks


def block2_project(c):
    M, H, PS, TAPS = c.M, c.H, c.PS, 31
    V = M[:, 16:20, :].rearrange("p a (b n) -> p (a b) n", n=HALF)
    U = c.T[:, 0:2, :].rearrange("p a b -> p (a b)")[:, 0:TAPS - 1 + T]
    wf = c.T[:, 1, 512:576].rearrange("p (k h) -> p k h", h=8)
    z, l = c.T[0:8, 2, :], c.T[0:8, 3, :]
    with c.stage("products", "drained", "gated", "u_ready", "taps", "wf_landed", "row_step", "padded", "mul") as (
            block, products, drained, gated, u_ready, taps, wf_landed, row_step, padded, mul):
        @block.sync
        def _(sp):
            sp.dma_start(wf, c.inp["w_f_2"].rearrange("p (k h) -> p k h", h=8)).then_inc(wf_landed, 16)
            refill(c, sp, products, "w_in_cm_2", 0, 4)

        @block.tensor
        def _(pe):
            plain_project_pe(c, pe, products, drained, 4, H)
            plain_token_major_pe(c, pe, products, drained, 2, H, 32)
            pe.wait_ge(wf_landed, 16)
            for n in range(2):
                pe.wait_ge(drained, 40 + n + 1)
                for k in range(KT):
                    mm = pe.matmul(PS[0:8, n, :], wf[:, k, :], H[:, k, n * HALF:(n + 1) * HALF], start=k == 0,
                                   stop=k == KT - 1)
                mm.then_inc(products, 1)

        @block.scalar
        def _(act):
            act.sem_inc(drained, 8)

            def copies(first, last):
                with act.Fori(first, last) as i:
                    for j in range(8):
                        act.wait_ge(products, j + 1 + i * 8)
                        act.activation(M[:, ds(i * 4 + j // 2, 1), (j % 2) * HALF:(j % 2 + 1) * HALF],
                                       PS[:, j:j + 1, :], ACT.Copy).then_inc(drained, 1)

            copies(0, 2)
            act.wait_ge(drained, 24)
            for k in range(4):
                act.activation(M[:, 4 + k, :], M[:, 4 + k, :], ACT.Sigmoid).then_inc(gated, 1)
            copies(2, 4)
            for t in range(8):
                act.wait_ge(products, 32 + t + 1)
                act.activation(V[:, t, :], PS[:, t, :], ACT.Copy).then_inc(drained, 1)
            for n in range(2):
                act.wait_ge(products, 40 + n + 1)
                act.activation(z[:, n * HALF:(n + 1) * HALF], PS[0:8, n, :], ACT.Identity,
                               bias=c.row_par[0:8, 0:1]).then_inc(row_step, 1)
            act.wait_ge(row_step, 2)
            act.activation(l, z, ACT.Abs).then_inc(row_step, 1)
            act.wait_ge(row_step, 3)
            act.activation(l, l, ACT.Exp, scale=-1.0).then_inc(row_step, 1)
            act.wait_ge(row_step, 4)
            act.activation(l, l, ACT.Ln, bias=1.0).then_inc(row_step, 1)

        @block.vector
        def _(dve):
            at_w, at_b = param_columns()[0]["conv_dw_w_2"][0], param_columns()[0]["conv_dw_b_2"][0]
            dve.memset(U[:, 0:TAPS - 1], 0.0).then_inc(padded, 1)
            dve.wait_ge(padded, 1)
            dve.sem_inc(taps, 1)
            with dve.Fori(0, 4) as k:
                out = M[:, ds(k, 1), :]
                col = lambda n: c.par[:, ds(k + n, 1)]
                u = lambda j: U[:, j:j + T].unsqueeze(1)
                dve.wait_ge(gated, k + 1)
                dve.wait_ge(taps, k * TAPS + 1)
                dve.tensor_tensor(u(TAPS - 1), out, M[:, ds(k + 4, 1), :], ALU.mult).then_inc(u_ready, 1)
                dve.wait_ge(u_ready, k + 1)
                dve.tensor_scalar(out, u(0), col(at_w), col(at_b), ALU.mult, ALU.add).then_inc(taps, 1)
                for j in range(1, TAPS):
                    dve.wait_ge(taps, k * TAPS + j + 1)
                    dve.scalar_tensor_tensor(out=out, in0=u(j), scalar=col(at_w + 4 * j), in1=out, op0=ALU.mult,
                                             op1=ALU.add).then_inc(taps, 1)
            dve.wait_ge(row_step, 5)
            dve.scalar_tensor_tensor(out=z, in0=z, scalar=0.0, in1=l, op0=ALU.min, op1=ALU.subtract).then_inc(row_step, 1)
            dve.wait_ge(row_step, 6)
            dve.tensor_tensor_scan(l, c.ones[0:8, 0:1].to_broadcast([8, T]), z, 0.0, ALU.mult,
                                   ALU.add).then_inc(row_step, 1)
            dve.wait_ge(row_step, 7)
            dve.tensor_scalar(c.rows[0:8, 0:T], l, -8.0, None, ALU.mult).then_inc(row_step, 1)


def block2_pointwise(c, prefetch):
    M, H, PS = c.M, c.H, c.PS
    sq = c.T[:, :, :].rearrange("p a (b n) -> p (a b) n", n=HALF)
    out = lambda g: H[:, 4 + g // 2, (g % 2) * HALF:(g % 2 + 1) * HALF]
    with c.stage("products", "biased", "squared", "var_done", "logs", "rstd_ready", "done") as (
            block, products, biased, squared, var_done, logs, rstd_ready, done):
        @block.sync
        def _(sp):
            prefetch_after(c, sp, products, 8, prefetch)

        @block.tensor
        def _(pe):
            pe.wait_ge(c.landed[0], c.loads[0] + 16)
            for g in range(8):
                for k in range(4):
                    mm = pe.matmul(PS[:, g, :], c.W[:, 0, k * HALF + g // 2 * P:k * HALF + (g // 2 + 1) * P],
                                   M[:, k, (g % 2) * HALF:(g % 2 + 1) * HALF], start=k == 0, stop=k == 3)
                mm.then_inc(products, 1)
            for g in range(8):
                pe.wait_ge(squared, g + 1)
                pe.matmul(PS[:, g, :], c.group_ones[:, :], sq[:, g, :], start=True, stop=True).then_inc(var_done, 1)

        @block.scalar
        def _(act):
            for g in range(8):
                act.wait_ge(products, g + 1)
                act.activation(out(g), PS[:, g, :], ACT.Identity, bias=c.vec("b_conv_pw_2", g // 2)).then_inc(biased, 1)
                act.wait_ge(biased, g + 1)
                act.activation(sq[:, g, :], out(g), ACT.Square).then_inc(squared, 1)
            for g in range(8):
                act.wait_ge(var_done, g + 1)
                act.activation(sq[:, g, :], PS[:, g, :], ACT.Ln, bias=c.rms_eps[:, :]).then_inc(logs, 1)
                act.wait_ge(logs, g + 1)
                act.activation(sq[:, g, :], sq[:, g, :], ACT.Exp, scale=-0.5).then_inc(rstd_ready, 1)

        @block.vector
        def _(dve):
            for g in range(8):
                dve.wait_ge(rstd_ready, g + 1)
                dve.scalar_tensor_tensor(out=out(g), in0=out(g), scalar=c.vec("conv_out_g_2", g // 2), in1=sq[:, g, :],
                                         op0=ALU.mult, op1=ALU.mult).then_inc(done, 1)
    c.loads[0] += 16


def block2_attention(c, prefetch):
    M, H, PS, S = c.M, c.H, c.PS, c.small
    V = M[:, 16:20, :].rearrange("p a (b n) -> p (a b) n", n=HALF)
    O = M[:, 0:4, :].rearrange("p a (b n) -> p (a b) n", n=HALF)
    Q, K = [c.T[:, 0, :], c.T[:, 2, :]], [c.T[:, 1, :], c.T[:, 3, :]]
    prob, turned = [M[:, 4, :], M[:, 5, :]], [M[:, 6, :], M[:, 7, :]]
    sc = [PS[:, 0:2, :].rearrange("p a b -> p (a b)"), PS[:, 2:4, :].rearrange("p a b -> p (a b)")]
    tp = PS[:, 4:6, :].rearrange("p a b -> p (a b)")
    with c.stage("row_landed_0", "row_landed_1", "ones_rows", "qk_ready", "scores_done", "diag_masked", "max_step",
                 "max_ready", "p_ready", "turned_done", "turned_ready", "pv_done", "o_step", "o_written", "rms",
                 "turned_o", "h_written") as (
            block, row_landed_0, row_landed_1, ones_rows, qk_ready, scores_done, diag_masked, max_step, max_ready,
            p_ready, turned_done, turned_ready, pv_done, o_step, o_written, rms, turned_o, h_written):
        row_landed = [row_landed_0, row_landed_1]

        @block.sync
        def _(sp):
            prefetch_after(c, sp, None, 0, prefetch)
            for h in range(8):
                if h >= 2:
                    sp.wait_ge(scores_done, 8 * (h - 1) + 1)
                sp.dma_start(K[h % 2][64:65, :], c.rows[h:h + 1, 0:T]).then_inc(row_landed[h % 2], 16)

        @block.gpsimd
        def _(pool):
            for e in range(2):
                pool.memset(Q[e][64:65, :], 1.0).then_inc(ones_rows, 1)
            with pool.Fori(0, 4) as p:
                for e in range(2):
                    pool.wait_ge(scores_done, p * 16 + 1)
                    half = slice(64 * e, 64 * e + 64)
                    pool.tensor_copy(Q[e][0:64, :].unsqueeze(1), M[half, ds(p + 8, 1), :]).then_inc(qk_ready, 1)
                    pool.tensor_copy(K[e][0:64, :].unsqueeze(1), M[half, ds(p + 12, 1), :]).then_inc(qk_ready, 1)

        @block.tensor
        def _(pe):
            pe.sem_inc(turned_done, 2)
            pe.sem_inc(pv_done, 2)
            pe.sem_inc(scores_done, 1)
            pe.wait_ge(ones_rows, 2)
            with pe.Fori(0, 4) as p:
                def scores(s):
                    e, i = s // 8, s % 8
                    if i == 0:
                        pe.wait_ge(qk_ready, p * 4 + 2 * e + 2)
                        pe.wait_ge(row_landed[e], p * 16 + 16)
                    pe.wait_ge(p_ready, p * 16 + s + 1)
                    for a in range(0, (i + 1) * P, HALF):
                        b = min((i + 1) * P, a + HALF)
                        mm = pe.matmul(sc[s % 2][:, a:b], Q[e][0:65, i * P:(i + 1) * P], K[e][0:65, a:b], start=True,
                                       stop=True)
                    mm.then_inc(scores_done, 1)

                def turn(s):
                    pe.wait_ge(p_ready, p * 16 + s + 3)
                    pe.wait_ge(turned_ready, p * 16 + s + 1)
                    for b in range(s % 8 + 1):
                        mm = pe.transpose(tp[:, b * P:(b + 1) * P], prob[s % 2][:, b * P:(b + 1) * P], c.ident[:, :])
                    mm.then_inc(turned_done, 1)

                def outputs(s):
                    pe.wait_ge(turned_ready, p * 16 + s + 2)
                    pe.wait_ge(o_written, p * 16 + s + 1)
                    n = s % 8 + 1
                    for b in range(n):
                        mm = pe.matmul(PS[:, 6 + s % 2, 0:64], turned[s % 2][:, b * P:(b + 1) * P],
                                       V[:, b, ds(p * P + 64 * (s // 8), 64)], start=b == 0, stop=b == n - 1)
                    mm.then_inc(pv_done, 1)

                for s in range(18):
                    if s < 16:
                        scores(s)
                    if 1 <= s < 17:
                        turn(s - 1)
                    if s >= 2:
                        outputs(s - 2)
            pe.wait_ge(rms, 5)
            for g in range(8):
                m, n = g // 2, g % 2
                for b in range(4):
                    mm = pe.transpose(PS[:, g, b * P:(b + 1) * P], O[:, n * 4 + b, m * P:(m + 1) * P], c.ident[:, :])
                mm.then_inc(turned_o, 1)

        @block.scalar
        def _(act):
            act.sem_inc(p_ready, 2)
            act.sem_inc(turned_ready, 1)
            with act.Fori(0, 4) as p:
                def exps(s):
                    n = (s % 8 + 1) * P
                    act.wait_ge(max_ready, p * 16 + s + 1)
                    act.wait_ge(turned_done, p * 16 + s + 1)
                    act.activation(prob[s % 2][:, 0:n], sc[s % 2][:, 0:n], ACT.Exp, bias=S[:, 16 + s:17 + s], scale=0.125,
                                   accum_out=S[:, 32 + s:33 + s]).then_inc(p_ready, 1)

                def copies(s):
                    n = (s % 8 + 1) * P
                    act.wait_ge(turned_done, p * 16 + s + 3)
                    act.wait_ge(pv_done, p * 16 + s + 1)
                    act.activation(turned[s % 2][:, 0:n], tp[:, 0:n], ACT.Copy).then_inc(turned_ready, 1)

                for s in range(17):
                    if s < 16:
                        exps(s)
                    if s >= 1:
                        copies(s - 1)
            act.wait_ge(o_written, 66)
            act.activation(c.T[:, :, :], M[:, 0:4, :], ACT.Square).then_inc(rms, 1)
            act.wait_ge(rms, 2)
            act.activation(c.rows[:, 0:64], c.rows[:, 0:64], ACT.Ln, scale=1.0 / 64, bias=c.rms_eps[:, :]).then_inc(rms, 1)
            act.wait_ge(rms, 3)
            act.activation(c.rows[:, 0:64], c.rows[:, 0:64], ACT.Exp, scale=-0.5).then_inc(rms, 1)
            for g in range(8):
                act.wait_ge(turned_o, g + 1)
                act.activation(H[:, g // 2, (g % 2) * HALF:(g % 2 + 1) * HALF], PS[:, g, :], ACT.Identity,
                               scale=c.vec("attn_out_g_2", g // 2)).then_inc(h_written, 1)

        @block.vector
        def _(dve):
            dve.sem_inc(o_written, 2)
            with dve.Fori(0, 4) as p:
                def maxima(s):
                    i = s % 8
                    diag = sc[s % 2][:, i * P:(i + 1) * P]
                    dve.wait_ge(scores_done, p * 16 + s + 2)
                    dve.tensor_tensor(diag, diag, c.from_above, ALU.add).then_inc(diag_masked, 1)
                    dve.wait_ge(diag_masked, p * 16 + s + 1)
                    dve.reduce_max(S[:, s:s + 1], sc[s % 2][:, 0:(i + 1) * P], AX_X).then_inc(max_step, 1)
                    dve.wait_ge(max_step, p * 16 + s + 1)
                    dve.tensor_scalar(S[:, 16 + s:17 + s], S[:, s:s + 1], -0.125, None, ALU.mult).then_inc(max_ready, 1)

                def normalise(s):
                    dve.wait_ge(pv_done, p * 16 + s + 3)
                    dve.reciprocal(S[:, 48 + s % 8:49 + s % 8], S[:, 32 + s:33 + s]).then_inc(o_step, 1)
                    dve.wait_ge(o_step, p * 16 + s + 1)
                    dve.tensor_scalar(O[:, s % 8, ds(p * P + 64 * (s // 8), 64)], PS[:, 6 + s % 2, 0:64],
                                      S[:, 48 + s % 8:49 + s % 8], None, ALU.mult).then_inc(o_written, 1)

                for s in range(18):
                    if s < 16:
                        maxima(s)
                    if s >= 2:
                        normalise(s - 2)
            dve.wait_ge(rms, 1)
            dve.reduce_sum(c.rows[:, 0:64].unsqueeze(2), c.T[:, :, :].rearrange("p a (b n) -> p (a b) n", n=64),
                           AX_X).then_inc(rms, 1)
            dve.wait_ge(rms, 4)
            o = M[:, 0:4, :].rearrange("p a (b n) -> p (a b) n", n=64)
            dve.tensor_tensor(o, o, c.rows[:, 0:64].unsqueeze(2).to_broadcast([P, 64, 64]), ALU.mult).then_inc(rms, 1)


def block3_ada(c, prefetch):
    cond = c.small[:, 0:16].rearrange("p (k s) -> p k s", s=2)
    SLABS = 24
    base = list(c.loads)
    with c.stage("cond_ready", "products", "biased", "plus_one") as (block, cond_ready, products, biased, plus_one):
        @block.sync
        def _(sp):
            sp.dma_start(c.T[:, 0:2, :].rearrange("p a b -> p (a b)"), c.inp["ctx"]).then_inc(c.ctx_landed, 16)
            for slot in range(4):
                c.load(sp, slot, "w_ada_3", slot)
            with sp.Fori(1, SLABS // 4) as i:
                for slot in range(4):
                    sp.wait_ge(products, i * 4 + slot - 3)
                    c.load(sp, slot, "w_ada_3", i * 4 + slot)
            prefetch_after(c, sp, products, SLABS, prefetch)

        @block.scalar
        def _(act):
            for s, name in enumerate(("c_3", "c_ctx_3")):
                act.activation(cond[:, :, s:s + 1], c.vec(name, 0, 8).unsqueeze(2), ACT.Silu).then_inc(cond_ready, 1)

        @block.tensor
        def _(pe):
            pe.wait_ge(cond_ready, 2)
            with pe.Fori(0, SLABS // 4) as i:
                for slot in range(4):
                    pe.wait_ge(c.landed[slot], base[slot] + 16 + i * 16)
                    for m in range(2):
                        for k in range(KT):
                            mm = pe.matmul(c.PS[:, 0:1, ds(i * 16 + slot * 4 + m * 2, 2)],
                                           c.W[:, slot, k * 256 + m * P:k * 256 + (m + 1) * P],
                                           cond[:, k:k + 1, :], start=k == 0, stop=k == KT - 1)
                    mm.then_inc(products, 1)

        @block.vector
        def _(dve):
            dve.wait_ge(products, SLABS)
            ada = c.ada[:, :].rearrange("p (j s) -> p j s", s=2)
            dve.tensor_tensor(ada, c.PS[:, 0, 0:96].rearrange("p (j s) -> p j s", s=2),
                              c.vec("b_ada_3", 0, 48).unsqueeze(2).to_broadcast([P, 48, 2]), ALU.add).then_inc(biased, 1)
            dve.wait_ge(biased, 1)
            for j in (8, 32):
                dve.tensor_scalar(ada[:, j:j + 8, :], ada[:, j:j + 8, :], 1.0, None, ALU.add).then_inc(plus_one, 1)
            dve.tensor_tensor(c.gate_bias[:, :].unsqueeze(2), ada[:, 40:48, 0:1], c.vec("b2_3", 0, 8).unsqueeze(2),
                              ALU.mult).then_inc(plus_one, 1)
    for slot in range(4):
        c.loads[slot] += 16 * (SLABS // 4)


def block3_context(c, prefetch):
    N = c.T[:, 0:2, :].rearrange("p a (b n) -> p (a b) n", n=CTX)
    raw = c.H[:, 1, 0:2 * CTX].rearrange("p (a n) -> p a n", n=CTX)
    k = c.T[:, 2, 0:2 * CTX].rearrange("p (a n) -> p a n", n=CTX)
    v = c.T[:, 3, :].rearrange("p (a n) -> p a n", n=HALF)
    PS = c.PS
    with c.stage("products", "drained", "taps") as (block, products, drained, taps):
        @block.sync
        def _(sp):
            prefetch_after(c, sp, products, 5, prefetch)

        @block.tensor
        def _(pe):
            pe.wait_ge(c.landed[1], c.loads[1] + 16)
            for kk in range(KT):
                mm = pe.matmul(PS[:, 0, 0:CTX], c.W[:, 1, kk * P:(kk + 1) * P], N[:, kk, :], start=kk == 0, stop=kk == 7)
            mm.then_inc(products, 1)
            pe.wait_ge(c.landed[0], c.loads[0] + 16)
            for m in range(2):
                for kk in range(KT):
                    mm = pe.matmul(PS[:, 1 + m, 0:CTX], c.W[:, 0, kk * 256 + m * P:kk * 256 + (m + 1) * P], N[:, kk, :],
                                   start=kk == 0, stop=kk == 7)
                mm.then_inc(products, 1)
            pe.wait_ge(c.landed[2], c.loads[2] + 16)
            w = c.W[:, 2:4, :].rearrange("p a (k n) -> p (a k) n", n=HALF)
            for t in range(2):
                for kk in range(KT):
                    mm = pe.matmul(PS[:, 3 + t, :], N[:, kk, t * P:(t + 1) * P], w[:, kk, :], start=kk == 0, stop=kk == 7)
                mm.then_inc(products, 1)

        @block.scalar
        def _(act):
            act.wait_ge(products, 1)
            act.activation(c.rows[:, T:TT], PS[:, 0, 0:CTX], ACT.Identity, bias=c.row_par[:, 1:2]).then_inc(drained, 1)
            for m in range(2):
                act.wait_ge(products, 2 + m)
                act.activation(raw[:, m, :], PS[:, 1 + m, 0:CTX], ACT.Copy).then_inc(drained, 1)
            for t in range(2):
                act.wait_ge(products, 4 + t)
                act.activation(v[:, t, :], PS[:, 3 + t, :], ACT.Copy).then_inc(drained, 1)
            act.wait_ge(taps, 6)
            act.activation(k, k, ACT.Silu).then_inc(drained, 1)

        @block.vector
        def _(dve):
            for m in range(2):
                dve.wait_ge(drained, 2 + m)
                conv3(c, dve, raw[:, m, :], k[:, m, :], 2 + m, CTX, taps, 3 * m)
    for slot in range(3):
        c.loads[slot] += 16


def conv3(c, dve, x, out, tile, n, taps, base):
    w = lambda j: c.vec("conv_qk_3", 4 * j + tile)
    dve.tensor_scalar(out, x, w(1), None, ALU.mult).then_inc(taps, 1)
    dve.wait_ge(taps, base + 1)
    dve.scalar_tensor_tensor(out=out[:, 1:n], in0=x[:, 0:n - 1], scalar=w(0), in1=out[:, 1:n], op0=ALU.mult,
                             op1=ALU.add).then_inc(taps, 1)
    dve.wait_ge(taps, base + 2)
    dve.scalar_tensor_tensor(out=out[:, 0:n - 1], in0=x[:, 1:n], scalar=w(2), in1=out[:, 0:n - 1], op0=ALU.mult,
                             op1=ALU.add).then_inc(taps, 1)


def block3_project(c):
    M, H, PS, S = c.M, c.H, c.PS, c.small
    v = M[:, 12:16, :].rearrange("p a (b n) -> p (a b) n", n=HALF)
    vals = M[:, 16:20, :].rearrange("p a (b n) -> p (a b) n", n=HALF)
    gain, bias = c.T[:, 0, 0:HALF], c.T[:, 0, HALF:]
    ws, bs = c.W[:, 1, 0:HALF], c.W[0:1, 1, HALF:2 * HALF]
    stats = S[:, 0:48].rearrange("p (a b) -> p a b", b=6)
    aggr = S[:, 48:64].rearrange("p (a b) -> p a b", b=2)
    rstd = c.gate_tmp
    with c.stage("products", "drained", "gain_landed", "spatial_landed", "stats_done", "aggr_done", "rstd_done",
                 "v_step", "taps", "silu_done", "scaled", "mixed", "gated") as (
            block, products, drained, gain_landed, spatial_landed, stats_done, aggr_done, rstd_done, v_step, taps,
            silu_done, scaled, mixed, gated):
        @block.sync
        def _(sp):
            sp.dma_start(c.T[:, 0, :], c.inp["ln_v_rows"]).then_inc(gain_landed, 16)
            sp.wait_ge(products, 2)
            c.load(sp, 0, "w_in_cm_3", 0)
            sp.wait_ge(products, 10)
            c.load(sp, 2, "w_in_vv_3", 0)
            refill(c, sp, products, "w_in_cm_3", 0, 3, g0=10)
            sp.wait_ge(products, 34)
            sp.dma_start(ws, c.inp["w_s_3"]).then_inc(spatial_landed, 16)
            sp.wait_ge(spatial_landed, 16)
            sp.dma_start(bs, c.inp["b_s_3"]).then_inc(spatial_landed, 16)

        @block.tensor
        def _(pe):
            pe.wait_ge(c.landed[0], c.loads[0] + 16)
            for n in range(2):
                for k in range(KT):
                    mm = pe.matmul(PS[:, n, :], c.W[:, 0, k * P:(k + 1) * P], H[:, k, n * HALF:(n + 1) * HALF],
                                   start=k == 0, stop=k == KT - 1)
                mm.then_inc(products, 1)
            c.loads[0] += 16
            plain_token_major_pe(c, pe, products, drained, 2, H, 2)
            plain_project_pe(c, pe, products, drained, 3, H, g0=10)
            plain_token_major_pe(c, pe, products, drained, 2, H, 34)
            pe.wait_ge(spatial_landed, 32)
            pe.wait_ge(v_step, 24)
            for g in range(8):
                pe.wait_ge(drained, 42 + g + 1)
                for i in range(4):
                    t = (g % 2) * 4 + i
                    out = PS[:, (42 + g) % 8, i * P:(i + 1) * P]
                    pe.matmul(out, v[:, t, g // 2 * P:(g // 2 + 1) * P], ws[:, g // 2 * P:(g // 2 + 1) * P],
                              start=i == 0, stop=False, skip_group_check=True)
                    mm = pe.matmul(out, c.ones[0:1, :], bs[:, g // 2 * P:(g // 2 + 1) * P], start=False, stop=i == 3,
                                   skip_group_check=True)
                mm.then_inc(mixed, 1)

        @block.scalar
        def _(act):
            act.sem_inc(drained, 8)
            for n in range(2):
                act.wait_ge(products, n + 1)
                act.activation(c.rows[:, n * HALF:(n + 1) * HALF], PS[:, n, :], ACT.Identity,
                               bias=c.row_par[:, 1:2]).then_inc(drained, 1)
            for t in range(8):
                act.wait_ge(products, 2 + t + 1)
                act.activation(v[:, t, :], PS[:, (2 + t) % 8, :], ACT.Copy).then_inc(drained, 1)
            act.wait_ge(aggr_done, 8)
            act.activation(rstd[:, 0:8].unsqueeze(2), aggr[:, :, 1:2], ACT.Ln, bias=c.ln_eps[:, :]).then_inc(rstd_done, 1)
            act.wait_ge(rstd_done, 1)
            act.activation(rstd[:, 0:8], rstd[:, 0:8], ACT.Exp, scale=-0.5).then_inc(rstd_done, 1)
            with act.Fori(0, 3) as i:
                for j in range(8):
                    act.wait_ge(products, j + 11 + i * 8)
                    act.activation(M[:, ds(i * 4 + j // 2, 1), (j % 2) * HALF:(j % 2 + 1) * HALF],
                                   PS[:, (10 + j) % 8, :].unsqueeze(1), ACT.Copy).then_inc(drained, 1)
            act.wait_ge(drained, 42)
            act.activation(M[:, 8:12, :], M[:, 8:12, :], ACT.Sigmoid).then_inc(gated, 1)
            for t in range(8):
                act.wait_ge(products, 34 + t + 1)
                act.activation(vals[:, t, :], PS[:, (34 + t) % 8, :], ACT.Copy).then_inc(drained, 1)
            for tile in range(4):
                act.wait_ge(taps, 3 * tile + 3)
                act.activation(M[:, 4 + tile, :], c.T[:, 1, :], ACT.Silu).then_inc(silu_done, 1)

        @block.vector
        def _(dve):
            for t in range(8):
                dve.wait_ge(drained, 8 + 2 + t + 1)
                dve.bn_stats(stats[:, t, :], v[:, t, :]).then_inc(stats_done, 1)
            for t in range(8):
                dve.wait_ge(stats_done, t + 1)
                dve.bn_aggr(aggr[:, t, :], stats[:, t:t + 1, :]).then_inc(aggr_done, 1)
            dve.wait_ge(gain_landed, 16)
            dve.wait_ge(rstd_done, 2)
            for t in range(8):
                dve.tensor_scalar(v[:, t, :], v[:, t, :], aggr[:, t, 0:1], rstd[:, t:t + 1], ALU.subtract,
                                  ALU.mult).then_inc(v_step, 1)
                dve.wait_ge(v_step, 3 * t + 1)
                dve.tensor_tensor(v[:, t, :], v[:, t, :], gain, ALU.mult).then_inc(v_step, 1)
                dve.wait_ge(v_step, 3 * t + 2)
                dve.tensor_tensor(v[:, t, :], v[:, t, :], bias, ALU.add).then_inc(v_step, 1)
            dve.wait_ge(drained, 8 + 10 + 16)
            for tile in range(4):
                if tile >= 1:
                    dve.wait_ge(silu_done, tile)
                conv3(c, dve, M[:, 4 + tile, :], c.T[:, 1, :], tile, T, taps, 3 * tile)
            dve.wait_ge(silu_done, 2)
            dve.tensor_scalar(M[:, 4:6, :], M[:, 4:6, :], 0.125, None, ALU.mult).then_inc(scaled, 1)
            dve.wait_ge(products, 42)
            for g in range(8):
                dve.wait_ge(mixed, g + 1)
                half = slice((g % 2) * HALF, (g % 2 + 1) * HALF)
                dve.tensor_tensor(H[:, g // 2, half], PS[:, (42 + g) % 8, :], M[:, g // 2, half], ALU.mult).then_inc(scaled, 1)


ROWS = 36
CHUNKS = TT // CH
ORDER = ([8, 9] + list(range(8)), [9, 8] + list(range(7, -1, -1)))


def row_regions(c):
    w = c.W[:, 2:4, :].rearrange("p a b -> p (a b)")
    h = c.H[:, 4:8, :].rearrange("p a b -> p (a b)")
    t = c.T[:, 0:2, :].rearrange("p a b -> p (a b)")
    cut = lambda a, n: a[0:ROWS, n * TT:(n + 1) * TT]
    return {
        "l": cut(w, 0), "neg": cut(w, 1), "b": cut(w, 2), "m": cut(h, 0), "g": cut(h, 1), "reset": cut(h, 2),
        "neg_m": cut(t, 0),
        "cols": t[:, TT:TT + 320].rearrange("p (c q r) -> p c q r", q=4, r=8),
        "carry": t[:, TT + 320:TT + 360].rearrange("p (j c) -> p j c", c=CHUNKS),
        "small": t[0:ROWS, TT + 400:TT + 400 + 64],
        "sel": c.M[0:ROWS, 12, :].rearrange("p (j n) -> p j n", n=P),
        "kt": c.M[:, 13:15, :].rearrange("p a (c n) -> p (a c) n", n=256),
        "kt_ctx": c.M[:, 15, 0:512].rearrange("p (c n) -> p c n", n=256),
        "sel2": c.M[0:ROWS, 15, 512:1024].rearrange("p (j n) -> p j n", n=P),
    }


def block3_gates(c, prefetch):
    r = row_regions(c)
    rows, PS = c.rows, c.PS
    m0, neg_last, carry = r["small"][:, 0:10], r["small"][:, 16:26], r["small"][:, 32:42]
    kc = c.T[:, 2, 0:2 * CTX].rearrange("p (a n) -> p a n", n=CTX)
    with c.stage("sel_landed", "sel2_landed", "zeroed", "f_read", "i_moved", "l_step", "lf", "b_ready", "g_ready",
                 "m_step", "last_ready", "thr", "exps", "cols_done", "cols_copied", "turned", "kt_copied", "carried",
                 "bc_done") as (
            block, sel_landed, sel2_landed, zeroed, f_read, i_moved, l_step, lf, b_ready, g_ready, m_step, last_ready,
            thr, exps, cols_done, cols_copied, turned, kt_copied, carried, bc_done):
        @block.sync
        def _(sp):
            sp.dma_start(r["sel"], c.inp["sel"].rearrange("p (j n) -> p j n", n=P)).then_inc(sel_landed, 16)
            sp.dma_start(r["sel2"], c.inp["sel2"].rearrange("p (j n) -> p j n", n=P)).then_inc(sel2_landed, 16)
            prefetch_after(c, sp, None, 0, prefetch)
            sp.wait_ge(sel_landed, 16)

        @block.gpsimd
        def _(pool):
            pool.memset(r["reset"], 1.0).then_inc(zeroed, 1)
            pool.memset(r["l"], 0.0).then_inc(zeroed, 1)
            pool.memset(r["neg"], 0.0).then_inc(zeroed, 1)
            pool.memset(r["b"], 0.0).then_inc(zeroed, 1)
            pool.memset(r["m"], 0.0).then_inc(zeroed, 1)
            pool.memset(r["small"], 0.0).then_inc(zeroed, 1)
            pool.wait_ge(zeroed, 6)
            chunked = r["reset"].rearrange("p (c n) -> p c n", n=CH)
            pool.memset(chunked[0:4, :, 0:1], 0.0).then_inc(zeroed, 1)
            pool.memset(chunked[32:36, :, CH - 1:CH], 0.0).then_inc(zeroed, 1)

        @block.scalar
        def _(act):
            act.wait_ge(zeroed, 8)
            for d, at in ((0, 32), (1, 96)):
                act.activation(r["l"][32 * d:32 * d + 4, :], rows[at:at + 4, :], ACT.Abs).then_inc(f_read, 1)
                act.activation(r["neg"][32 * d:32 * d + 4, :], rows[at:at + 4, :], ACT.Relu, scale=-1.0).then_inc(f_read, 1)
            act.wait_ge(f_read, 4)
            act.activation(rows[32:36, :], rows[64:68, :], ACT.Copy).then_inc(i_moved, 1)
            act.activation(r["l"], r["l"], ACT.Exp, scale=-1.0).then_inc(l_step, 1)
            act.wait_ge(l_step, 1)
            act.activation(r["l"], r["l"], ACT.Ln, bias=1.0).then_inc(l_step, 1)
            act.wait_ge(thr, 1)
            act.activation(r["l"], r["l"], ACT.Exp, scale=-1.0).then_inc(exps, 1)
            act.wait_ge(last_ready, 3)
            for ch in range(CHUNKS):
                at = slice(ch * CH, (ch + 1) * CH)
                act.activation(r["neg"][:, at], r["m"][:, at], ACT.Exp, scale=-1.0, bias=m0[:, ch:ch + 1]).then_inc(exps, 1)
                act.activation(r["reset"][:, at], r["g"][:, at], ACT.Exp, bias=neg_last[:, ch:ch + 1]).then_inc(exps, 1)
            act.activation(carry, carry, ACT.Exp).then_inc(exps, 1)

        @block.vector
        def _(dve):
            dve.wait_ge(l_step, 2)
            dve.scalar_tensor_tensor(out=r["l"], in0=r["l"], scalar=-1.0, in1=r["neg"], op0=ALU.mult,
                                     op1=ALU.subtract).then_inc(lf, 1)
            dve.wait_ge(lf, 1)
            dve.wait_ge(zeroed, 8)
            dve.tensor_tensor_scan(r["b"][0:4, :], r["reset"][0:4, :], r["l"][0:4, :], 0.0, ALU.mult,
                                   ALU.add).then_inc(b_ready, 1)
            dve.tensor_tensor_scan(r["b"][32:36, ::-1], r["reset"][32:36, ::-1], r["l"][32:36, ::-1], 0.0, ALU.mult,
                                   ALU.add).then_inc(b_ready, 1)
            dve.wait_ge(b_ready, 2)
            dve.wait_ge(i_moved, 1)
            dve.tensor_tensor(r["g"], rows[0:ROWS, :], r["b"], ALU.subtract).then_inc(g_ready, 1)
            dve.wait_ge(g_ready, 1)
            n = 0
            for step in range(CHUNKS):
                for d in range(2):
                    ch, q = ORDER[d][step], slice(32 * d, 32 * d + 4)
                    at = slice(ch * CH, (ch + 1) * CH)
                    g, m = r["g"][q, at], r["m"][q, at]
                    if d:
                        g, m = g[:, ::-1], m[:, ::-1]
                    dve.tensor_tensor_scan(m, g, g, m0[q, ch:ch + 1], ALU.max, ALU.max).then_inc(m_step, 1)
                n += 2
                dve.wait_ge(m_step, n)
                if step + 1 < CHUNKS:
                    for d in range(2):
                        ch, q = ORDER[d][step], slice(32 * d, 32 * d + 4)
                        last, nxt = ch * CH + (0 if d else CH - 1), ORDER[d][step + 1]
                        dve.tensor_tensor(m0[q, nxt:nxt + 1], r["b"][q, last:last + 1], r["m"][q, last:last + 1],
                                          ALU.add).then_inc(m_step, 1)
                    n += 2
                    dve.wait_ge(m_step, n)
            dve.tensor_tensor(r["l"], r["b"], r["m"], ALU.add).then_inc(thr, 1)
            chunked = r["m"].rearrange("p (c n) -> p c n", n=CH)
            dve.tensor_scalar(neg_last[0:4, :].unsqueeze(2), chunked[0:4, :, CH - 1:CH], -1.0, None,
                              ALU.mult).then_inc(last_ready, 1)
            dve.tensor_scalar(neg_last[32:36, :].unsqueeze(2), chunked[32:36, :, 0:1], -1.0, None,
                              ALU.mult).then_inc(last_ready, 1)
            dve.wait_ge(last_ready, 2)
            dve.tensor_tensor(carry, m0, neg_last, ALU.add).then_inc(last_ready, 1)
            dve.tensor_scalar(r["neg_m"], r["m"], -1.0, None, ALU.mult).then_inc(thr, 1)
            for b in range(5):
                dve.wait_ge(turned, b + 1)
                out = r["kt"][:, 2 * b:2 * b + 2, :] if b < 4 else r["kt_ctx"]
                dve.tensor_copy(out, PS[:, 4 if b == 4 else b, :].rearrange("p (c n) -> p c n", n=256)).then_inc(kt_copied, 1)
            for b in range(4):
                dve.wait_ge(cols_done, b + 1)
                nc_ = min(3, CHUNKS - 3 * b)
                ps = PS[:, b, 0:nc_ * 4 * ROWS].rearrange("p (c q r) -> p c q r", q=4, r=ROWS)
                for q in range(4):
                    out = r["cols"][:, 3 * b:3 * b + nc_, q, :]
                    dve.tensor_copy(out[:, :, 0:4], ps[:, :, q, 0:4]).then_inc(cols_copied, 1)
                    dve.tensor_copy(out[:, :, 4:8], ps[:, :, q, 32:36]).then_inc(cols_copied, 1)
            dve.wait_ge(bc_done, 1)
            dve.tensor_copy(r["carry"], PS[:, 5, 0:40].rearrange("p (j c) -> p j c", c=CHUNKS)).then_inc(carried, 1)

        @block.tensor
        def _(pe):
            for b in range(5):
                for i in range(2):
                    for tile in range(2):
                        src = c.M[:, 6 + tile, (2 * b + i) * P:(2 * b + i + 1) * P] if b < 4 else \
                            kc[:, tile, i * P:(i + 1) * P]
                        mm = pe.transpose(PS[:, b, i * 256 + tile * P:i * 256 + (tile + 1) * P], src, c.ident[:, :])
                mm.then_inc(turned, 1)
            pe.wait_ge(kt_copied, 5)
            pe.wait_ge(exps, 22)
            for b in range(4):
                for i in range(min(3, CHUNKS - 3 * b)):
                    at = slice((3 * b + i) * CH, (3 * b + i + 1) * CH)
                    for q, name in enumerate(("g", "l", "neg", "reset")):
                        j = (i * 4 + q) * ROWS
                        mm = pe.transpose(PS[:, b, j:j + ROWS], r[name][:, at], c.ident[0:ROWS, 0:ROWS])
                mm.then_inc(cols_done, 1)
            pe.wait_ge(sel2_landed, 16)
            for j in range(4):
                mm = pe.matmul(PS[:, 5, j * CHUNKS:(j + 1) * CHUNKS], r["sel2"][:, j, :], carry, start=j == 0, stop=j == 3,
                               skip_group_check=True)
            mm.then_inc(bc_done, 1)


def block3_mlstm(c, prefetch):
    r = row_regions(c)
    M, PS = c.M, c.PS
    vals = M[:, 16:20, :].rearrange("p a (b n) -> p (a b) n", n=HALF)
    vals_ctx = c.T[:, 3, :].rearrange("p (a n) -> p a n", n=HALF)
    out_h = M[:, 0:4, :].rearrange("p a (b n) -> p (a b) n", n=HALF)
    H = c.H[:, 4:8, :].rearrange("p a b -> p (a b)")
    qs = [H[:, d * 256:(d + 1) * 256].rearrange("p (a n) -> p a n", n=P) for d in range(2)]
    ks = [H[:, 512 + d * 256:512 + (d + 1) * 256].rearrange("p (a n) -> p a n", n=P) for d in range(2)]
    kw = [H[:, 1024 + d * 256:1024 + (d + 1) * 256] for d in range(2)]
    state = [H[:, 1536 + d * 258:1536 + (d + 1) * 258].rearrange("p (a n) -> p a n", n=129) for d in range(2)]
    small = [H[:, 2052 + d * 16:2052 + (d + 1) * 16] for d in range(2)]
    wt = [H[:, 2560 + d * 512:2560 + (d + 1) * 512].rearrange("p (h n) -> p h n", n=P) for d in range(2)]
    W = c.W[:, 2:4, :].rearrange("p a b -> p (a b)")
    num = [W[:, d * 512:(d + 1) * 512].rearrange("p (h n) -> p h n", n=P) for d in range(2)]
    vs = [W[:, 1024 + d * 512:1024 + (d + 1) * 512] for d in range(2)]
    GB, INTRA, ST, SMALL = PS[:, 1, :], PS[:, 2, :], PS[:, 5, :], PS[:, 6, :]
    heads = lambda a: a.rearrange("p (h n) -> p h n", n=P)
    inter = PS[:, 3:5, 0:258].rearrange("p e (j n) -> p j e n", n=129)
    scores = PS[:, 0:8:7, 0:256].rearrange("p e (j n) -> p j e n", n=P)
    neg = [c.from_below, c.from_above]
    with c.stage("staged", "kw_ready", "added", "stepped", "sc_done", "gb_done", "arg_ready", "w_ready", "weighted",
                 "intra_done", "inter_done", "den", "num_step", "h_added", "zeroed") as (
            block, staged, kw_ready, added, stepped, sc_done, gb_done, arg_ready, w_ready, weighted, intra_done,
            inter_done, den, num_step, h_added, zeroed):
        def chunk(i, d):
            return i if d == 0 else i * -1 + 7

        @block.sync
        def _(sp):
            prefetch_after(c, sp, None, 0, prefetch)

        @block.gpsimd
        def _(pool):
            for d in range(2):
                pool.memset(state[d], 0.0).then_inc(zeroed, 1)
            pool.memset(out_h, 0.0).then_inc(zeroed, 1)
            with pool.Fori(0, 8) as i:
                for d in range(2):
                    pool.wait_ge(intra_done, i * 2 + d + 1)
                    at = ds((i * P if d == 0 else i * -P + 7 * P), P)
                    pool.tensor_copy(qs[d], M[:, 4:6, at]).then_inc(staged, 1)
                    pool.tensor_copy(ks[d], M[:, 6:8, at]).then_inc(staged, 1)
                    pool.tensor_copy(vs[d].unsqueeze(1), vals[:, ds(chunk(i, d), 1), :]).then_inc(staged, 1)

        def update_pe(pe, d, n, v):
            pe.wait_ge(kw_ready, n + 1)
            if type(n) is not int or n > 0:
                pe.wait_ge(stepped, n)
            for h in range(4):
                p0 = 64 * (h % 2)
                out = ST[p0:p0 + 64, (h // 2) * 129:(h // 2) * 129 + 129]
                pe.matmul(out[:, 0:P], kw[d][:, h * 64:(h + 1) * 64], v[:, h * P:(h + 1) * P], start=h < 2,
                          stop=False, skip_group_check=True)
                mm = pe.matmul(out[:, P:P + 1], kw[d][:, h * 64:(h + 1) * 64], c.ones[:, 0:1], start=False,
                               stop=h >= 2, skip_group_check=True)
            mm.then_inc(added, 1)

        def update_dve(dve, d, n, ch):
            dve.wait_ge(added, n + 1)
            for j in range(2):
                col = r["carry"][:, 2 * d + j, ch]
                ins = dve.scalar_tensor_tensor(out=state[d][:, j, :], in0=state[d][:, j, :], scalar=col,
                                               in1=ST[:, j * 129:(j + 1) * 129], op0=ALU.mult, op1=ALU.add)
            ins.then_inc(stepped, 1)

        @block.tensor
        def _(pe):
            pe.sem_inc(intra_done, 2)
            for n in range(4):
                d, ch = n % 2, ORDER[n % 2][n // 2] - 8
                update_pe(pe, d, n, vals_ctx[:, ch, :])
            with pe.Fori(0, 8) as i:
                for d in range(2):
                    n = lambda per, k: i * (2 * per) + d * per + k
                    pe.wait_ge(staged, n(3, 3))
                    pe.wait_ge(weighted, n(1, 1))
                    for h in range(4):
                        p0 = 64 * (h % 2)
                        mm = pe.matmul(scores[:, h // 2, h % 2, :], ks[d][p0:p0 + 64, h // 2, :],
                                       qs[d][p0:p0 + 64, h // 2, :], start=h < 2, stop=h >= 2, skip_group_check=True)
                    mm.then_inc(sc_done, 1)
                    pe.wait_ge(arg_ready, n(1, 1))
                    at = ds((i * P if d == 0 else i * -P + 7 * P), P)
                    for h in range(4):
                        mm = pe.matmul(heads(GB)[:, h, :], r["sel"][:, 4 * d + h, :], r["neg_m"][:, at], start=h == 0,
                                       stop=h == 3, skip_group_check=True)
                    mm.then_inc(gb_done, 1)
                    pe.wait_ge(stepped, n(1, 3))
                    pe.wait_ge(num_step, n(2, 1))
                    for h in range(4):
                        p0 = 64 * (h % 2)
                        mm = pe.matmul(inter[:, h // 2, h % 2, :], qs[d][p0:p0 + 64, h // 2, :],
                                       state[d][p0:p0 + 64, h // 2, :], start=h < 2, stop=h >= 2,
                                       skip_group_check=True)
                    mm.then_inc(inter_done, 1)
                    update_pe(pe, d, n(1, 4), vs[d])
                    pe.wait_ge(weighted, n(1, 2))
                    for h in range(4):
                        pe.matmul(heads(INTRA)[:, h, :], wt[d][:, h, :], vs[d][:, h * P:(h + 1) * P], start=h == 0,
                                  stop=False, skip_group_check=True)
                        mm = pe.matmul(SMALL[:, h:h + 1], wt[d][:, h, :], c.ones[:, 0:1], start=h == 0, stop=h == 3,
                                       skip_group_check=True)
                    mm.then_inc(intra_done, 1)

        @block.scalar
        def _(act):
            with act.Fori(0, 8) as i:
                for d in range(2):
                    act.wait_ge(arg_ready, i * 2 + d + 2)
                    act.activation(wt[d], wt[d], ACT.Exp).then_inc(w_ready, 1)

        @block.vector
        def _(dve):
            def keys(d, n, kt, ch):
                dve.tensor_tensor(kw[d].rearrange("p (h n) -> p h n", n=64), kt,
                                  ch_cols(ch, 3, d).to_broadcast([P, 4, 64]), ALU.mult).then_inc(kw_ready, 1)

            def ch_cols(ch, q, d):
                if type(ch) is int:
                    return r["cols"][:, ch, q, 4 * d:4 * d + 4].unsqueeze(2)
                return r["cols"][:, ds(ch, 1), q, 4 * d:4 * d + 4].rearrange("p a h -> p h a")

            dve.wait_ge(zeroed, 3)
            for credit in (weighted, arg_ready, num_step):
                dve.sem_inc(credit, 1)
            for n in range(4):
                d, ch = n % 2, ORDER[n % 2][n // 2]
                if n >= 2:
                    dve.wait_ge(stepped, n - 1)
                keys(d, n, r["kt_ctx"][:, ch - 8, :].rearrange("p (h n) -> p h n", n=64), ch)
                update_dve(dve, d, n, slice(ch, ch + 1))
            with dve.Fori(0, 8) as i:
                for d in range(2):
                    n = lambda per, k: i * (2 * per) + d * per + k
                    ch = chunk(i, d)
                    gcol = lambda q: ch_cols(ch, q, d)
                    dve.wait_ge(added, n(1, 3))
                    keys(d, None, r["kt"][:, ds(ch, 1), :].rearrange("p a (h n) -> p (a h) n", n=64), ch)
                    dve.wait_ge(gb_done, n(1, 1))
                    for h in range(4):
                        ins = dve.scalar_tensor_tensor(out=wt[d][:, h, :], in0=heads(GB)[:, h, :],
                                                       scalar=r["cols"][:, ds(ch, 1), 0, 4 * d + h],
                                                       in1=neg[d], op0=ALU.add, op1=ALU.add)
                    ins.then_inc(arg_ready, 1)
                    dve.wait_ge(inter_done, n(1, 1))
                    update_dve(dve, d, n(1, 4), ds(ch, 1))
                    dve.wait_ge(w_ready, n(1, 1))
                    dve.wait_ge(sc_done, n(1, 1))
                    w4 = wt[d].rearrange("p (j e) n -> p j e n", e=2)
                    dve.tensor_tensor(w4, scores, w4, ALU.mult).then_inc(weighted, 1)
                    dve.tensor_tensor(num[d].rearrange("p (a h) n -> p a h n", a=2), inter[:, :, :, 0:P],
                                      gcol(2).rearrange("p (a h) n -> p a h n", a=2).to_broadcast([P, 2, 2, P]),
                                      ALU.mult).then_inc(num_step, 1)
                    dt = small[d][:, 0:4].unsqueeze(2)
                    dve.tensor_tensor(dt.rearrange("p (a h) n -> p a h n", a=2), inter[:, :, :, P:P + 1],
                                      gcol(2).rearrange("p (a h) n -> p a h n", a=2), ALU.mult).then_inc(den, 1)
                    dve.wait_ge(intra_done, n(1, 3))
                    dve.wait_ge(den, n(5, 1))
                    dve.tensor_tensor(small[d][:, 4:8], small[d][:, 0:4], SMALL[:, 0:4], ALU.add).then_inc(den, 1)
                    dve.wait_ge(den, n(5, 2))
                    dve.scalar_tensor_tensor(out=small[d][:, 8:12], in0=small[d][:, 4:8], scalar=-1.0,
                                             in1=small[d][:, 4:8], op0=ALU.mult, op1=ALU.max).then_inc(den, 1)
                    dve.wait_ge(den, n(5, 3))
                    dve.tensor_tensor(small[d][:, 8:12].unsqueeze(2), small[d][:, 8:12].unsqueeze(2), gcol(1),
                                      ALU.max).then_inc(den, 1)
                    dve.wait_ge(den, n(5, 4))
                    dve.reciprocal(small[d][:, 12:16], small[d][:, 8:12]).then_inc(den, 1)
                    dve.wait_ge(num_step, n(2, 2))
                    dve.tensor_tensor(num[d], num[d], heads(INTRA), ALU.add).then_inc(num_step, 1)
                    dve.wait_ge(num_step, n(2, 3))
                    dve.wait_ge(den, n(5, 5))
                    dve.tensor_tensor(num[d], num[d], small[d][:, 12:16].unsqueeze(2).to_broadcast([P, 4, P]),
                                      ALU.mult).then_inc(h_added, 1)
                    dve.wait_ge(h_added, n(2, 1))
                    o = out_h[:, ds(ch, 1), :]
                    dve.tensor_tensor(o, o, num[d].rearrange("p h n -> p (h n)").unsqueeze(1),
                                      ALU.add).then_inc(h_added, 1)


def block3_head_norm(c, prefetch):
    M, H, PS, S = c.M, c.H, c.PS, c.small
    h = M[:, 0:4, :].rearrange("p a (g n) -> p (a g) n", n=P)
    tm = M[:, 0:4, :].rearrange("p a (b n) -> p (a b) n", n=HALF)
    mean, var = S[:, 0:32], S[:, 32:64]
    bc = lambda a: a.unsqueeze(2).to_broadcast([P, 32, P])
    with c.stage("step", "x_scaled", "turned", "written") as (block, step, x_scaled, turned, written):
        @block.sync
        def _(sp):
            prefetch_after(c, sp, None, 0, prefetch)

        @block.vector
        def _(dve):
            dve.reduce_sum(mean.unsqueeze(2), h, AX_X).then_inc(step, 1)
            dve.wait_ge(step, 1)
            dve.tensor_scalar(mean, mean, 1.0 / P, None, ALU.mult).then_inc(step, 1)
            dve.wait_ge(step, 2)
            dve.tensor_tensor(h, h, bc(mean), ALU.subtract).then_inc(step, 1)
            dve.wait_ge(step, 4)
            dve.reduce_sum(var.unsqueeze(2), c.T[:, :, :].rearrange("p a (g n) -> p (a g) n", n=P), AX_X).then_inc(step, 1)
            dve.wait_ge(step, 7)
            dve.tensor_tensor(h, h, bc(var), ALU.mult).then_inc(step, 1)
            for g in range(8):
                dve.wait_ge(turned, g + 1)
                half = slice((g % 2) * HALF, (g % 2 + 1) * HALF)
                dve.scalar_tensor_tensor(out=H[:, 4 + g // 2, half], in0=PS[:, g, :], scalar=c.vec("hn_g_3", g // 2),
                                         in1=M[:, 8 + g // 2, half], op0=ALU.mult, op1=ALU.mult).then_inc(written, 1)

        @block.scalar
        def _(act):
            act.wait_ge(step, 3)
            act.activation(c.T[:, :, :], M[:, 0:4, :], ACT.Square).then_inc(step, 1)
            act.activation(c.X[:, :, :], c.X[:, :, :], ACT.Copy, scale=ALPHA).then_inc(x_scaled, 1)
            act.wait_ge(step, 5)
            act.activation(var, var, ACT.Ln, scale=1.0 / P, bias=c.ln_eps[:, :]).then_inc(step, 1)
            act.wait_ge(step, 6)
            act.activation(var, var, ACT.Exp, scale=-0.5).then_inc(step, 1)

        @block.tensor
        def _(pe):
            pe.wait_ge(step, 8)
            for g in range(8):
                for b in range(4):
                    mm = pe.transpose(PS[:, g, b * P:(b + 1) * P], tm[:, (g % 2) * 4 + b, g // 2 * P:(g // 2 + 1) * P],
                                      c.ident[:, :])
                mm.then_inc(turned, 1)


def store_stage(c, stored):
    with c.nc.Block() as block:
        @block.sync
        def _(sp):
            sp.dma_start(c.out, c.X[:, :, :]).then_inc(stored, 16)
            sp.wait_ge(stored, 16)


def build(nc, inputs, out, blocks=(1, 2, 3), upto=99):
    with ExitStack() as ctx:
        c = Core(nc, ctx, inputs, out)
        c.rms_eps = ctx.enter_context(nc.sbuf_tensor("rms_eps", [P, 1], F32))
        c.ln_eps = ctx.enter_context(nc.sbuf_tensor("ln_eps", [P, 1], F32))
        c.x_landed = ctx.enter_context(nc.semaphore("x_landed"))
        c.ctx_landed = ctx.enter_context(nc.semaphore("ctx_landed"))
        c.par_landed = ctx.enter_context(nc.semaphore("params_landed"))
        stored = ctx.enter_context(nc.semaphore("stored"))
        with c.stage("memsets", "tables") as (block, memsets, tables):
            @block.sync
            def _(sp):
                if blocks[0] == 1:
                    c.load(sp, 0, "w_in_cm", 0)
                sp.dma_start(c.X[:, :, :], inputs["x"]).then_inc(c.x_landed, 16)
                if blocks[0] == 1:
                    c.load(sp, 1, "w_in_cm", 1)
                sp.dma_start(c.par[:, :], inputs["params"]).then_inc(c.par_landed, 16)
                if blocks[0] == 1:
                    c.load(sp, 2, "w_in_v", 0)
                sp.wait_ge(c.x_landed, 16)
                sp.wait_ge(c.par_landed, 16)

            @block.scalar
            def _(act):
                act.dma_start(c.ident[:, :], inputs["ident"]).then_inc(tables, 16)
                act.dma_start(c.masks[:, :, :], inputs["masks"]).then_inc(tables, 16)
                act.dma_start(c.group_ones[:, :], inputs["group_ones"]).then_inc(tables, 16)
                act.dma_start(c.row_par[:, :], inputs["row_params"]).then_inc(tables, 16)
                act.wait_ge(tables, 64)

            @block.vector
            def _(dve):
                dve.memset(c.ones[:, :], 1.0)
                dve.memset(c.ones_d[:, :], 1.0 / D)
                dve.memset(c.rms_eps[:, :], RMS_EPS)
                dve.memset(c.ln_eps[:, :], LN_EPS)
                dve.memset(c.ones_h[:, :], 1.0 / 512)
                dve.wait_ge(tables, 64)
                dve.tensor_scalar(c.masks[:, LEVELS:, :], c.masks[:, LEVELS:, :], 1.0, 1e30, ALU.subtract,
                                  ALU.mult).then_inc(memsets, 1)
        X, H, MR, HR = tile_of(c.X), tile_of(c.H), tile_of(c.MR), tile_of(c.HR)
        g = lambda name: lambda k: c.vec(name, k)
        scaled_copy = lambda dve, k, n: dve.tensor_scalar(X(k, n), H(k, n), ALPHA, None, ALU.mult)
        ones_d, ln_eps, rms_eps = c.ones_d[:, :], c.ln_eps[:, :], c.rms_eps[:, :]
        pre = ((0, "w_in_cm_2", 0), (1, "w_in_cm_2", 1), (2, "w_in_v_2", 0))
        plan = [
            (1, lambda f: block1_project(c)),
            (1, lambda f: block1_hgrn(c, f(((0, "w_out", 0), (1, "w_out", 1))))),
            (1, lambda f: w_out_stage(c, "out1", "w_out", (), ALPHA)),
            (1, lambda f: layer_norm_stage(c, "ln1", X, H, KT, ones_d, ln_eps, g("ln1_g"), g("ln1_b"), copies=scaled_copy, hi=MR, lo=HR,
                                           prefetch=f(((0, "w_up", 0), (1, "w_down", 0))))),
            (1, lambda f: ffn_stage(c, "ffn1", "w_up", "w_down", 22, conv=True)),
            (1, lambda f: layer_norm_stage(c, "ln2", X, X, KT, ones_d, ln_eps, g("ln2_g"), g("ln2_b"))),
            (2, lambda f: layer_norm_stage(c, "rms1", X, H, KT, ones_d, rms_eps, g("norm_mix_g_2"), centre=False,
                                           prefetch=f(pre))),
            (2, lambda f: block2_project(c)),
            (2, lambda f: layer_norm_stage(c, "cln", tile_of(c.M), tile_of(c.M), 4, c.ones_h[:, :], rms_eps,
                                           g("conv_ln_g_2"), g("conv_ln_b_2"), func=ACT.Silu,
                                           prefetch=f(((0, "w_pw_2", 0),)))),
            (2, lambda f: block2_pointwise(c, ())),
            (2, lambda f: block2_attention(c, f(((0, "w_out_2", 0), (1, "w_out_2", 1))))),
            (2, lambda f: w_out_stage(c, "out2", "w_out_2", (), 1.0)),
            (2, lambda f: layer_norm_stage(c, "rms2", X, H, KT, ones_d, rms_eps, g("norm_ffn_g_2"), centre=False, hi=MR, lo=HR,
                                           prefetch=f(((0, "w_up_2", 0), (1, "w_down_2", 0))))),
            (2, lambda f: ffn_stage(c, "ffn2", "w_up_2", "w_down_2", 16)),
            (2, lambda f: layer_norm_stage(c, "rms3", X, X, KT, ones_d, rms_eps, g("norm_final_g_2"), centre=False)),
        ]
        ada = lambda first, of=0: lambda k: c.ada[:, 2 * (first + k) + of:2 * (first + k) + of + 1]
        ctx_tile = lambda k, n: c.T[:, k // 4, (k % 4) * CTX:(k % 4 + 1) * CTX]
        next_x = lambda dve, k, n: dve.tensor_scalar(X(k, n), X(k, n), ALPHA, c.gate_bias[:, k:k + 1], ALU.mult, ALU.add)
        plan += [
            (3, lambda f: block3_ada(c, f(((0, "w_k_3", 0), (1, "w_gates_3", 0), (2, "w_in_vv_3", 0))))),
            (3, lambda f: layer_norm_stage(c, "cln3", ctx_tile, ctx_tile, KT, ones_d, ln_eps, ada(8, 1), ada(0, 1),
                                           halves=1, width=CTX, arrive=c.ctx_landed, scratch=False)),
            (3, lambda f: block3_context(c, ())),
            (3, lambda f: layer_norm_stage(c, "mod1", X, H, KT, ones_d, ln_eps, ada(8), ada(0), scratch=False,
                                           prefetch=f(((0, "w_gates_3", 0), (1, "w_in_cm_3", 1), (2, "w_in_v_3", 0))))),
            (3, lambda f: block3_project(c)),
            (3, lambda f: block3_gates(c, ())),
            (3, lambda f: block3_mlstm(c, ())),
            (3, lambda f: block3_head_norm(c, f(((0, "w_out_3", 0), (1, "w_out_3", 1))))),
            (3, lambda f: w_out_stage(c, "out3", "w_out_3", (), None, gate=32)),
            (3, lambda f: layer_norm_stage(c, "ln1_3", X, X, KT, ones_d, ln_eps, g("ln1_g_3"), g("ln1_b_3"),
                                           prefetch=f(((0, "w1_3", 0), (1, "w2_3", 0))))),
            (3, lambda f: layer_norm_stage(c, "mod2", X, H, KT, ones_d, ln_eps, ada(32), ada(24), copies=next_x, hi=MR, lo=HR)),
            (3, lambda f: ffn_stage(c, "ffn3", "w1_3", "w2_3", 16, bias="b1_3", gate=ada(40))),
            (3, lambda f: layer_norm_stage(c, "ln2_3", X, X, KT, ones_d, ln_eps, g("ln2_g_3"), g("ln2_b_3"))),
            (3, lambda f: store_stage(c, stored)),
        ]
        todo = [s for b, s in plan if b in blocks][:upto]
        for n, s in enumerate(todo):
            s(lambda loads, n=n: loads if n + 1 < len(todo) else ())


def slabs(w):
    n = w.shape[1] // 256
    return w.reshape(KT, P, n, 256).transpose(2, 1, 0, 3).reshape(n * P, SLAB)


def wide_slab(w):
    return w.reshape(KT, P, HALF).transpose(1, 0, 2).reshape(P, KT * HALF)


def down_slabs(w):
    n = w.shape[0] // 256
    return w.reshape(n, 2, P, D).transpose(0, 2, 1, 3).reshape(n * P, SLAB)


def layouts(a):
    w_in, w2 = a["w_in"][0], a["w_in_2"][0]
    rows = np.zeros((P, 4), np.float32)
    rows[0:8, 0] = a["b_forget_2"][0]
    w3, gates = a["w_in_3"][0], np.zeros((D, P), np.float32)
    for j in range(4):
        rows[32 * j:32 * j + 4, 1] = a["b_gates_3"][0, 4 * j:4 * j + 4]
        gates[:, 32 * j:32 * j + 4] = w3[:, 2560 + 4 * j:2564 + 4 * j]
    sel, sel2 = np.zeros((ROWS, 8, P), np.float32), np.zeros((ROWS, 4, P), np.float32)
    for j in range(8):
        row = 32 * (j // 4) + j % 4
        sel[row, j] = 1.0
        sel2[row, j // 2, 64 * (j % 2):64 * (j % 2) + 64] = 1.0
    cols = []
    for name, n in param_spec():
        cols.append(a[name].reshape(n, P).T)
    s, t = np.arange(P)[:, None], np.arange(P)[None, :]
    masks = []
    for r in range(LEVELS):
        m = 64 >> r
        masks.append((s // (2 * m) == t // (2 * m)) & (s % (2 * m) < m) & (t % (2 * m) >= m))
    masks += [s <= t, s >= t]
    inv = np.stack([1.0 / np.minimum(np.arange(1, 17), 2 ** (g + 1)) for g in range(4)]).reshape(1, 64)
    return {
        "x": a["x"][0].T.reshape(KT, P, T).transpose(1, 0, 2),
        "params": np.concatenate(cols, axis=1),
        "ident": np.eye(P, dtype=np.float32),
        "masks": np.stack(masks, axis=1).astype(np.float32),
        "inv_count": np.repeat(inv, P, axis=0).astype(np.float32),
        "pool_w": a["pool_w"][0].transpose(1, 0, 2).reshape(P, 512),
        "w_in_cm": slabs(np.concatenate([w_in[:, 0:1536], w_in[:, 2048:2560]], axis=1)),
        "w_in_v": wide_slab(w_in[:, 1536:2048]),
        "w_out": slabs(a["w_out"][0]),
        "w_up": slabs(np.concatenate([a["w_up"][0].reshape(D, 2, 22, P)[:, s, c] for c in range(22) for s in range(2)], axis=1)),
        "w_down": a["w_down"][0],
        "group_ones": np.kron(np.eye(2), np.full((64, 64), 1.0 / 64)).astype(np.float32),
        "row_params": rows,
        "w_in_cm_2": slabs(np.concatenate([w2[:, 1536:2560], w2[:, 0:1024]], axis=1)),
        "w_in_v_2": wide_slab(w2[:, 1024:1536]),
        "w_f_2": w2[:, 2560:2568].reshape(KT, P, 8).transpose(1, 0, 2).reshape(P, 64),
        "w_pw_2": a["w_conv_pw_2"][0].reshape(4, P, 512).transpose(1, 0, 2).reshape(P, SLAB),
        "w_out_2": slabs(a["w_out_2"][0]),
        "w_up_2": slabs(a["w_ffn_up_2"][0]),
        "w_down_2": down_slabs(a["w_ffn_down_2"][0]),
        "w_ada_3": slabs(a["w_ada_3"][0]),
        "ctx": a["ctx_3"][0].T.reshape(KT, P, CTX).transpose(1, 0, 2).reshape(P, KT * CTX),
        "w_k_3": slabs(w3[:, 1280:1536]),
        "w_gates_3": gates.reshape(KT, P, P).transpose(1, 0, 2).reshape(P, KT * P),
        "w_in_cm_3": slabs(np.concatenate([w3[:, 0:512], w3[:, 1024:1536], w3[:, 2048:2560]], axis=1)),
        "w_in_v_3": wide_slab(w3[:, 512:1024]),
        "w_in_vv_3": wide_slab(w3[:, 1536:2048]),
        "ln_v_rows": np.broadcast_to(np.concatenate([a["ln_v_g_3"][0], a["ln_v_b_3"][0]]), (P, 1024)),
        "w_s_3": a["w_s_3"][0].transpose(2, 0, 1).reshape(P, 512),
        "b_s_3": a["b_s_3"][0].reshape(1, 512),
        "sel": sel.reshape(ROWS, 8 * P),
        "sel2": sel2.reshape(ROWS, 4 * P),
        "w_out_3": slabs(a["w_out_3"][0]),
        "w1_3": slabs(a["w1_3"][0]),
        "w2_3": down_slabs(a["w2_3"][0]),
    }


def kernel(**inputs):
    import concourse.bacc as bacc
    from concourse.bass_utils import run_bass_kernel_spmd

    arrays = layouts({k: np.asarray(v) for k, v in inputs.items()})
    arrays = {k: np.ascontiguousarray(v) for k, v in arrays.items()}
    nc = bacc.Bacc("TRN2", target_bir_lowering=False, num_devices=1)
    aps = {k: nc.dram_tensor(f"in_{k}", v.shape, F32, kind="ExternalInput").ap() for k, v in arrays.items()}
    out = nc.dram_tensor("out", (P, KT, T), F32, kind="ExternalOutput").ap()
    build(nc, aps, out)
    r = run_bass_kernel_spmd(nc, [{f"in_{k}": v for k, v in arrays.items()}], core_ids=[0])
    return r.results[0]["out"].transpose(1, 0, 2).reshape(1, D, T).transpose(0, 2, 1)
```

```python
from contextlib import ExitStack, contextmanager

import numpy as np

import concourse.bass as bass
from concourse import mybir
from concourse.alu_op_type import AluOpType as ALU

ACT = mybir.ActivationFunctionType
F32 = mybir.dt.float32
F32R = mybir.dt.float32r
AX_X = mybir.AxisListType.X
ds = bass.ds

P = 128
D = 1024
T = 1024
KT = D // P
HALF = 512
SLAB = 2048
PRE = 4
ALPHA = 2.0 ** 0.25
LN_EPS, RMS_EPS = 1e-5, 1e-6
LEVELS = 7
CH = 128
NC_ = T // CH
CTX = 256
TT = T + CTX


def param_spec():
    return [
        ("pool_scale", 4), ("hgrn_lb", 8), ("hgrn_gnorm", 1), ("ln1_g", 8), ("ln1_b", 8),
        ("conv_w", 3 * 44), ("conv_b", 44), ("ln2_g", 8), ("ln2_b", 8),
        ("norm_mix_g_2", 8), ("conv_dw_w_2", 31 * 4), ("conv_dw_b_2", 4), ("conv_ln_g_2", 4),
        ("conv_ln_b_2", 4), ("b_conv_pw_2", 4), ("attn_out_g_2", 4), ("conv_out_g_2", 4),
        ("norm_ffn_g_2", 8), ("norm_final_g_2", 8),
        ("c_3", 8), ("c_ctx_3", 8), ("b_ada_3", 48), ("ln_v_g_3", 4), ("ln_v_b_3", 4),
        ("conv_qk_3", 3 * 4), ("hn_g_3", 4), ("ln1_g_3", 8), ("ln1_b_3", 8), ("b1_3", 32),
        ("b2_3", 8), ("ln2_g_3", 8), ("ln2_b_3", 8),
    ]


def param_columns():
    at, n = {}, 0
    for name, width in param_spec():
        at[name] = (n, width)
        n += width
    return at, n


class Core:

    def __init__(self, nc, ctx, inputs, out):
        self.nc, self.inp, self.out = nc, inputs, out

        def sb(name, shape, dt=F32):
            return ctx.enter_context(nc.sbuf_tensor(name, shape, dt))

        base = nc.sbuf_base + -nc.sbuf_base % 32
        sb("arena", [P, 48, T])

        def over(name, first, shape, dt=F32):
            return nc.alloc_sbuf_tensor_at(name, shape, dt, offset=base + first * T * 4)

        self.X = over("residual", 0, [P, KT, T])
        self.H = over("gemm_input", 8, [P, KT, T])
        self.M = over("mixer", 16, [P, 20, T])
        self.T = over("scratch", 36, [P, 4, T])
        self.W = over("weight_slots", 40, [P, 4, SLAB])
        self.XR = over("residual_r", 0, [P, KT, T], F32R)
        self.HR = over("gemm_input_r", 8, [P, KT, T], F32R)
        self.MR = over("mixer_r", 28, [P, KT, T], F32R)
        self.hidR = over("hidden_r", 16, [P, 8, T], F32R)
        self.WR = over("weights_r", 44, [P, 4, T], F32R)
        self.downR = over("down_r", 36, [P, 4, T], F32R)
        self.down1R = over("down1_r", 26, [P, 2, T], F32R)
        self.spill = nc.dram_tensor("residual_spill", (P, KT, T), F32, kind="Internal").ap()
        self.par = sb("params", [P, param_columns()[1]])
        self.ident = sb("ident", [P, P])
        self.masks = sb("masks", [P, LEVELS + 2, P])
        self.ones_d = sb("ones_d", [P, P])
        self.ones = sb("ones", [P, P])
        self.small = sb("small", [P, 64])
        self.group_ones = sb("group_ones", [P, P])
        self.from_below, self.from_above = self.masks[:, LEVELS, :], self.masks[:, LEVELS + 1, :]
        self.rows = sb("rows", [P, TT])
        self.ada = sb("ada", [P, 96])
        self.gate_bias = sb("gate_bias", [P, 8])
        self.gate_tmp = sb("v_rstd", [P, 8])
        self.row_par = sb("row_params", [P, 4])
        self.ones_h = sb("ones_half", [P, P])
        self.PS = ctx.enter_context(nc.psum_tensor("psum", [P, 8, 512], F32))
        self.landed = [ctx.enter_context(nc.semaphore(f"slab_landed_{i}")) for i in range(4)]
        self.loads = [0] * 4
        self.retired, self.stages = [], 0

    def vec(self, name, j=0, n=1):
        at = param_columns()[0][name][0]
        return self.par[:, at + j:at + j + n]

    def mask(self, level):
        return self.masks[:, level:level + 1, :].to_broadcast([P, NC_, P])

    @contextmanager
    def stage(self, *names):
        nc = self.nc
        self.stages += 1
        sems = [nc.alloc_semaphore(name=f"{n}_{self.stages}") for n in names]
        retired, self.retired = self.retired, sems
        with nc.Block() as block:
            if retired:
                @block.gpsimd
                def _(pool):
                    for s in retired:
                        pool.sem_clear(s)

            yield (block, *sems)
        for s in retired:
            nc.release_semaphore(s)

    def load(self, sp, slot, name, i):
        w = self.inp[name]
        width = w.shape[1]
        dst = self.W[:, slot, 0:width] if width <= SLAB else self.W[:, slot:slot + 2, :].rearrange("p a b -> p (a b)")
        sp.dma_start(dst, w[ds(i * P, P), :]).then_inc(self.landed[slot], 16)


def project_pe(c, pe, products, drained, w_ready, loops, hi, lo, g0=0, h0=0, lo_ready=None):
    with pe.Fori(0, loops) as i:
        for j in range(4):
            pe.wait_ge(w_ready, h0 + j + 1 + i * 4)
            for n in range(2):
                if lo_ready is not None:
                    pe.wait_ge(lo_ready, (n + 1) * KT)
                pe.wait_ge(drained, g0 + 2 * j + n + 1 + i * 8)
                half_slab_pe(c, pe, (g0 + 2 * j + n) % 8, j % 2, n, hi, lo).then_inc(products, 1)


def half_slab_pe(c, pe, bank, buf, n, hi, lo):
    half = slice(n * HALF, (n + 1) * HALF)
    for k in range(KT):
        w_hi, w_lo = c.WR[:, 2 * buf, k * P:(k + 1) * P], c.WR[:, 2 * buf + 1, k * P:(k + 1) * P]
        pe.matmul(c.PS[:, bank, :], w_hi, hi[:, k, half], start=k == 0, stop=False)
        pe.matmul(c.PS[:, bank, :], w_hi, lo[:, k, half], start=False, stop=False)
        mm = pe.matmul(c.PS[:, bank, :], w_lo, hi[:, k, half], start=False, stop=k == KT - 1)
    return mm


def token_major_pe(c, pe, products, drained, w_ready, pieces, hi, lo, g0, h0, slabs_=2):
    for s_ in range(slabs_):
        for x in range(2):
            w_hi, w_lo = [c.WR[:, 2 * x + y, :].rearrange("p (k n) -> p k n", n=256) for y in range(2)]
            pe.wait_ge(w_ready, h0 + 2 * s_ + x + 1)
            for t in range(NC_):
                g, at = g0 + 8 * s_ + t, slice(t * P, (t + 1) * P)
                out = c.PS[:, g % 8, 0:256]
                if x == 0:
                    pe.wait_ge(drained, g + 1)
                for k in range(4):
                    kk = 4 * x + k
                    pe.matmul(out, hi[:, kk, at], w_hi[:, k, :], start=kk == 0, stop=False)
                    pe.matmul(out, hi[:, kk, at], w_lo[:, k, :], start=False, stop=False)
                    mm = pe.matmul(out, lo[:, kk, at], w_hi[:, k, :], start=False, stop=kk == KT - 1)
                if x == 1:
                    mm.then_inc(products, 1)
            if x == 0:
                mm.then_inc(pieces, 1)


def pool_round(c, pool, out, x):
    one = c.ones[:, 0:1].unsqueeze(2).to_broadcast(list(x.shape))
    return pool.tensor_tensor(out, x, one, ALU.mult)


class Split:

    def __init__(self, c, pool, products, w_step, w_ready, pieces=None):
        self.c, self.pool, self.products, self.w_step, self.w_ready = c, pool, products, w_step, w_ready
        self.pieces = pieces
        self.base, self.slab, self.steps, self.wholes, self.last = list(c.loads), 0, 0, 0, None

    def split(self, raw, parts, step, count=1):
        pool_round(self.c, self.pool, parts[0], raw).then_inc(self.w_step, 1)
        self.pool.wait_ge(self.w_step, step)
        self.pool.tensor_tensor(parts[1], raw, parts[0].bitcast(F32), ALU.subtract).then_inc(self.w_ready, count)

    def halves(self, loops, g0):
        c, pool = self.c, self.pool
        with pool.Fori(0, loops) as i:
            for j in range(4):
                m, at = j % 2, self.slab + j // 2
                if m == 0:
                    pool.wait_ge(c.landed[at % 2], self.base[at % 2] + 16 * (at // 2 + 1) + i * 16)
                pool.wait_ge(self.products, PRE + g0 + 2 * j - 2 + i * 8)
                raw = c.W[:, at % 2, :].rearrange("p (k n) -> p k n", n=256)[:, :, m * P:(m + 1) * P]
                self.split(raw, [c.WR[:, 2 * m + x, :].rearrange("p (k n) -> p k n", n=P) for x in range(2)],
                           self.steps + j + 1 + i * 4)
        self.slab += 2 * loops
        self.steps += 4 * loops
        self.last = "halves"

    def half(self, g0, buf):
        c, pool, slot = self.c, self.pool, self.slab % 2
        pool.wait_ge(c.landed[slot], self.base[slot] + 16 * (self.slab // 2 + 1))
        if g0:
            pool.wait_ge(self.products, PRE + g0 - 2)
        raw = c.W[:, slot, :].rearrange("p (k n) -> p k n", n=256)[:, :, 0:P]
        self.steps += 1
        self.split(raw, [c.WR[:, 2 * buf + x, :].rearrange("p (k n) -> p k n", n=P) for x in range(2)], self.steps, 2)
        self.slab += 1
        self.last = "half"

    def whole(self, g0):
        c, pool, slot = self.c, self.pool, self.slab % 2
        pool.wait_ge(c.landed[slot], self.base[slot] + 16 * (self.slab // 2 + 1))
        for x in range(2):
            if self.last == "whole" and x == 0:
                pool.wait_ge(self.pieces, self.wholes)
            elif self.last is not None:
                pool.wait_ge(self.products, PRE + g0 - 2 * (1 - x))
            self.steps += 1
            self.split(c.W[:, slot:slot + 1, x * T:(x + 1) * T],
                       [c.WR[:, 2 * x + y:2 * x + y + 1, :] for y in range(2)], self.steps)
        self.slab += 1
        self.wholes += 1
        self.last = "whole"




def stream(c, sp, w_ready, name, slabs_):
    with sp.Fori(1, slabs_ // 2) as i:
        for slot in range(2):
            sp.wait_ge(w_ready, 2 * slot - 2 + i * 4)
            c.load(sp, slot, name, slot + i * 2)
    if slabs_ % 2:
        sp.wait_ge(w_ready, 2 * (slabs_ - 2))
        c.load(sp, 0, name, slabs_ - 1)


def stream_done(c, slabs_):
    c.loads[0] += 16 * ((slabs_ + 1) // 2)
    c.loads[1] += 16 * (slabs_ // 2)


def evacuate_token_major(act, c, products, drained, out, g0, slabs_=2):
    for s_ in range(slabs_):
        for t in range(NC_):
            act.wait_ge(products, PRE + g0 + 8 * s_ + t + 1)
            act.activation(out[:, t, s_ * 256:(s_ + 1) * 256], c.PS[:, (g0 + t) % 8, 0:256],
                           ACT.Copy).then_inc(drained, 1)


def w_out_stage(c, name, w, prefetch, scale, gate=None):
    with c.stage("products", "drained", "w_step", "w_ready", "hi_ready", "lo_ready") as (
            block, products, drained, w_step, w_ready, hi_ready, lo_ready):
        @block.sync
        def _(sp):
            stream(c, sp, w_ready, w, 4)
            prefetch_after(c, sp, products, PRE + 16, prefetch)

        @block.gpsimd
        def _(pool):
            Split(c, pool, products, w_step, w_ready).halves(2, 0)

        @block.tensor
        def _(pe):
            pe.sem_inc(products, PRE)
            project_pe(c, pe, products, drained, w_ready, 2, c.MR, c.HR, lo_ready=lo_ready)

        @block.scalar
        def _(act):
            for n in range(2):
                for k in range(KT):
                    half = slice(n * HALF, (n + 1) * HALF)
                    act.activation(c.MR[:, k, half], c.H[:, k, half], ACT.Copy).then_inc(hi_ready, 1)

        @block.vector
        def _(dve):
            dve.sem_inc(drained, 8)
            for n in range(2):
                for k in range(KT):
                    half = slice(n * HALF, (n + 1) * HALF)
                    dve.wait_ge(hi_ready, n * KT + k + 1)
                    dve.tensor_tensor(c.HR[:, k, half], c.H[:, k, half], c.MR[:, k, half].bitcast(F32),
                                      ALU.subtract).then_inc(lo_ready, 1)
            with dve.Fori(0, 2) as i:
                for j in range(8):
                    dve.wait_ge(products, PRE + j + 1 + i * 8)
                    x = c.X[:, ds(i * 4 + j // 2, 1), (j % 2) * HALF:(j % 2 + 1) * HALF]
                    ps = c.PS[:, j:j + 1, :]
                    if gate is None:
                        dve.scalar_tensor_tensor(out=x, in0=x, scalar=scale, in1=ps, op0=ALU.mult,
                                                 op1=ALU.add).then_inc(drained, 1)
                    else:
                        dve.scalar_tensor_tensor(out=x, in0=ps, scalar=c.ada[:, ds(i * 8 + gate + j // 2 * 2, 1)],
                                                 in1=x, op0=ALU.mult, op1=ALU.add).then_inc(drained, 1)
    stream_done(c, 4)


def prefetch_after(c, sp, sem, value, loads):
    if loads:
        if sem is not None:
            sp.wait_ge(sem, value)
        for slot, w, i in loads:
            c.load(sp, slot, w, i)


def layer_norm_stage(c, src, dst, tiles, ones, eps, g, b=None, centre=True, copies=None, prefetch=(),
                     func=ACT.Identity, halves=2, width=HALF, arrive=None, scratch=True,
                     hi=None, lo=None, spill=False, store=None):
    R = 4
    halfs = lambda a: a.rearrange("p a b -> p (a b)").rearrange("p (a n) -> p a n", n=HALF)[:, :, 0:width]
    sq = halfs(c.M[:, 1:3, :] if arrive else c.T[:, 0:2, :])
    sums = [sq, halfs(c.T[:, 2:4, :] if scratch else c.M[:, 3:5, :])]
    rstd = halfs(c.T[:, 2:3, :] if scratch else c.M[:, 0:1, :])
    affine = b is not None or func != ACT.Identity
    bias = lambda k: b(k) if b else 0.0
    each = [(n, k, n * tiles + k) for n in range(halves) for k in range(tiles)]
    with c.stage("spilled", "sums_dve", "sums_pool", "mean_done", "centred", "squared", "squares_used", "std_ready",
                 "rstd_ready", "scaled", "hi_ready", "written", "copied", "lo_ready") as (
            block, spilled, sums_dve, sums_pool, mean_done, centred, squared, squares_used, std_ready, rstd_ready,
            scaled, hi_ready, written, copied, lo_ready):
        def pair_sums(eng, pairs, done):
            if arrive:
                eng.wait_ge(arrive, 16)
            for n in range(halves):
                for q in pairs:
                    eng.tensor_tensor(sums[n][:, q, :], src(2 * q, n), src(2 * q + 1, n), ALU.add).then_inc(done, 1)

        of_dve, of_pool = range(0, tiles // 4), range(tiles // 4, tiles // 2)

        @block.sync
        def _(sp):
            if spill:
                sp.dma_start(c.spill, c.X[:, :, :]).then_inc(spilled, 16)
            prefetch_after(c, sp, None, 0, prefetch)
            if spill:
                sp.wait_ge(spilled, 16)
            if store is not None:
                for n, a, e in ((0, 0, 8), (1, 0, 4), (1, 4, 8)):
                    sp.wait_ge(written, n * tiles + e)
                    half = slice(n * HALF, (n + 1) * HALF)
                    sp.dma_start(c.out[:, a:e, half], c.X[:, a:e, half]).then_inc(store[n + a // 4], 16)
                for stored in store:
                    sp.wait_ge(stored, 16)

        @block.gpsimd
        def _(pool):
            if centre:
                pair_sums(pool, of_pool, sums_pool)
            if copies is not None:
                for n, k, i in each:
                    pool.wait_ge(written, i + 1)
                    copies(pool, k, n).then_inc(copied, 1)

        @block.tensor
        def _(pe):
            if centre:
                for n in range(halves):
                    for q in range(tiles // 2):
                        if q in of_dve:
                            pe.wait_ge(sums_dve, n * len(of_dve) + q + 1)
                        else:
                            pe.wait_ge(sums_pool, n * len(of_pool) + q - len(of_dve) + 1)
                        mm = pe.matmul(c.PS[:, n, 0:width], ones, sums[n][:, q, :], start=q == 0,
                                       stop=q == tiles // 2 - 1)
                    mm.then_inc(mean_done, 1)
            for n, k, i in each:
                pe.wait_ge(squared, i + 1)
                pe.matmul(c.PS[:, 2 + n, 0:width], ones, sq[:, i % R, :], start=k == 0,
                          stop=k == tiles - 1).then_inc(squares_used, 1)

        @block.scalar
        def _(act):
            def load_ln_table():
                act.activation(c.gate_tmp[:, 0:1], c.ones[:, 0:1], ACT.Ln)

            load_ln_table()
            for n, k, i in each:
                if centre:
                    act.wait_ge(centred, i + 1)
                if i >= R:
                    act.wait_ge(squares_used, i - R + 1)
                act.activation(sq[:, i % R, :], (dst if centre else src)(k, n), ACT.Square).then_inc(squared, 1)
            if spill:
                act.wait_ge(spilled, 16)
            for n in range(halves):
                act.wait_ge(squares_used, (n + 1) * tiles)
                act.activation(rstd[:, n, :], c.PS[:, 2 + n, 0:width], ACT.Ln, bias=eps).then_inc(std_ready, 1)
                act.wait_ge(std_ready, n + 1)
                act.activation(rstd[:, n, :], rstd[:, n, :], ACT.Exp, scale=-0.5).then_inc(rstd_ready, 1)
                if n + 1 < halves:
                    load_ln_table()
                for k in range(tiles):
                    i = n * tiles + k
                    if affine:
                        act.wait_ge(scaled, i + 1)
                        if hi:
                            act.activation(hi(k, n), dst(k, n), func, scale=g(k), bias=bias(k)).then_inc(hi_ready, 1)
                            act.wait_ge(hi_ready, i + 1)
                        act.activation(dst(k, n), dst(k, n), func, scale=g(k), bias=bias(k)).then_inc(written, 1)
                    elif hi:
                        act.wait_ge(written, i + 1)
                        act.activation(hi(k, n), dst(k, n), ACT.Copy).then_inc(hi_ready, 1)

        @block.vector
        def _(dve):
            if centre:
                pair_sums(dve, of_dve, sums_dve)
                for n in range(halves):
                    dve.wait_ge(mean_done, n + 1)
                    for k in range(tiles):
                        dve.tensor_tensor(dst(k, n), src(k, n), c.PS[:, n, 0:width], ALU.subtract).then_inc(centred, 1)
            for n in range(halves):
                dve.wait_ge(rstd_ready, n + 1)
                for k in range(tiles):
                    x = (dst if centre else src)(k, n)
                    if affine:
                        dve.tensor_tensor(dst(k, n), x, rstd[:, n, :], ALU.mult).then_inc(scaled, 1)
                    else:
                        dve.scalar_tensor_tensor(out=dst(k, n), in0=x, scalar=g(k), in1=rstd[:, n, :], op0=ALU.mult,
                                                 op1=ALU.mult).then_inc(written, 1)
                for k in range(tiles if hi else 0):
                    i = n * tiles + k
                    dve.wait_ge(written, i + 1)
                    dve.wait_ge(hi_ready, i + 1)
                    if copies is not None:
                        dve.wait_ge(copied, i + 1)
                    dve.tensor_tensor(lo(k, n), dst(k, n), hi(k, n).bitcast(F32), ALU.subtract).then_inc(lo_ready, 1)


def tile_of(buf, first=0):
    return lambda k, n: buf[:, first + k, n * HALF:(n + 1) * HALF]


def block1_project(c):
    M, H, S = c.M, c.H, c.small
    V = M[:, 16:20, :].rearrange("p a (b n) -> p (a b) n", n=HALF)
    reset = c.T[:, 0, :]
    sums = [c.T[:, 1, :], c.T[:, 2, :]]
    fix = S[:, 32:48]
    with c.stage("products", "drained", "sig", "forget", "logf", "bounds", "exps", "pooled", "d_ready", "consts", "pw",
                 "gates", "chain", "w_step", "w_ready", "pieces", "hi_ready", "lo_ready", "g_ready") as (
            block, products, drained, sig, forget, logf, bounds, exps, pooled, d_ready, consts, pw_landed, gates, chain,
            w_step, w_ready, pieces, hi_ready, lo_ready, g_ready):
        pool_w = c.T[:, 3, 0:512]
        inv = c.T[:, 3, 512:576]

        @block.sync
        def _(sp):
            sp.dma_start(pool_w, c.inp["pool_w"]).then_inc(pw_landed, 16)
            sp.dma_start(inv, c.inp["inv_count"]).then_inc(gates, 16)
            stream(c, sp, w_ready, "w_in", 10)

        @block.tensor
        def _(pe):
            pe.sem_inc(products, PRE)
            project_pe(c, pe, products, drained, w_ready, 4, c.HR, c.XR, lo_ready=lo_ready)
            token_major_pe(c, pe, products, drained, w_ready, pieces, c.HR, c.XR, 32, 16)
            pe.wait_ge(pw_landed, 16)
            for g in range(4):
                pe.wait_ge(d_ready, g + 1)
                for n in range(2):
                    pe.wait_ge(drained, 48 + 2 * g + n + 1)
                    pe.matmul(c.PS[:, 2 * g + n, :], pool_w[:, g * P:(g + 1) * P], M[:, g, n * HALF:(n + 1) * HALF],
                              start=True, stop=True).then_inc(products, 1)

        @block.scalar
        def _(act):
            act.sem_inc(drained, 8)
            act.wait_ge(c.x_landed, 16)
            for n in range(2):
                for k in range(KT):
                    half = slice(n * HALF, (n + 1) * HALF)
                    act.activation(c.HR[:, k, half], c.X[:, k, half], ACT.Copy).then_inc(hi_ready, 1)
            act.wait_ge(bounds, 1)
            act.activation(S[:, 8:12], S[:, 0:4], ACT.Exp).then_inc(exps, 1)
            act.activation(S[:, 12:16], S[:, 4:8], ACT.Exp).then_inc(exps, 1)
            with act.Fori(0, 4) as i:
                for j in range(8):
                    act.wait_ge(products, PRE + j + 1 + i * 8)
                    act.activation(M[:, ds(i * 4 + j // 2, 1), (j % 2) * HALF:(j % 2 + 1) * HALF], c.PS[:, j:j + 1, :],
                                   ACT.Copy).then_inc(drained, 1)
            act.wait_ge(drained, 40)
            for h in range(4):
                act.activation(M[:, 8 + h, :], M[:, 8 + h, :], ACT.Sigmoid).then_inc(sig, 1)
            for h in range(4):
                act.activation(M[:, 4 + h, :], M[:, 4 + h, :], ACT.Silu).then_inc(g_ready, 1)
                act.activation(M[:, 12 + h, :], M[:, 12 + h, :], ACT.Silu).then_inc(g_ready, 1)
            evacuate_token_major(act, c, products, drained, V, 32)
            for h in range(4):
                act.wait_ge(forget, 4 + h + 1)
                act.activation(M[:, 8 + h, :], M[:, 8 + h, :], ACT.Ln).then_inc(logf, 1)
            for g in range(4):
                for n in range(2):
                    act.wait_ge(products, PRE + 48 + 2 * g + n + 1)
                    act.activation(H[:, g, n * HALF:(n + 1) * HALF], c.PS[:, 2 * g + n, :], ACT.Identity,
                                   scale=c.vec("pool_scale", g)).then_inc(drained, 1)

        @block.gpsimd
        def _(pool):
            split = Split(c, pool, products, w_step, w_ready, pieces)
            split.halves(4, 0)
            split.whole(32)
            split.whole(40)
            pool.memset(reset, 1.0).then_inc(consts, 1)
            pool.wait_ge(consts, 1)
            pool.memset(c.T[:, 0, :].rearrange("p (a b) -> p a b", b=CH)[:, :, 0:1], 0.0).then_inc(consts, 1)

        @block.vector
        def _(dve):
            step = [0]

            def then(ins):
                step[0] += 1
                ins.then_inc(chain, 1)
                dve.wait_ge(chain, step[0])

            dve.wait_ge(c.x_landed, 16)
            for n in range(2):
                for k in range(KT):
                    half = slice(n * HALF, (n + 1) * HALF)
                    dve.wait_ge(hi_ready, n * KT + k + 1)
                    dve.tensor_tensor(c.XR[:, k, half], c.X[:, k, half], c.HR[:, k, half].bitcast(F32),
                                      ALU.subtract).then_inc(lo_ready, 1)
            dve.wait_ge(c.par_landed, 16)
            lb = c.vec("hgrn_lb", 0, 8)
            then(dve.tensor_tensor(S[:, 16:20], lb[:, 0:4], lb[:, 4:8], ALU.max))
            dve.tensor_tensor(S[:, 0:4], lb[:, 0:4], S[:, 16:20], ALU.subtract)
            dve.tensor_tensor(S[:, 4:8], lb[:, 4:8], S[:, 16:20], ALU.subtract).then_inc(bounds, 1)
            dve.wait_ge(exps, 2)
            then(dve.tensor_tensor(S[:, 16:20], S[:, 8:12], S[:, 12:16], ALU.add))
            then(dve.reciprocal(S[:, 16:20], S[:, 16:20]))
            then(dve.tensor_tensor(S[:, 20:24], S[:, 8:12], S[:, 16:20], ALU.mult))
            then(dve.tensor_scalar(S[:, 24:28], S[:, 20:24], -1.0, 1.0, ALU.mult, ALU.add))
            dve.wait_ge(drained, 40)
            dve.wait_ge(gates, 16)
            for g in range(4):
                a, turn = M[:, g, :], 0
                for lag in [2 ** j for j in range(g + 1)]:
                    s = sums[turn]
                    dve.tensor_copy(s[:, 0:lag], a[:, 0:lag])
                    then(dve.tensor_tensor(s[:, lag:T], a[:, lag:T], a[:, 0:T - lag], ALU.add))
                    a, turn = s, 1 - turn
                then(dve.tensor_tensor(fix, a[:, 0:16], inv[:, g * 16:(g + 1) * 16], ALU.mult))
                then(dve.tensor_tensor(fix, fix, M[:, g, 0:16], ALU.subtract))
                then(dve.scalar_tensor_tensor(out=M[:, g, :], in0=a, scalar=1.0 / 2 ** (g + 1), in1=M[:, g, :],
                                              op0=ALU.mult, op1=ALU.subtract))
                dve.tensor_copy(M[:, g, 0:16], fix).then_inc(d_ready, 1)
            for h in range(4):
                dve.wait_ge(sig, h + 1)
                dve.tensor_scalar(M[:, 8 + h, :], M[:, 8 + h, :], S[:, 24 + h:25 + h], S[:, 20 + h:21 + h], ALU.mult,
                                  ALU.add).then_inc(forget, 1)
            dve.wait_ge(products, PRE + 48)
            for h in range(4):
                dve.wait_ge(forget, h + 1)
                dve.tensor_scalar(H[:, 4 + h, :], M[:, 8 + h, :], -1.0, 1.0, ALU.mult, ALU.add).then_inc(forget, 1)
            dve.wait_ge(consts, 2)
            for h in range(4):
                dve.wait_ge(logf, h + 1)
                then(dve.tensor_tensor_scan(sums[h % 2], reset, M[:, 8 + h, :], 0.0, ALU.mult, ALU.add))
                dve.tensor_copy(M[:, 8 + h, :], sums[h % 2])
    stream_done(c, 10)


def block1_hgrn(c, prefetch):
    M, H, PS = c.M, c.H, c.PS
    Wl = [c.T[:, 0, :], c.T[:, 1, :]]
    E = [c.T[:, 2, :], c.T[:, 3, :]]
    Sm = [M[:, 0, :], M[:, 1, :]]
    Vh, St = M[:, 2, :], M[:, 3, :]
    V = M[:, 16:20, :].rearrange("p a (b n) -> p (a b) n", n=HALF)
    OUT, MEAN = PS[:, 4:6, :], PS[:, 6:8, :]
    ch = lambda a, i: a[:, i * CH:(i + 1) * CH]
    with c.stage("v_ready", "d_ready", "e_ready", "w_ready", "scores_done", "masked", "o_done", "squared", "mean_done",
                 "std_ready", "o_consumed", "chain", "written", "step", "x_back") as (
            block, v_ready, d_ready, e_ready, w_ready, scores_done, masked, o_done, squared, mean_done, std_ready,
            o_consumed, chain, written, stepped, x_back):

        def score_bank(r, i):
            return PS[:, 2 * (r % 2) + i // 4, (i % 4) * CH:(i % 4 + 1) * CH]

        @block.sync
        def _(sp):
            sp.dma_start(c.X[:, :, :], c.inp["x"]).then_inc(x_back, 16)
            prefetch_after(c, sp, None, 0, prefetch)
            sp.wait_ge(x_back, 16)

        @block.gpsimd
        def _(pool):
            with pool.Fori(0, 4) as h:
                pool.wait_ge(o_done, h * 9 + 1)
                pool.tensor_copy(Vh.rearrange("p (a b) -> p a b", b=CH), V[:, :, ds(h * CH, CH)]).then_inc(v_ready, 1)

        @block.tensor
        def _(pe):
            pe.sem_inc(o_done, 1)
            with pe.Fori(0, 4) as h:
                def scores(r):
                    pe.wait_ge(w_ready, h * 10 + r + 1)
                    if r >= 2:
                        pe.wait_ge(masked, h * 10 + r - 1)
                    for i in range(NC_):
                        rhs = c.M[:, ds(h + 4, 1), i * CH:(i + 1) * CH] if r == 7 else ch(Wl[r % 2], i)
                        mm = pe.matmul(score_bank(r, i), ch(Wl[r % 2], i), rhs, start=i % 4 == 0, stop=i % 4 == 3,
                                       skip_group_check=True)
                    mm.then_inc(scores_done, 1)

                def outputs(r):
                    pe.wait_ge(masked, h * 10 + r + 1)
                    for i in range(NC_):
                        mm = pe.matmul(OUT[:, i // 4, (i % 4) * CH:(i % 4 + 1) * CH], ch(Vh, i), ch(Sm[r % 2], i),
                                       start=r == 0 and i % 4 == 0, stop=False, skip_group_check=True)
                    mm.then_inc(o_done, 1)

                for r in range(8):
                    scores(r)
                    if r == 1:
                        pe.wait_ge(v_ready, h + 1)
                        pe.wait_ge(o_consumed, h + 1)
                    if r >= 1:
                        outputs(r - 1)
                pe.wait_ge(w_ready, h * 10 + 9)
                pe.wait_ge(masked, h * 10 + 7)
                for i in range(NC_):
                    mm = pe.transpose(score_bank(8, i), ch(Wl[0], i), c.ident[:, :])
                mm.then_inc(scores_done, 1)
                outputs(7)
                pe.wait_ge(masked, h * 10 + 9)
                for i in range(NC_):
                    mm = pe.matmul(score_bank(9, i), ch(Sm[0], i), ch(Vh, i), start=i % 4 == 0, stop=i % 4 == 3,
                                   skip_group_check=True)
                mm.then_inc(scores_done, 1)
                pe.wait_ge(masked, h * 10 + 10)
                pe.wait_ge(w_ready, h * 10 + 10)
                for i in range(1, NC_):
                    mm = pe.matmul(OUT[:, i // 4, (i % 4) * CH:(i % 4 + 1) * CH], ch(St, i), ch(Wl[1], i), start=False,
                                   stop=i % 4 == 3, skip_group_check=True)
                mm.then_inc(o_done, 1)
                pe.wait_ge(squared, h + 1)
                for n in range(2):
                    mm = pe.matmul(MEAN[:, n, :], c.ones[:, :], Sm[0][:, n * HALF:(n + 1) * HALF], start=True, stop=True)
                mm.then_inc(mean_done, 1)

        @block.scalar
        def _(act):
            def decays(h, levels):
                for q in levels:
                    act.wait_ge(d_ready, h * 8 + q + 1)
                    act.activation(E[q % 2], E[q % 2], ACT.Exp).then_inc(e_ready, 1)

            def body(h, more):
                decays(h, range(2, 8))
                act.wait_ge(w_ready, h * 10 + 7)
                act.activation(c.T[:, 2:3, :], M[:, ds(h + 8, 1), :], ACT.Exp).then_inc(e_ready, 1)
                act.wait_ge(o_done, h * 9 + 10)
                act.activation(Sm[0].rearrange("p (a n) -> p a n", n=HALF), OUT, ACT.Square).then_inc(squared, 1)
                if more:
                    decays(h + 1, range(2))
                act.wait_ge(mean_done, h + 1)
                act.activation(Sm[1].rearrange("p (a n) -> p a n", n=HALF), MEAN, ACT.Ln,
                               scale=1.0 / P, bias=c.rms_eps[:, :]).then_inc(std_ready, 1)
                act.wait_ge(std_ready, h * 2 + 1)
                act.activation(Sm[1], Sm[1], ACT.Exp, scale=-0.5).then_inc(std_ready, 1)

            decays(0, range(2))
            with act.Fori(0, 3) as h:
                body(h, True)
            body(3, False)

        @block.vector
        def _(dve):
            dve.sem_inc(o_consumed, 1)
            b = lambda h, m: M[:, ds(h + 8, 1), :].rearrange("p a (n m) -> p (a n) m", m=m)
            kk = lambda h, m: H[:, ds(h + 4, 1), :].rearrange("p a (n m) -> p (a n) m", m=m)
            qq = lambda h, m: M[:, ds(h + 4, 1), :].rearrange("p a (n m) -> p (a n) m", m=m)
            blocks = lambda a, m: a.rearrange("p (n m) -> p n m", m=m)

            def exponents(h, r):
                m = 64 >> r
                bv, e = b(h, 2 * m), blocks(E[r % 2], 2 * m)
                ref = bv[:, :, m - 1:m].to_broadcast([P, T // (2 * m), m])
                if r >= 2:
                    dve.wait_ge(w_ready, h * 10 + r - 1)
                dve.tensor_tensor(e[:, :, 0:m], ref, bv[:, :, 0:m], ALU.subtract)
                dve.tensor_tensor(e[:, :, m:2 * m], bv[:, :, m:2 * m], ref, ALU.subtract).then_inc(d_ready, 1)

            def decayed(h, r):
                m = 64 >> r
                e, w = blocks(E[r % 2], 2 * m), blocks(Wl[r % 2], 2 * m)
                dve.wait_ge(e_ready, h * 9 + r + 1)
                if r >= 2:
                    dve.wait_ge(scores_done, h * 10 + r - 1)
                dve.tensor_tensor(w[:, :, 0:m], kk(h, 2 * m)[:, :, 0:m], e[:, :, 0:m], ALU.mult)
                dve.tensor_tensor(w[:, :, m:2 * m], qq(h, 2 * m)[:, :, m:2 * m], e[:, :, m:2 * m],
                                  ALU.mult).then_inc(w_ready, 1)

            def masks(h, r):
                dve.wait_ge(scores_done, h * 10 + r + 1)
                if r >= 2:
                    dve.wait_ge(o_done, h * 9 + r)
                s = PS[:, 2 * (r % 2):2 * (r % 2) + 2, :].rearrange("p a (b n) -> p (a b) n", n=CH)
                mask = c.ident[:, :].unsqueeze(1).to_broadcast([P, NC_, P]) if r == 7 else c.mask(r)
                dve.tensor_tensor(blocks(Sm[r % 2], CH), s, mask, ALU.mult).then_inc(masked, 1)

            def first_levels(h):
                exponents(h, 0)
                exponents(h, 1)
                decayed(h, 0)
                exponents(h, 2)
                decayed(h, 1)

            def body(h, more):
                masks(h, 0)
                for r in range(2, LEVELS):
                    if r + 1 < LEVELS:
                        exponents(h, r + 1)
                    decayed(h, r)
                    masks(h, r - 1)
                dve.wait_ge(scores_done, h * 10 + 6)
                dve.tensor_scalar(blocks(Wl[1], T), kk(h, T), 1.0, None, ALU.mult).then_inc(w_ready, 1)
                bv = b(h, CH)
                dve.wait_ge(w_ready, h * 10 + 6)
                dve.tensor_tensor(blocks(E[1], CH), bv[:, :, CH - 1:CH].to_broadcast([P, NC_, CH]), bv,
                                  ALU.subtract).then_inc(d_ready, 1)
                masks(h, 6)
                dve.wait_ge(e_ready, h * 9 + 8)
                dve.wait_ge(scores_done, h * 10 + 7)
                dve.tensor_tensor(blocks(Wl[0], CH), kk(h, CH), blocks(E[1], CH), ALU.mult).then_inc(w_ready, 1)
                masks(h, 7)
                dve.wait_ge(e_ready, h * 9 + 9)
                dve.wait_ge(scores_done, h * 10 + 8)
                dve.tensor_tensor(blocks(Wl[1], CH), qq(h, CH), blocks(E[0], CH), ALU.mult).then_inc(w_ready, 1)
                dve.wait_ge(scores_done, h * 10 + 9)
                dve.wait_ge(o_done, h * 9 + 8)
                dve.tensor_copy(Sm[0].rearrange("p (a n) -> p a n", n=HALF), PS[:, 0:2, :]).then_inc(masked, 1)
                dve.wait_ge(scores_done, h * 10 + 10)
                dve.tensor_copy(ch(St, 1), score_bank(9, 0)).then_inc(stepped, 1)
                for i in range(2, NC_):
                    dve.wait_ge(stepped, h * 7 + i - 1)
                    ins = dve.scalar_tensor_tensor(out=ch(St, i), in0=ch(St, i - 1), scalar=E[0][:, i * CH - 1:i * CH],
                                                   in1=score_bank(9, i - 1), op0=ALU.mult, op1=ALU.add)
                    ins.then_inc(stepped, 1)
                dve.wait_ge(stepped, h * 7 + 7)
                dve.tensor_copy(c.small[:, 60:61], ch(St, 7)[:, 0:1]).then_inc(masked, 1)
                if more:
                    first_levels(h + 1)
                dve.wait_ge(std_ready, h * 2 + 2)
                rstd = Sm[1].rearrange("p (a n) -> p a n", n=HALF)
                dve.tensor_tensor(rstd, OUT, rstd, ALU.mult).then_inc(o_consumed, 1)
                dve.wait_ge(o_consumed, h + 2)
                dve.scalar_tensor_tensor(out=H[:, ds(h + 4, 1), :], in0=M[:, 1:2, :], scalar=c.vec("hgrn_gnorm"),
                                         in1=M[:, ds(h + 12, 1), :], op0=ALU.mult, op1=ALU.mult).then_inc(chain, 1)
                dve.wait_ge(chain, h + 1)

            first_levels(0)
            with dve.Fori(0, 3) as h:
                body(h, True)
            body(3, False)


def ffn_stage(c, name, up, down, chunks, conv=False, bias=None, gate=None, prefetch=()):
    KD = 1 if conv else 2
    M, X, PS = c.M, c.X, c.PS
    hid_hi = [c.hidR[:, 4 * b:4 * b + KD, :] for b in range(2)]
    hid_lo = [c.hidR[:, 4 * b + 2:4 * b + 2 + KD, :] for b in range(2)]
    down_parts = c.down1R if conv else c.downR
    w_down = [down_parts[:, x * KD:(x + 1) * KD, :] for x in range(2)]
    mixed = M[:, 8:10, :]
    PAD = 2
    raw = c.T[:, :, :].rearrange("p a b -> p (a b)")[:, 0:2 * (T + PAD)].rearrange("p (a b) -> p a b", b=T + PAD)
    at = lambda i, per, const: const if i is None else i * (2 * per) + const
    base = list(c.loads)
    with c.stage("up_done", "up_drained", "conv_done", "tap_done", "gelu_done", "hi_done", "sq_done", "hid_ready",
                 "down_done", "down_drained", "padded", "bias_ready", "up_step", "up_ready", "down_step",
                 "down_ready") as (
            block, up_done, up_drained, conv_done, tap_done, gelu_done, hi_done, sq_done, hid_ready, down_done,
            down_drained, padded, bias_ready, up_step, up_ready, down_step, down_ready):
        def schedule(eng, first, body):
            n = (chunks - 1) // 2
            first(None, 0)
            with eng.Fori(0, n) as i:
                for off in (0, 1):
                    body(i, off, True)
            for o in range(2 * n, chunks):
                body(None, o, o + 1 < chunks)

        @block.sync
        def _(sp):
            with sp.Fori(0, chunks - 1) as j:
                sp.wait_ge(up_ready, j * 2 + 2)
                c.load(sp, 0, up, j + 1)
                sp.wait_ge(down_ready, j + 1)
                c.load(sp, 1, down, j + 1)
            prefetch_after(c, sp, down_done, chunks * 16, prefetch)

        @block.gpsimd
        def _(pool):
            def split_up(ch, used):
                pool.wait_ge(c.landed[0], ch * 16 + base[0] + 16)
                for m in range(2):
                    if used:
                        pool.wait_ge(up_done, ch * 4 + 2 * m - 2)
                    src = c.W[:, 0, :].rearrange("p (k n) -> p k n", n=256)[:, :, m * P:(m + 1) * P]
                    hi, lo = [c.WR[:, 2 * m + x, :].rearrange("p (k n) -> p k n", n=P) for x in range(2)]
                    pool_round(c, pool, hi, src).then_inc(up_step, 1)
                    pool.wait_ge(up_step, ch * 2 + m + 1)
                    pool.tensor_tensor(lo, src, hi.bitcast(F32), ALU.subtract).then_inc(up_ready, 1)

            def split_down(ch, used):
                pool.wait_ge(c.landed[1], ch * 16 + base[1] + 16)
                if used:
                    pool.wait_ge(down_done, ch * 16)
                src = c.W[:, 1, 0:KD * D].rearrange("p (k n) -> p k n", k=KD)
                pool_round(c, pool, w_down[0], src).then_inc(down_step, 1)
                pool.wait_ge(down_step, ch + 1)
                pool.tensor_tensor(w_down[1], src, w_down[0].bitcast(F32), ALU.subtract).then_inc(down_ready, 1)

            split_up(0, False)
            split_down(0, False)
            split_up(1, True)
            with pool.Fori(2, chunks) as j:
                split_up(j, True)
                split_down(j - 1, True)
            split_down(chunks - 1, True)

        @block.tensor
        def _(pe):
            def up_part(i, o):
                for g in range(4):
                    m, n = g // 2, g % 2
                    if n == 0:
                        pe.wait_ge(up_ready, at(i, 2, 2 * o + m + 1))
                    pe.wait_ge(up_drained, at(i, 4, 4 * o + g + 1))
                    half_slab_pe(c, pe, g, m, n, c.MR, c.HR).then_inc(up_done, 1)

            def down_part(i, o):
                pe.wait_ge(down_ready, at(i, 1, o + 1))
                pe.wait_ge(hid_ready, at(i, KD, KD * (o + 1)))
                h_hi, h_lo = hid_hi[o % 2], hid_lo[o % 2]
                for g in range(16):
                    m, n = g // 2, g % 2
                    half, bank = slice(n * HALF, (n + 1) * HALF), PS[:, 4 + g % 4, :]
                    pe.wait_ge(down_drained, at(i, 16, 16 * o + g + 1 + 16))
                    for k in range(KD):
                        w_hi, w_lo = [w[:, k, m * P:(m + 1) * P] for w in w_down]
                        pe.matmul(bank, w_hi, h_hi[:, k, half], start=k == 0, stop=False)
                        pe.matmul(bank, w_lo, h_hi[:, k, half], start=False, stop=False)
                        mm = pe.matmul(bank, w_hi, h_lo[:, k, half], start=False, stop=k == KD - 1)
                    mm.then_inc(down_done, 1)

            def body(i, o, more):
                if more:
                    up_part(i, o + 1)
                down_part(i, o)

            schedule(pe, up_part, body)

        bias_cols = [c.small[:, 0:2], c.small[:, 2:4]]

        def stage_bias(act, i, o):
            col = param_columns()[0][bias][0] + 2 * o
            src = c.par[:, col:col + 2] if i is None else c.par[:, ds(i * 4 + col, 2)]
            act.copy(bias_cols[o % 2], src).then_inc(bias_ready, 1)

        @block.scalar
        def _(act):
            def up_part(i, o):
                if bias is not None:
                    act.wait_ge(bias_ready, at(i, 1, o + 1))
                for m in range(2):
                    if i is not None or o > 0:
                        used = conv_done if conv else hid_ready
                        act.wait_ge(used, at(i, 2, 2 * (o - 1) + m + 1))
                    for n in range(2):
                        act.wait_ge(up_done, at(i, 4, 4 * o + 2 * m + n + 1))
                        ps = PS[:, 2 * m + n, :]
                        if conv:
                            act.activation(raw[:, m, PAD + n * HALF:PAD + (n + 1) * HALF], ps,
                                           ACT.Copy).then_inc(up_drained, 1)
                        else:
                            b = 0.0 if bias is None else bias_cols[o % 2][:, m:m + 1]
                            act.activation(mixed[:, m, n * HALF:(n + 1) * HALF], ps, ACT.Relu,
                                           bias=b).then_inc(up_drained, 1)
                    if not conv:
                        act.wait_ge(up_drained, at(i, 4, 4 + 4 * o + 2 * m + 2))
                        act.activation(hid_hi[o % 2][:, m, :], mixed[:, m, :], ACT.Square).then_inc(hi_done, 1)
                if conv:
                    act.wait_ge(conv_done, at(i, 2, 2 * o + 1))
                    act.activation(mixed[:, 0, :], mixed[:, 0, :], ACT.Gelu_apprx_tanh).then_inc(gelu_done, 1)
                if bias is not None and (i is not None or o + 1 < chunks):
                    stage_bias(act, i, o + 1)

            act.sem_inc(up_drained, 4)
            if bias is not None:
                stage_bias(act, None, 0)
            schedule(act, up_part, lambda i, o, more: up_part(i, o + 1) if more else None)

        @block.vector
        def _(dve):
            def conv_tile(i, o, tile):
                at_w = param_columns()[0]["conv_w"][0] + tile * 22 + o
                at_b = param_columns()[0]["conv_b"][0] + tile * 22 + o
                col = lambda n: c.par[:, n:n + 1] if i is None else c.par[:, ds(i * 2 + n, 1)]
                out = mixed[:, tile, :]
                if i is not None or o > 0:
                    dve.wait_ge(hid_ready, at(i, 1, o))
                dve.wait_ge(up_drained, at(i, 4, 4 * o + 2 * tile + 2 + 4))
                dve.tensor_scalar(out, raw[:, tile, 2:2 + T], col(at_w + 88), col(at_b), ALU.mult,
                                  ALU.add).then_inc(tap_done, 1)
                dve.wait_ge(tap_done, at(i, 4, 4 * o + 2 * tile + 1))
                dve.scalar_tensor_tensor(out=out, in0=raw[:, tile, 1:1 + T], scalar=col(at_w + 44), in1=out,
                                         op0=ALU.mult, op1=ALU.add).then_inc(tap_done, 1)
                dve.wait_ge(tap_done, at(i, 4, 4 * o + 2 * tile + 2))
                dve.scalar_tensor_tensor(out=out, in0=raw[:, tile, 0:T], scalar=col(at_w), in1=out,
                                         op0=ALU.mult, op1=ALU.add).then_inc(conv_done, 1)

            def low_part(i, o, m, n):
                dve.wait_ge(sq_done, at(i, n, n * o + m + 1))
                dve.tensor_tensor(hid_lo[o % 2][:, m, :], mixed[:, m, :], hid_hi[o % 2][:, m, :].bitcast(F32),
                                  ALU.subtract).then_inc(hid_ready, 1)

            def square(i, o, m):
                dve.wait_ge(hi_done, at(i, 2, 2 * o + m + 1))
                dve.tensor_tensor(mixed[:, m, :], mixed[:, m, :], mixed[:, m, :], ALU.mult).then_inc(sq_done, 1)
                low_part(i, o, m, 2)

            def gated(i, o):
                a, v = mixed[:, 0, :], mixed[:, 1, :]
                dve.wait_ge(gelu_done, at(i, 1, o + 1))
                dve.wait_ge(conv_done, at(i, 2, 2 * o + 2))
                dve.tensor_tensor(hid_hi[o % 2][:, 0, :], a, v, ALU.mult).then_inc(hi_done, 1)
                dve.wait_ge(hi_done, at(i, 1, o + 1))
                dve.tensor_tensor(a, a, v, ALU.mult).then_inc(sq_done, 1)
                low_part(i, o, 0, 1)

            def drain(i, o):
                for g in range(16):
                    m, n = g // 2, g % 2
                    x, ps = X[:, m, n * HALF:(n + 1) * HALF], PS[:, 4 + g % 4, :]
                    dve.wait_ge(down_drained, at(i, 16, 16 * o + g + 1 + 4))
                    dve.wait_ge(down_done, at(i, 16, 16 * o + g + 1))
                    if gate is None:
                        dve.tensor_tensor(x, x, ps, ALU.add).then_inc(down_drained, 1)
                    else:
                        dve.scalar_tensor_tensor(out=x, in0=ps, scalar=gate(m), in1=x, op0=ALU.mult,
                                                 op1=ALU.add).then_inc(down_drained, 1)

            def early(i, o):
                conv_tile(i, o, 0) if conv else square(i, o, 0)

            def late(i, o):
                if conv:
                    conv_tile(i, o, 1)
                    gated(i, o)
                else:
                    square(i, o, 1)

            def first(i, o):
                early(i, o)
                late(i, o)

            def body(i, o, more):
                if more:
                    early(i, o + 1)
                drain(i, o)
                if more:
                    late(i, o + 1)

            dve.sem_inc(down_drained, 20)
            if conv:
                dve.memset(raw[:, :, 0:PAD], 0.0).then_inc(padded, 1)
                dve.wait_ge(padded, 1)
            schedule(dve, first, body)
    c.loads[0] += 16 * chunks
    c.loads[1] += 16 * chunks


def block2_project(c):
    M, H, PS, TAPS = c.M, c.H, c.PS, 31
    V = M[:, 16:20, :].rearrange("p a (b n) -> p (a b) n", n=HALF)
    U = c.T[:, 0:2, :].rearrange("p a b -> p (a b)")[:, 0:TAPS - 1 + T]
    z, l = c.T[0:8, 2, :], c.T[0:8, 3, :]
    with c.stage("products", "drained", "gated", "u_ready", "taps", "w_step", "w_ready", "pieces", "row_step", "padded", "mul") as (
            block, products, drained, gated, u_ready, taps, w_step, w_ready, pieces, row_step, padded, mul):
        @block.sync
        def _(sp):
            stream(c, sp, w_ready, "w_in_2", 11)

        @block.gpsimd
        def _(pool):
            split = Split(c, pool, products, w_step, w_ready, pieces)
            split.half(0, 1)
            split.halves(4, 2)
            split.whole(34)
            split.whole(42)

        @block.tensor
        def _(pe):
            pe.sem_inc(products, PRE)
            pe.wait_ge(w_ready, 2)
            for n in range(2):
                pe.wait_ge(drained, n + 1)
                half_slab_pe(c, pe, n, 1, n, c.XR, c.HR).then_inc(products, 1)
            project_pe(c, pe, products, drained, w_ready, 4, c.XR, c.HR, g0=2, h0=2)
            token_major_pe(c, pe, products, drained, w_ready, pieces, c.XR, c.HR, 34, 18)

        @block.scalar
        def _(act):
            act.sem_inc(drained, 8)

            def copies(first, last):
                with act.Fori(first, last) as i:
                    for j in range(8):
                        act.wait_ge(products, PRE + 2 + j + 1 + i * 8)
                        act.activation(M[:, ds(i * 4 + j // 2, 1), (j % 2) * HALF:(j % 2 + 1) * HALF],
                                       PS[:, (2 + j) % 8, :].unsqueeze(1), ACT.Copy).then_inc(drained, 1)

            for n in range(2):
                act.wait_ge(products, PRE + n + 1)
                act.activation(z[:, n * HALF:(n + 1) * HALF], PS[0:8, n, :], ACT.Identity,
                               bias=c.row_par[0:8, 0:1]).then_inc(drained, 1)
            act.wait_ge(drained, 10)
            act.activation(l, z, ACT.Abs).then_inc(row_step, 1)
            act.wait_ge(row_step, 1)
            act.activation(l, l, ACT.Exp, scale=-1.0).then_inc(row_step, 1)
            act.wait_ge(row_step, 2)
            act.activation(l, l, ACT.Ln, bias=1.0).then_inc(row_step, 1)
            copies(0, 2)
            act.wait_ge(drained, 26)
            for k in range(4):
                act.activation(M[:, 4 + k, :], M[:, 4 + k, :], ACT.Sigmoid).then_inc(gated, 1)
            copies(2, 4)
            evacuate_token_major(act, c, products, drained, V, 34)

        @block.vector
        def _(dve):
            at_w, at_b = param_columns()[0]["conv_dw_w_2"][0], param_columns()[0]["conv_dw_b_2"][0]
            dve.wait_ge(row_step, 3)
            dve.scalar_tensor_tensor(out=z, in0=z, scalar=0.0, in1=l, op0=ALU.min, op1=ALU.subtract).then_inc(row_step, 1)
            dve.wait_ge(row_step, 4)
            dve.tensor_tensor_scan(l, c.ones[0:8, 0:1].to_broadcast([8, T]), z, 0.0, ALU.mult,
                                   ALU.add).then_inc(row_step, 1)
            dve.wait_ge(row_step, 5)
            dve.tensor_scalar(c.rows[0:8, 0:T], l, -8.0, None, ALU.mult).then_inc(row_step, 1)
            dve.memset(U[:, 0:TAPS - 1], 0.0).then_inc(padded, 1)
            dve.wait_ge(padded, 1)
            dve.sem_inc(taps, 1)
            with dve.Fori(0, 4) as k:
                out = M[:, ds(k, 1), :]
                col = lambda n: c.par[:, ds(k + n, 1)]
                u = lambda j: U[:, j:j + T].unsqueeze(1)
                dve.wait_ge(gated, k + 1)
                dve.wait_ge(taps, k * TAPS + 1)
                dve.tensor_tensor(u(TAPS - 1), out, M[:, ds(k + 4, 1), :], ALU.mult).then_inc(u_ready, 1)
                dve.wait_ge(u_ready, k + 1)
                dve.tensor_scalar(out, u(0), col(at_w), col(at_b), ALU.mult, ALU.add).then_inc(taps, 1)
                for j in range(1, TAPS):
                    dve.wait_ge(taps, k * TAPS + j + 1)
                    dve.scalar_tensor_tensor(out=out, in0=u(j), scalar=col(at_w + 4 * j), in1=out, op0=ALU.mult,
                                             op1=ALU.add).then_inc(taps, 1)
    stream_done(c, 11)


def block2_pointwise(c, prefetch):
    M, H, PS = c.M, c.H, c.PS
    sq = c.T[:, :, :].rearrange("p a (b n) -> p (a b) n", n=HALF)
    out = lambda g: H[:, 4 + g // 2, (g % 2) * HALF:(g % 2 + 1) * HALF]
    with c.stage("products", "biased", "squared", "var_done", "logs", "rstd_ready", "done", "x_back") as (
            block, products, biased, squared, var_done, logs, rstd_ready, done, x_back):
        @block.sync
        def _(sp):
            sp.dma_start(c.X[:, :, :], c.spill).then_inc(x_back, 16)
            prefetch_after(c, sp, products, 8, prefetch)
            sp.wait_ge(x_back, 16)

        @block.tensor
        def _(pe):
            pe.wait_ge(c.landed[0], c.loads[0] + 16)
            for g in range(8):
                for k in range(4):
                    mm = pe.matmul(PS[:, g, :], c.W[:, 0, k * HALF + g // 2 * P:k * HALF + (g // 2 + 1) * P],
                                   M[:, k, (g % 2) * HALF:(g % 2 + 1) * HALF], start=k == 0, stop=k == 3)
                mm.then_inc(products, 1)
            for g in range(8):
                pe.wait_ge(squared, g + 1)
                pe.matmul(PS[:, g, :], c.group_ones[:, :], sq[:, g, :], start=True, stop=True).then_inc(var_done, 1)

        @block.scalar
        def _(act):
            for g in range(8):
                act.wait_ge(products, g + 1)
                act.activation(out(g), PS[:, g, :], ACT.Identity, bias=c.vec("b_conv_pw_2", g // 2)).then_inc(biased, 1)
                act.wait_ge(biased, g + 1)
                act.activation(sq[:, g, :], out(g), ACT.Square).then_inc(squared, 1)
            for g in range(8):
                act.wait_ge(var_done, g + 1)
                act.activation(sq[:, g, :], PS[:, g, :], ACT.Ln, bias=c.rms_eps[:, :]).then_inc(logs, 1)
            for g in range(8):
                act.wait_ge(logs, g + 1)
                act.activation(sq[:, g, :], sq[:, g, :], ACT.Exp, scale=-0.5).then_inc(rstd_ready, 1)

        @block.vector
        def _(dve):
            for g in range(8):
                dve.wait_ge(rstd_ready, g + 1)
                dve.scalar_tensor_tensor(out=out(g), in0=out(g), scalar=c.vec("conv_out_g_2", g // 2), in1=sq[:, g, :],
                                         op0=ALU.mult, op1=ALU.mult).then_inc(done, 1)
    c.loads[0] += 16


def block2_attention(c, prefetch):
    M, H, PS, S = c.M, c.H, c.PS, c.small
    V = M[:, 16:20, :].rearrange("p a (b n) -> p (a b) n", n=HALF)
    O = M[:, 0:4, :].rearrange("p a (b n) -> p (a b) n", n=HALF)
    Q, K = [c.T[:, 0, :], c.T[:, 2, :]], [c.T[:, 1, :], c.T[:, 3, :]]
    prob, turned = [M[:, 4, :], M[:, 5, :]], [M[:, 6, :], M[:, 7, :]]
    sc = [PS[:, 0:2, :].rearrange("p a b -> p (a b)"), PS[:, 2:4, :].rearrange("p a b -> p (a b)")]
    tp = PS[:, 4:6, :].rearrange("p a b -> p (a b)")
    with c.stage("row_landed_0", "row_landed_1", "ones_rows", "qk_ready", "scores_done", "diag_masked", "max_step",
                 "max_ready", "p_ready", "turned_done", "turned_ready", "pv_done", "o_step", "o_written", "rms",
                 "turned_o", "h_written") as (
            block, row_landed_0, row_landed_1, ones_rows, qk_ready, scores_done, diag_masked, max_step, max_ready,
            p_ready, turned_done, turned_ready, pv_done, o_step, o_written, rms, turned_o, h_written):
        row_landed = [row_landed_0, row_landed_1]

        @block.sync
        def _(sp):
            prefetch_after(c, sp, None, 0, prefetch)
            for h in range(8):
                if h >= 2:
                    sp.wait_ge(scores_done, 8 * (h - 1) + 1)
                sp.dma_start(K[h % 2][64:65, :], c.rows[h:h + 1, 0:T]).then_inc(row_landed[h % 2], 16)

        @block.gpsimd
        def _(pool):
            for e in range(2):
                pool.memset(Q[e][64:65, :], 1.0).then_inc(ones_rows, 1)
            with pool.Fori(0, 4) as p:
                for e in range(2):
                    pool.wait_ge(scores_done, p * 16 + 1)
                    half = slice(64 * e, 64 * e + 64)
                    pool.tensor_copy(Q[e][0:64, :].unsqueeze(1), M[half, ds(p + 8, 1), :]).then_inc(qk_ready, 1)
                    pool.tensor_copy(K[e][0:64, :].unsqueeze(1), M[half, ds(p + 12, 1), :]).then_inc(qk_ready, 1)

        @block.tensor
        def _(pe):
            pe.sem_inc(turned_done, 2)
            pe.sem_inc(pv_done, 2)
            pe.sem_inc(scores_done, 1)
            pe.wait_ge(ones_rows, 2)
            with pe.Fori(0, 4) as p:
                def scores(s):
                    e, i = s // 8, s % 8
                    if i == 0:
                        pe.wait_ge(qk_ready, p * 4 + 2 * e + 2)
                        pe.wait_ge(row_landed[e], p * 16 + 16)
                    pe.wait_ge(p_ready, p * 16 + s + 1)
                    for a in range(0, (i + 1) * P, HALF):
                        b = min((i + 1) * P, a + HALF)
                        mm = pe.matmul(sc[s % 2][:, a:b], Q[e][0:65, i * P:(i + 1) * P], K[e][0:65, a:b], start=True,
                                       stop=True)
                    mm.then_inc(scores_done, 1)

                def turn(s):
                    pe.wait_ge(p_ready, p * 16 + s + 3)
                    pe.wait_ge(turned_ready, p * 16 + s + 1)
                    for b in range(s % 8 + 1):
                        mm = pe.transpose(tp[:, b * P:(b + 1) * P], prob[s % 2][:, b * P:(b + 1) * P], c.ident[:, :])
                    mm.then_inc(turned_done, 1)

                def outputs(s):
                    pe.wait_ge(turned_ready, p * 16 + s + 2)
                    pe.wait_ge(o_written, p * 16 + s + 1)
                    n = s % 8 + 1
                    for b in range(n):
                        mm = pe.matmul(PS[:, 6 + s % 2, 0:P], turned[s % 2][:, b * P:(b + 1) * P],
                                       V[:, b, ds(p * P, P)], start=b == 0, stop=b == n - 1)
                    mm.then_inc(pv_done, 1)

                for s in range(19):
                    if s < 16:
                        scores(s)
                    if 2 <= s < 18:
                        turn(s - 2)
                    if s >= 3:
                        outputs(s - 3)
            pe.wait_ge(rms, 5)
            for g in range(8):
                m, n = g // 2, g % 2
                for b in range(4):
                    mm = pe.transpose(PS[:, g, b * P:(b + 1) * P], O[:, n * 4 + b, m * P:(m + 1) * P], c.ident[:, :])
                mm.then_inc(turned_o, 1)

        @block.scalar
        def _(act):
            act.sem_inc(p_ready, 2)
            act.sem_inc(turned_ready, 1)
            with act.Fori(0, 4) as p:
                def exps(s):
                    n = (s % 8 + 1) * P
                    act.wait_ge(max_ready, p * 16 + s + 1)
                    act.wait_ge(turned_done, p * 16 + s + 1)
                    act.activation(prob[s % 2][:, 0:n], sc[s % 2][:, 0:n], ACT.Exp, bias=S[:, 16 + s:17 + s], scale=0.125,
                                   accum_out=S[:, 32 + s:33 + s]).then_inc(p_ready, 1)

                def copies(s):
                    n = (s % 8 + 1) * P
                    act.wait_ge(turned_done, p * 16 + s + 3)
                    act.wait_ge(pv_done, p * 16 + s + 1)
                    act.activation(turned[s % 2][:, 0:n], tp[:, 0:n], ACT.Copy).then_inc(turned_ready, 1)

                for s in range(18):
                    if s < 16:
                        exps(s)
                    if s >= 2:
                        copies(s - 2)
            act.wait_ge(o_written, 66)
            act.activation(c.T[:, :, :], M[:, 0:4, :], ACT.Square).then_inc(rms, 1)
            act.wait_ge(rms, 2)
            act.activation(c.rows[:, 0:64], c.rows[:, 0:64], ACT.Ln, scale=1.0 / 64, bias=c.rms_eps[:, :]).then_inc(rms, 1)
            act.wait_ge(rms, 3)
            act.activation(c.rows[:, 0:64], c.rows[:, 0:64], ACT.Exp, scale=-0.5).then_inc(rms, 1)
            for g in range(8):
                act.wait_ge(turned_o, g + 1)
                act.activation(H[:, g // 2, (g % 2) * HALF:(g % 2 + 1) * HALF], PS[:, g, :], ACT.Identity,
                               scale=c.vec("attn_out_g_2", g // 2)).then_inc(h_written, 1)

        @block.vector
        def _(dve):
            dve.sem_inc(o_written, 2)
            with dve.Fori(0, 4) as p:
                def maxima(s):
                    i = s % 8
                    diag = sc[s % 2][:, i * P:(i + 1) * P]
                    dve.wait_ge(scores_done, p * 16 + s + 2)
                    dve.tensor_tensor(diag, diag, c.from_above, ALU.add).then_inc(diag_masked, 1)
                    dve.wait_ge(diag_masked, p * 16 + s + 1)
                    dve.reduce_max(S[:, s:s + 1], sc[s % 2][:, 0:(i + 1) * P], AX_X).then_inc(max_step, 1)
                    dve.wait_ge(max_step, p * 16 + s + 1)
                    dve.tensor_scalar(S[:, 16 + s:17 + s], S[:, s:s + 1], -0.125, None, ALU.mult).then_inc(max_ready, 1)

                def normalise(s):
                    dve.wait_ge(pv_done, p * 16 + s + 3)
                    dve.reciprocal(S[:, 48 + s % 8:49 + s % 8], S[:, 32 + s:33 + s]).then_inc(o_step, 1)
                    dve.wait_ge(o_step, p * 16 + s + 1)
                    dve.tensor_scalar(O[:, s % 8, ds(p * P + 64 * (s // 8), 64)], PS[:, 6 + s % 2, 64 * (s // 8):64 * (s // 8) + 64],
                                      S[:, 48 + s % 8:49 + s % 8], None, ALU.mult).then_inc(o_written, 1)

                for s in range(19):
                    if s < 16:
                        maxima(s)
                    if s >= 3:
                        normalise(s - 3)
            dve.wait_ge(rms, 1)
            dve.reduce_sum(c.rows[:, 0:64].unsqueeze(2), c.T[:, :, :].rearrange("p a (b n) -> p (a b) n", n=64),
                           AX_X).then_inc(rms, 1)
            dve.wait_ge(rms, 4)
            o = M[:, 0:4, :].rearrange("p a (b n) -> p (a b) n", n=64)
            dve.tensor_tensor(o, o, c.rows[:, 0:64].unsqueeze(2).to_broadcast([P, 64, 64]), ALU.mult).then_inc(rms, 1)


def block3_ada(c, prefetch):
    row = c.M[0:2, 0:6, :].rearrange("p a b -> p (a b)")
    cond = c.small[:, 0:16].rearrange("p (k s) -> p k s", s=2)
    SLABS = 24
    base = list(c.loads)
    with c.stage("cond_ready", "products", "row_written", "turned", "biased", "plus_one") as (block, cond_ready, products, row_written, turned, biased, plus_one):
        @block.sync
        def _(sp):
            sp.dma_start(c.T[:, 0:2, :].rearrange("p a b -> p (a b)"), c.inp["ctx"]).then_inc(c.ctx_landed, 16)
            with sp.Fori(1, SLABS // 4) as i:
                for slot in range(4):
                    sp.wait_ge(products, i * 4 + slot - 3)
                    c.load(sp, slot, "w_ada_3", i * 4 + slot)
            prefetch_after(c, sp, products, SLABS, prefetch)

        @block.scalar
        def _(act):
            for s, name in enumerate(("c_3", "c_ctx_3")):
                act.activation(cond[:, :, s:s + 1], c.vec(name, 0, 8).unsqueeze(2), ACT.Silu).then_inc(cond_ready, 1)
            with act.Fori(0, SLABS // 4) as i:
                for slot in range(4):
                    act.wait_ge(products, i * 4 + slot + 1)
                    act.activation(c.M[0:2, ds(i, 1), slot * 256:(slot + 1) * 256], c.PS[0:2, slot:slot + 1, 0:256],
                                   ACT.Copy).then_inc(row_written, 1)

        @block.tensor
        def _(pe):
            pe.wait_ge(cond_ready, 2)
            pe.sem_inc(row_written, 4)
            with pe.Fori(0, SLABS // 4) as i:
                for slot in range(4):
                    pe.wait_ge(c.landed[slot], base[slot] + 16 + i * 16)
                    pe.wait_ge(row_written, i * 4 + slot + 1)
                    for k in range(KT):
                        mm = pe.matmul(c.PS[0:2, slot, 0:256], cond[:, k, :], c.W[:, slot, k * 256:(k + 1) * 256],
                                       start=k == 0, stop=k == KT - 1)
                    mm.then_inc(products, 1)
            pe.wait_ge(row_written, 4 + SLABS)
            for q in range(12):
                if q >= 8:
                    pe.wait_ge(biased, q - 7)
                for a in range(4):
                    at = (q * 4 + a) * P
                    mm = pe.matmul(c.PS[:, (4 + q) % 8, a * P:(a + 1) * P], row[:, at:at + P], c.ident[0:2, :],
                                   start=a == 0, stop=a == 3, skip_group_check=True)
                mm.then_inc(turned, 1)

        @block.vector
        def _(dve):
            ada = c.ada[:, :].rearrange("p (j s) -> p j s", s=2)
            for q in range(12):
                dve.wait_ge(turned, q + 1)
                dve.tensor_tensor(ada[:, 4 * q:4 * q + 4, :],
                                  c.PS[:, (4 + q) % 8, :].rearrange("p (a n) -> p a n", n=P)[:, :, 0:2],
                                  c.vec("b_ada_3", 4 * q, 4).unsqueeze(2).to_broadcast([P, 4, 2]),
                                  ALU.add).then_inc(biased, 1)
            dve.wait_ge(biased, 12)
            for j in (8, 32):
                dve.tensor_scalar(ada[:, j:j + 8, :], ada[:, j:j + 8, :], 1.0, None, ALU.add).then_inc(plus_one, 1)
            dve.tensor_tensor(c.gate_bias[:, :].unsqueeze(2), ada[:, 40:48, 0:1], c.vec("b2_3", 0, 8).unsqueeze(2),
                              ALU.mult).then_inc(plus_one, 1)
    for slot in range(4):
        c.loads[slot] += 16 * (SLABS // 4)


def block3_context(c, prefetch):
    N = c.T[:, 0:2, :].rearrange("p a (b n) -> p (a b) n", n=CTX)
    raw = c.H[:, 1, 0:2 * CTX].rearrange("p (a n) -> p a n", n=CTX)
    k = c.T[:, 2, 0:2 * CTX].rearrange("p (a n) -> p a n", n=CTX)
    v = c.T[:, 3, :].rearrange("p (a n) -> p a n", n=HALF)
    PS = c.PS
    with c.stage("products", "drained", "taps") as (block, products, drained, taps):
        @block.sync
        def _(sp):
            prefetch_after(c, sp, products, 5, prefetch)

        @block.tensor
        def _(pe):
            pe.wait_ge(c.landed[1], c.loads[1] + 16)
            for kk in range(KT):
                mm = pe.matmul(PS[:, 0, 0:CTX], c.W[:, 1, kk * P:(kk + 1) * P], N[:, kk, :], start=kk == 0, stop=kk == 7)
            mm.then_inc(products, 1)
            pe.wait_ge(c.landed[0], c.loads[0] + 16)
            for m in range(2):
                for kk in range(KT):
                    mm = pe.matmul(PS[:, 1 + m, 0:CTX], c.W[:, 0, kk * 256 + m * P:kk * 256 + (m + 1) * P], N[:, kk, :],
                                   start=kk == 0, stop=kk == 7)
                mm.then_inc(products, 1)
            pe.wait_ge(c.landed[2], c.loads[2] + 16)
            w = c.W[:, 2:4, :].rearrange("p a (k n) -> p (a k) n", n=HALF)
            for t in range(2):
                for kk in range(KT):
                    mm = pe.matmul(PS[:, 3 + t, :], N[:, kk, t * P:(t + 1) * P], w[:, kk, :], start=kk == 0, stop=kk == 7)
                mm.then_inc(products, 1)

        @block.scalar
        def _(act):
            act.wait_ge(products, 1)
            act.activation(c.rows[:, T:TT], PS[:, 0, 0:CTX], ACT.Identity, bias=c.row_par[:, 1:2]).then_inc(drained, 1)
            for m in range(2):
                act.wait_ge(products, 2 + m)
                act.activation(raw[:, m, :], PS[:, 1 + m, 0:CTX], ACT.Copy).then_inc(drained, 1)
            for t in range(2):
                act.wait_ge(products, 4 + t)
                act.activation(v[:, t, :], PS[:, 3 + t, :], ACT.Copy).then_inc(drained, 1)
            act.wait_ge(taps, 6)
            act.activation(k, k, ACT.Silu).then_inc(drained, 1)

        @block.vector
        def _(dve):
            for m in range(2):
                dve.wait_ge(drained, 2 + m)
                conv3(c, dve, raw[:, m, :], k[:, m, :], 2 + m, CTX, taps, 3 * m)
    for slot in range(3):
        c.loads[slot] += 16


def conv3(c, dve, x, out, tile, n, taps, base):
    w = lambda j: c.vec("conv_qk_3", 4 * j + tile)
    dve.tensor_scalar(out, x, w(1), None, ALU.mult).then_inc(taps, 1)
    dve.wait_ge(taps, base + 1)
    dve.scalar_tensor_tensor(out=out[:, 1:n], in0=x[:, 0:n - 1], scalar=w(0), in1=out[:, 1:n], op0=ALU.mult,
                             op1=ALU.add).then_inc(taps, 1)
    dve.wait_ge(taps, base + 2)
    dve.scalar_tensor_tensor(out=out[:, 0:n - 1], in0=x[:, 1:n], scalar=w(2), in1=out[:, 0:n - 1], op0=ALU.mult,
                             op1=ALU.add).then_inc(taps, 1)


def block3_project(c):
    M, H, PS, S = c.M, c.H, c.PS, c.small
    v = M[:, 12:16, :].rearrange("p a (b n) -> p (a b) n", n=HALF)
    vals = M[:, 16:20, :].rearrange("p a (b n) -> p (a b) n", n=HALF)
    gain, bias = c.T[:, 0, 0:HALF], c.T[:, 0, HALF:]
    ws, bs = c.W[:, 1, 0:HALF], c.W[0:1, 1, HALF:2 * HALF]
    stats = S[:, 0:48].rearrange("p (a b) -> p a b", b=6)
    aggr = S[:, 48:64].rearrange("p (a b) -> p a b", b=2)
    rstd = c.gate_tmp
    with c.stage("products", "drained", "gain_landed", "spatial_landed", "stats_done", "aggr_done", "rstd_done",
                 "v_step", "taps", "silu_done", "scaled", "mixed", "gated", "w_step", "w_ready", "pieces") as (
            block, products, drained, gain_landed, spatial_landed, stats_done, aggr_done, rstd_done, v_step, taps,
            silu_done, scaled, mixed, gated, w_step, w_ready, pieces):
        @block.sync
        def _(sp):
            sp.dma_start(c.T[:, 0, :], c.inp["ln_v_rows"]).then_inc(gain_landed, 16)
            stream(c, sp, w_ready, "w_in_3", 11)
            sp.wait_ge(w_ready, 20)
            sp.dma_start(ws, c.inp["w_s_3"]).then_inc(spatial_landed, 16)
            sp.wait_ge(spatial_landed, 16)
            sp.dma_start(bs, c.inp["b_s_3"]).then_inc(spatial_landed, 16)

        @block.gpsimd
        def _(pool):
            split = Split(c, pool, products, w_step, w_ready, pieces)
            split.whole(0)
            split.whole(8)
            split.halves(3, 16)
            split.whole(40)
            split.whole(48)
            split.half(56, 0)

        @block.tensor
        def _(pe):
            pe.sem_inc(products, PRE)
            token_major_pe(c, pe, products, drained, w_ready, pieces, c.XR, c.HR, 0, 0)
            project_pe(c, pe, products, drained, w_ready, 3, c.XR, c.HR, g0=16, h0=4)
            token_major_pe(c, pe, products, drained, w_ready, pieces, c.XR, c.HR, 40, 16)
            pe.wait_ge(w_ready, 22)
            for n in range(2):
                pe.wait_ge(drained, 56 + n + 1)
                half_slab_pe(c, pe, n, 0, n, c.XR, c.HR).then_inc(products, 1)
            pe.wait_ge(spatial_landed, 32)
            pe.wait_ge(v_step, 24)
            for g in range(8):
                pe.wait_ge(drained, 58 + g + 1)
                for i in range(4):
                    t = (g % 2) * 4 + i
                    out = PS[:, (58 + g) % 8, i * P:(i + 1) * P]
                    pe.matmul(out, v[:, t, g // 2 * P:(g // 2 + 1) * P], ws[:, g // 2 * P:(g // 2 + 1) * P],
                              start=i == 0, stop=False, skip_group_check=True)
                    mm = pe.matmul(out, c.ones[0:1, :], bs[:, g // 2 * P:(g // 2 + 1) * P], start=False, stop=i == 3,
                                   skip_group_check=True)
                mm.then_inc(mixed, 1)

        @block.scalar
        def _(act):
            act.sem_inc(drained, 8)
            evacuate_token_major(act, c, products, drained, v, 0)
            act.wait_ge(aggr_done, 8)
            act.activation(rstd[:, 0:8].unsqueeze(2), aggr[:, :, 1:2], ACT.Ln, bias=c.ln_eps[:, :]).then_inc(rstd_done, 1)
            act.wait_ge(rstd_done, 1)
            act.activation(rstd[:, 0:8], rstd[:, 0:8], ACT.Exp, scale=-0.5).then_inc(rstd_done, 1)
            with act.Fori(0, 3) as i:
                for j in range(8):
                    act.wait_ge(products, PRE + 16 + j + 1 + i * 8)
                    act.activation(M[:, ds(i * 4 + j // 2, 1), (j % 2) * HALF:(j % 2 + 1) * HALF],
                                   PS[:, j:j + 1, :], ACT.Copy).then_inc(drained, 1)
            act.wait_ge(drained, 48)
            act.activation(M[:, 8:12, :], M[:, 8:12, :], ACT.Sigmoid).then_inc(gated, 1)
            for tile in range(4):
                act.wait_ge(taps, 3 * tile + 3)
                act.activation(M[:, 4 + tile, :], c.T[:, 1, :], ACT.Silu).then_inc(silu_done, 1)
            evacuate_token_major(act, c, products, drained, vals, 40)
            for n in range(2):
                act.wait_ge(products, PRE + 56 + n + 1)
                act.activation(c.rows[:, n * HALF:(n + 1) * HALF], PS[:, n, :], ACT.Identity,
                               bias=c.row_par[:, 1:2]).then_inc(drained, 1)

        @block.vector
        def _(dve):
            for t in range(8):
                dve.wait_ge(drained, 8 + 8 + t + 1)
                dve.bn_stats(stats[:, t, :], v[:, t, :]).then_inc(stats_done, 1)
            for t in range(8):
                dve.wait_ge(stats_done, t + 1)
                dve.bn_aggr(aggr[:, t, :], stats[:, t:t + 1, :]).then_inc(aggr_done, 1)
            dve.wait_ge(gain_landed, 16)
            dve.wait_ge(rstd_done, 2)
            for t in range(8):
                dve.tensor_scalar(v[:, t, :], v[:, t, :], aggr[:, t, 0:1], rstd[:, t:t + 1], ALU.subtract,
                                  ALU.mult).then_inc(v_step, 1)
                dve.wait_ge(v_step, 3 * t + 1)
                dve.tensor_tensor(v[:, t, :], v[:, t, :], gain, ALU.mult).then_inc(v_step, 1)
                dve.wait_ge(v_step, 3 * t + 2)
                dve.tensor_tensor(v[:, t, :], v[:, t, :], bias, ALU.add).then_inc(v_step, 1)
            dve.wait_ge(drained, 8 + 16 + 16)
            for tile in range(4):
                if tile >= 1:
                    dve.wait_ge(silu_done, tile)
                conv3(c, dve, M[:, 4 + tile, :], c.T[:, 1, :], tile, T, taps, 3 * tile)
            dve.wait_ge(silu_done, 2)
            dve.tensor_scalar(M[:, 4:6, :], M[:, 4:6, :], 0.125, None, ALU.mult).then_inc(scaled, 1)
            dve.wait_ge(products, PRE + 58)
            for g in range(8):
                dve.wait_ge(mixed, g + 1)
                half = slice((g % 2) * HALF, (g % 2 + 1) * HALF)
                dve.tensor_tensor(H[:, g // 2, half], PS[:, (58 + g) % 8, :], M[:, g // 2, half], ALU.mult).then_inc(scaled, 1)
    stream_done(c, 11)


ROWS = 36
CHUNKS = TT // CH
ORDER = ([8, 9] + list(range(8)), [9, 8] + list(range(7, -1, -1)))


def row_regions(c):
    w = c.W[:, 2:4, :].rearrange("p a b -> p (a b)")
    h = c.H[:, 4:8, :].rearrange("p a b -> p (a b)")
    t = c.T[:, 0:2, :].rearrange("p a b -> p (a b)")
    cut = lambda a, n: a[0:ROWS, n * TT:(n + 1) * TT]
    return {
        "l": cut(w, 0), "neg": cut(w, 1), "b": cut(w, 2), "m": cut(h, 0), "g": cut(h, 1), "reset": cut(h, 2),
        "neg_m": cut(t, 0),
        "cols": t[:, TT:TT + 320].rearrange("p (c q r) -> p c q r", q=4, r=8),
        "carry": t[:, TT + 320:TT + 360].rearrange("p (j c) -> p j c", c=CHUNKS),
        "small": t[0:ROWS, TT + 400:TT + 400 + 64],
        "sel": c.M[0:ROWS, 12, :].rearrange("p (j n) -> p j n", n=P),
        "kt": c.M[:, 13:15, :].rearrange("p a (c n) -> p (a c) n", n=256),
        "kt_ctx": c.M[:, 15, 0:512].rearrange("p (c n) -> p c n", n=256),
        "sel2": c.M[0:ROWS, 15, 512:1024].rearrange("p (j n) -> p j n", n=P),
    }


def block3_gates(c, prefetch):
    r = row_regions(c)
    rows, PS = c.rows, c.PS
    m0, neg_last, carry = r["small"][:, 0:10], r["small"][:, 16:26], r["small"][:, 32:42]
    kc = c.T[:, 2, 0:2 * CTX].rearrange("p (a n) -> p a n", n=CTX)
    with c.stage("sel_landed", "sel2_landed", "zeroed", "f_read", "i_moved", "l_step", "lf", "b_ready", "g_ready",
                 "m_step", "last_ready", "thr", "exps", "cols_done", "cols_copied", "turned", "kt_copied", "carried",
                 "bc_done", "x_back") as (
            block, sel_landed, sel2_landed, zeroed, f_read, i_moved, l_step, lf, b_ready, g_ready, m_step, last_ready,
            thr, exps, cols_done, cols_copied, turned, kt_copied, carried, bc_done, x_back):
        @block.sync
        def _(sp):
            sp.dma_start(r["sel"], c.inp["sel"].rearrange("p (j n) -> p j n", n=P)).then_inc(sel_landed, 16)
            sp.dma_start(r["sel2"], c.inp["sel2"].rearrange("p (j n) -> p j n", n=P)).then_inc(sel2_landed, 16)
            sp.dma_start(c.X[:, :, :], c.spill).then_inc(x_back, 16)
            prefetch_after(c, sp, None, 0, prefetch)
            sp.wait_ge(x_back, 16)
            sp.wait_ge(sel_landed, 16)

        @block.gpsimd
        def _(pool):
            pool.memset(r["reset"], 1.0).then_inc(zeroed, 1)
            pool.memset(r["l"], 0.0).then_inc(zeroed, 1)
            pool.memset(r["neg"], 0.0).then_inc(zeroed, 1)
            pool.memset(r["b"], 0.0).then_inc(zeroed, 1)
            pool.memset(r["m"], 0.0).then_inc(zeroed, 1)
            pool.memset(r["small"], 0.0).then_inc(zeroed, 1)
            pool.wait_ge(zeroed, 6)
            chunked = r["reset"].rearrange("p (c n) -> p c n", n=CH)
            pool.memset(chunked[0:4, :, 0:1], 0.0).then_inc(zeroed, 1)
            pool.memset(chunked[32:36, :, CH - 1:CH], 0.0).then_inc(zeroed, 1)

        @block.scalar
        def _(act):
            act.wait_ge(zeroed, 8)
            for d, at in ((0, 32), (1, 96)):
                act.activation(r["l"][32 * d:32 * d + 4, :], rows[at:at + 4, :], ACT.Abs).then_inc(f_read, 1)
                act.activation(r["neg"][32 * d:32 * d + 4, :], rows[at:at + 4, :], ACT.Relu, scale=-1.0).then_inc(f_read, 1)
            act.wait_ge(f_read, 4)
            act.activation(rows[32:36, :], rows[64:68, :], ACT.Copy).then_inc(i_moved, 1)
            act.activation(r["l"], r["l"], ACT.Exp, scale=-1.0).then_inc(l_step, 1)
            act.wait_ge(l_step, 1)
            act.activation(r["l"], r["l"], ACT.Ln, bias=1.0).then_inc(l_step, 1)
            act.wait_ge(thr, 1)
            act.activation(r["l"], r["l"], ACT.Exp, scale=-1.0).then_inc(exps, 1)
            act.wait_ge(last_ready, 3)
            for ch in range(CHUNKS):
                at = slice(ch * CH, (ch + 1) * CH)
                act.activation(r["neg"][:, at], r["m"][:, at], ACT.Exp, scale=-1.0, bias=m0[:, ch:ch + 1]).then_inc(exps, 1)
                act.activation(r["reset"][:, at], r["g"][:, at], ACT.Exp, bias=neg_last[:, ch:ch + 1]).then_inc(exps, 1)
            act.activation(carry, carry, ACT.Exp).then_inc(exps, 1)

        @block.vector
        def _(dve):
            dve.wait_ge(l_step, 2)
            dve.scalar_tensor_tensor(out=r["l"], in0=r["l"], scalar=-1.0, in1=r["neg"], op0=ALU.mult,
                                     op1=ALU.subtract).then_inc(lf, 1)
            dve.wait_ge(lf, 1)
            dve.wait_ge(zeroed, 8)
            dve.tensor_tensor_scan(r["b"][0:4, :], r["reset"][0:4, :], r["l"][0:4, :], 0.0, ALU.mult,
                                   ALU.add).then_inc(b_ready, 1)
            dve.tensor_tensor_scan(r["b"][32:36, ::-1], r["reset"][32:36, ::-1], r["l"][32:36, ::-1], 0.0, ALU.mult,
                                   ALU.add).then_inc(b_ready, 1)
            dve.wait_ge(b_ready, 2)
            dve.wait_ge(i_moved, 1)
            dve.tensor_tensor(r["g"], rows[0:ROWS, :], r["b"], ALU.subtract).then_inc(g_ready, 1)
            dve.wait_ge(g_ready, 1)
            n = 0
            for step in range(CHUNKS):
                for d in range(2):
                    ch, q = ORDER[d][step], slice(32 * d, 32 * d + 4)
                    at = slice(ch * CH, (ch + 1) * CH)
                    g, m = r["g"][q, at], r["m"][q, at]
                    if d:
                        g, m = g[:, ::-1], m[:, ::-1]
                    dve.tensor_tensor_scan(m, g, g, m0[q, ch:ch + 1], ALU.max, ALU.max).then_inc(m_step, 1)
                n += 2
                dve.wait_ge(m_step, n)
                if step + 1 < CHUNKS:
                    for d in range(2):
                        ch, q = ORDER[d][step], slice(32 * d, 32 * d + 4)
                        last, nxt = ch * CH + (0 if d else CH - 1), ORDER[d][step + 1]
                        dve.tensor_tensor(m0[q, nxt:nxt + 1], r["b"][q, last:last + 1], r["m"][q, last:last + 1],
                                          ALU.add).then_inc(m_step, 1)
                    n += 2
                    dve.wait_ge(m_step, n)
            dve.tensor_tensor(r["l"], r["b"], r["m"], ALU.add).then_inc(thr, 1)
            chunked = r["m"].rearrange("p (c n) -> p c n", n=CH)
            dve.tensor_scalar(neg_last[0:4, :].unsqueeze(2), chunked[0:4, :, CH - 1:CH], -1.0, None,
                              ALU.mult).then_inc(last_ready, 1)
            dve.tensor_scalar(neg_last[32:36, :].unsqueeze(2), chunked[32:36, :, 0:1], -1.0, None,
                              ALU.mult).then_inc(last_ready, 1)
            dve.wait_ge(last_ready, 2)
            dve.tensor_tensor(carry, m0, neg_last, ALU.add).then_inc(last_ready, 1)
            dve.tensor_scalar(r["neg_m"], r["m"], -1.0, None, ALU.mult).then_inc(thr, 1)
            for b in range(5):
                dve.wait_ge(turned, b + 1)
                out = r["kt"][:, 2 * b:2 * b + 2, :] if b < 4 else r["kt_ctx"]
                dve.tensor_copy(out, PS[:, 4 if b == 4 else b, :].rearrange("p (c n) -> p c n", n=256)).then_inc(kt_copied, 1)
            for b in range(4):
                dve.wait_ge(cols_done, b + 1)
                nc_ = min(3, CHUNKS - 3 * b)
                ps = PS[:, b, 0:nc_ * 4 * ROWS].rearrange("p (c q r) -> p c q r", q=4, r=ROWS)
                for q in range(4):
                    out = r["cols"][:, 3 * b:3 * b + nc_, q, :]
                    dve.tensor_copy(out[:, :, 0:4], ps[:, :, q, 0:4]).then_inc(cols_copied, 1)
                    dve.tensor_copy(out[:, :, 4:8], ps[:, :, q, 32:36]).then_inc(cols_copied, 1)
            dve.wait_ge(bc_done, 1)
            dve.tensor_copy(r["carry"], PS[:, 5, 0:40].rearrange("p (j c) -> p j c", c=CHUNKS)).then_inc(carried, 1)

        @block.tensor
        def _(pe):
            for b in range(5):
                for i in range(2):
                    for tile in range(2):
                        src = c.M[:, 6 + tile, (2 * b + i) * P:(2 * b + i + 1) * P] if b < 4 else \
                            kc[:, tile, i * P:(i + 1) * P]
                        mm = pe.transpose(PS[:, b, i * 256 + tile * P:i * 256 + (tile + 1) * P], src, c.ident[:, :])
                mm.then_inc(turned, 1)
            pe.wait_ge(kt_copied, 5)
            pe.wait_ge(exps, 22)
            for b in range(4):
                for i in range(min(3, CHUNKS - 3 * b)):
                    at = slice((3 * b + i) * CH, (3 * b + i + 1) * CH)
                    for q, name in enumerate(("g", "l", "neg", "reset")):
                        j = (i * 4 + q) * ROWS
                        mm = pe.transpose(PS[:, b, j:j + ROWS], r[name][:, at], c.ident[0:ROWS, 0:ROWS])
                mm.then_inc(cols_done, 1)
            pe.wait_ge(sel2_landed, 16)
            for j in range(4):
                mm = pe.matmul(PS[:, 5, j * CHUNKS:(j + 1) * CHUNKS], r["sel2"][:, j, :], carry, start=j == 0, stop=j == 3,
                               skip_group_check=True)
            mm.then_inc(bc_done, 1)


def block3_mlstm(c, prefetch):
    r = row_regions(c)
    M, PS = c.M, c.PS
    vals = M[:, 16:20, :].rearrange("p a (b n) -> p (a b) n", n=HALF)
    vals_ctx = c.T[:, 3, :].rearrange("p (a n) -> p a n", n=HALF)
    out_h = M[:, 0:4, :].rearrange("p a (b n) -> p (a b) n", n=HALF)
    H = c.H[:, 4:8, :].rearrange("p a b -> p (a b)")
    qs = [H[:, d * 256:(d + 1) * 256].rearrange("p (a n) -> p a n", n=P) for d in range(2)]
    ks = [H[:, 512 + d * 256:512 + (d + 1) * 256].rearrange("p (a n) -> p a n", n=P) for d in range(2)]
    kw = [H[:, 1024 + d * 256:1024 + (d + 1) * 256] for d in range(2)]
    state = [H[:, 1536 + d * 258:1536 + (d + 1) * 258].rearrange("p (a n) -> p a n", n=129) for d in range(2)]
    small = [H[:, 2052 + d * 16:2052 + (d + 1) * 16] for d in range(2)]
    wt = [H[:, 2560 + d * 512:2560 + (d + 1) * 512].rearrange("p (h n) -> p h n", n=P) for d in range(2)]
    W = c.W[:, 2:4, :].rearrange("p a b -> p (a b)")
    num = [W[:, d * 512:(d + 1) * 512].rearrange("p (h n) -> p h n", n=P) for d in range(2)]
    vs = [W[:, 1024 + d * 516:1024 + (d + 1) * 516].rearrange("p (h n) -> p h n", n=129) for d in range(2)]
    GB, ST = PS[:, 1, :], PS[:, 5, :]
    intra = PS[:, 2:7:4, 0:258].rearrange("p j (e n) -> p j e n", n=129)
    heads = lambda a: a.rearrange("p (h n) -> p h n", n=P)
    inter = PS[:, 3:5, 0:258].rearrange("p e (j n) -> p j e n", n=129)
    scores = PS[:, 0:8:7, 0:256].rearrange("p e (j n) -> p j e n", n=P)
    neg = [c.from_below, c.from_above]
    with c.stage("staged", "kw_ready", "added", "stepped", "sc_done", "gb_done", "arg_ready", "w_ready", "weighted",
                 "intra_done", "inter_done", "den", "num_step", "h_added", "zeroed") as (
            block, staged, kw_ready, added, stepped, sc_done, gb_done, arg_ready, w_ready, weighted, intra_done,
            inter_done, den, num_step, h_added, zeroed):
        def chunk(i, d):
            return i if d == 0 else i * -1 + 7

        @block.sync
        def _(sp):
            prefetch_after(c, sp, None, 0, prefetch)

        @block.gpsimd
        def _(pool):
            for d in range(2):
                pool.memset(state[d], 0.0).then_inc(zeroed, 1)
                pool.memset(vs[d][:, :, P:P + 1], 1.0).then_inc(zeroed, 1)
            pool.memset(out_h, 0.0).then_inc(zeroed, 1)
            with pool.Fori(0, 8) as i:
                for d in range(2):
                    pool.wait_ge(intra_done, i * 2 + d + 1)
                    at = ds((i * P if d == 0 else i * -P + 7 * P), P)
                    pool.tensor_copy(qs[d], M[:, 4:6, at]).then_inc(staged, 1)
                    pool.tensor_copy(ks[d], M[:, 6:8, at]).then_inc(staged, 1)
                    pool.tensor_copy(vs[d][:, :, 0:P].unsqueeze(1),
                                     vals[:, ds(chunk(i, d), 1), :].rearrange("p a (h n) -> p a h n", n=P)).then_inc(staged, 1)

        def update_pe(pe, d, n, v):
            pe.wait_ge(kw_ready, n + 1)
            if type(n) is not int or n > 0:
                pe.wait_ge(stepped, n)
            for h in range(4):
                p0 = 64 * (h % 2)
                out = ST[p0:p0 + 64, (h // 2) * 129:(h // 2) * 129 + 129]
                if v is vs[d]:
                    mm = pe.matmul(out, kw[d][:, h * 64:(h + 1) * 64], v[:, h, :], start=h < 2, stop=h >= 2,
                                   skip_group_check=True)
                    continue
                pe.matmul(out[:, 0:P], kw[d][:, h * 64:(h + 1) * 64], v[:, h * P:(h + 1) * P], start=h < 2,
                          stop=False, skip_group_check=True)
                mm = pe.matmul(out[:, P:P + 1], kw[d][:, h * 64:(h + 1) * 64], c.ones[:, 0:1], start=False,
                               stop=h >= 2, skip_group_check=True)
            mm.then_inc(added, 1)

        def update_dve(dve, d, n, ch):
            dve.wait_ge(added, n + 1)
            for j in range(2):
                col = r["carry"][:, 2 * d + j, ch]
                ins = dve.scalar_tensor_tensor(out=state[d][:, j, :], in0=state[d][:, j, :], scalar=col,
                                               in1=ST[:, j * 129:(j + 1) * 129], op0=ALU.mult, op1=ALU.add)
            ins.then_inc(stepped, 1)

        @block.tensor
        def _(pe):
            pe.sem_inc(intra_done, 2)
            for n in range(4):
                d, ch = n % 2, ORDER[n % 2][n // 2] - 8
                update_pe(pe, d, n, vals_ctx[:, ch, :])
            with pe.Fori(0, 8) as i:
                for d in range(2):
                    n = lambda per, k: i * (2 * per) + d * per + k
                    pe.wait_ge(staged, n(3, 3))
                    pe.wait_ge(weighted, n(1, 1))
                    for h in range(4):
                        p0 = 64 * (h % 2)
                        mm = pe.matmul(scores[:, h // 2, h % 2, :], ks[d][p0:p0 + 64, h // 2, :],
                                       qs[d][p0:p0 + 64, h // 2, :], start=h < 2, stop=h >= 2, skip_group_check=True)
                    mm.then_inc(sc_done, 1)
                    pe.wait_ge(arg_ready, n(1, 1))
                    at = ds((i * P if d == 0 else i * -P + 7 * P), P)
                    for h in range(4):
                        mm = pe.matmul(heads(GB)[:, h, :], r["sel"][:, 4 * d + h, :], r["neg_m"][:, at], start=h == 0,
                                       stop=h == 3, skip_group_check=True)
                    mm.then_inc(gb_done, 1)
                    pe.wait_ge(stepped, n(1, 3))
                    pe.wait_ge(num_step, n(2, 1))
                    for h in range(4):
                        p0 = 64 * (h % 2)
                        mm = pe.matmul(inter[:, h // 2, h % 2, :], qs[d][p0:p0 + 64, h // 2, :],
                                       state[d][p0:p0 + 64, h // 2, :], start=h < 2, stop=h >= 2,
                                       skip_group_check=True)
                    mm.then_inc(inter_done, 1)
                    update_pe(pe, d, n(1, 4), vs[d])
                    pe.wait_ge(weighted, n(1, 2))
                    for h in range(4):
                        mm = pe.matmul(intra[:, h // 2, h % 2, :], wt[d][:, h, :], vs[d][:, h, :], start=h % 2 == 0,
                                       stop=h % 2 == 1, skip_group_check=True)
                    mm.then_inc(intra_done, 1)

        @block.scalar
        def _(act):
            with act.Fori(0, 8) as i:
                for d in range(2):
                    act.wait_ge(arg_ready, i * 2 + d + 2)
                    act.activation(wt[d], wt[d], ACT.Exp).then_inc(w_ready, 1)

        @block.vector
        def _(dve):
            def keys(d, n, kt, ch):
                dve.tensor_tensor(kw[d].rearrange("p (h n) -> p h n", n=64), kt,
                                  ch_cols(ch, 3, d).to_broadcast([P, 4, 64]), ALU.mult).then_inc(kw_ready, 1)

            def ch_cols(ch, q, d):
                if type(ch) is int:
                    return r["cols"][:, ch, q, 4 * d:4 * d + 4].unsqueeze(2)
                return r["cols"][:, ds(ch, 1), q, 4 * d:4 * d + 4].rearrange("p a h -> p h a")

            dve.wait_ge(zeroed, 5)
            for credit in (weighted, arg_ready, num_step):
                dve.sem_inc(credit, 1)
            for n in range(4):
                d, ch = n % 2, ORDER[n % 2][n // 2]
                if n >= 2:
                    dve.wait_ge(stepped, n - 1)
                keys(d, n, r["kt_ctx"][:, ch - 8, :].rearrange("p (h n) -> p h n", n=64), ch)
                update_dve(dve, d, n, slice(ch, ch + 1))
            with dve.Fori(0, 8) as i:
                for d in range(2):
                    n = lambda per, k: i * (2 * per) + d * per + k
                    ch = chunk(i, d)
                    gcol = lambda q: ch_cols(ch, q, d)
                    dve.wait_ge(added, n(1, 3))
                    keys(d, None, r["kt"][:, ds(ch, 1), :].rearrange("p a (h n) -> p (a h) n", n=64), ch)
                    dve.wait_ge(gb_done, n(1, 1))
                    for h in range(4):
                        ins = dve.scalar_tensor_tensor(out=wt[d][:, h, :], in0=heads(GB)[:, h, :],
                                                       scalar=r["cols"][:, ds(ch, 1), 0, 4 * d + h],
                                                       in1=neg[d], op0=ALU.add, op1=ALU.add)
                    ins.then_inc(arg_ready, 1)
                    dve.wait_ge(inter_done, n(1, 1))
                    update_dve(dve, d, n(1, 4), ds(ch, 1))
                    dve.wait_ge(w_ready, n(1, 1))
                    dve.wait_ge(sc_done, n(1, 1))
                    w4 = wt[d].rearrange("p (j e) n -> p j e n", e=2)
                    dve.tensor_tensor(w4, scores, w4, ALU.mult).then_inc(weighted, 1)
                    dve.tensor_tensor(num[d].rearrange("p (a h) n -> p a h n", a=2), inter[:, :, :, 0:P],
                                      gcol(2).rearrange("p (a h) n -> p a h n", a=2).to_broadcast([P, 2, 2, P]),
                                      ALU.mult).then_inc(num_step, 1)
                    dt = small[d][:, 0:4].unsqueeze(2)
                    dve.tensor_tensor(dt.rearrange("p (a h) n -> p a h n", a=2), inter[:, :, :, P:P + 1],
                                      gcol(2).rearrange("p (a h) n -> p a h n", a=2), ALU.mult).then_inc(den, 1)
                    dve.wait_ge(intra_done, n(1, 3))
                    dve.wait_ge(den, n(5, 1))
                    dve.tensor_tensor(small[d][:, 4:8].rearrange("p (a h) -> p a h", a=2).unsqueeze(3),
                                      small[d][:, 0:4].rearrange("p (a h) -> p a h", a=2).unsqueeze(3),
                                      intra[:, :, :, P:P + 1], ALU.add).then_inc(den, 1)
                    dve.wait_ge(den, n(5, 2))
                    dve.scalar_tensor_tensor(out=small[d][:, 8:12], in0=small[d][:, 4:8], scalar=-1.0,
                                             in1=small[d][:, 4:8], op0=ALU.mult, op1=ALU.max).then_inc(den, 1)
                    dve.wait_ge(den, n(5, 3))
                    dve.tensor_tensor(small[d][:, 8:12].unsqueeze(2), small[d][:, 8:12].unsqueeze(2), gcol(1),
                                      ALU.max).then_inc(den, 1)
                    dve.wait_ge(den, n(5, 4))
                    dve.reciprocal(small[d][:, 12:16], small[d][:, 8:12]).then_inc(den, 1)
                    dve.wait_ge(num_step, n(2, 2))
                    num4 = num[d].rearrange("p (a h) n -> p a h n", a=2)
                    dve.tensor_tensor(num4, num4, intra[:, :, :, 0:P], ALU.add).then_inc(num_step, 1)
                    dve.wait_ge(num_step, n(2, 3))
                    dve.wait_ge(den, n(5, 5))
                    dve.tensor_tensor(num[d], num[d], small[d][:, 12:16].unsqueeze(2).to_broadcast([P, 4, P]),
                                      ALU.mult).then_inc(h_added, 1)
                    dve.wait_ge(h_added, n(2, 1))
                    o = out_h[:, ds(ch, 1), :]
                    dve.tensor_tensor(o, o, num[d].rearrange("p h n -> p (h n)").unsqueeze(1),
                                      ALU.add).then_inc(h_added, 1)


def block3_head_norm(c, prefetch):
    M, H, PS, S = c.M, c.H, c.PS, c.small
    h = M[:, 0:4, :].rearrange("p a (g n) -> p (a g) n", n=P)
    tm = M[:, 0:4, :].rearrange("p a (b n) -> p (a b) n", n=HALF)
    mean, var = S[:, 0:32], S[:, 32:64]
    bc = lambda a: a.unsqueeze(2).to_broadcast([P, 32, P])
    with c.stage("step", "x_scaled", "turned", "written") as (block, step, x_scaled, turned, written):
        @block.sync
        def _(sp):
            prefetch_after(c, sp, None, 0, prefetch)

        @block.vector
        def _(dve):
            dve.reduce_sum(mean.unsqueeze(2), h, AX_X).then_inc(step, 1)
            dve.wait_ge(step, 1)
            dve.tensor_scalar(mean, mean, 1.0 / P, None, ALU.mult).then_inc(step, 1)
            dve.wait_ge(step, 2)
            dve.tensor_tensor(h, h, bc(mean), ALU.subtract).then_inc(step, 1)
            dve.wait_ge(step, 4)
            dve.reduce_sum(var.unsqueeze(2), c.T[:, :, :].rearrange("p a (g n) -> p (a g) n", n=P), AX_X).then_inc(step, 1)
            dve.wait_ge(step, 7)
            dve.tensor_tensor(h, h, bc(var), ALU.mult).then_inc(step, 1)
            for g in range(8):
                dve.wait_ge(turned, g + 1)
                half = slice((g % 2) * HALF, (g % 2 + 1) * HALF)
                dve.scalar_tensor_tensor(out=H[:, 4 + g // 2, half], in0=PS[:, g, :], scalar=c.vec("hn_g_3", g // 2),
                                         in1=M[:, 8 + g // 2, half], op0=ALU.mult, op1=ALU.mult).then_inc(written, 1)

        @block.scalar
        def _(act):
            act.wait_ge(step, 3)
            act.activation(c.T[:, :, :], M[:, 0:4, :], ACT.Square).then_inc(step, 1)
            act.activation(c.X[:, :, :], c.X[:, :, :], ACT.Copy, scale=ALPHA).then_inc(x_scaled, 1)
            act.wait_ge(step, 5)
            act.activation(var, var, ACT.Ln, scale=1.0 / P, bias=c.ln_eps[:, :]).then_inc(step, 1)
            act.wait_ge(step, 6)
            act.activation(var, var, ACT.Exp, scale=-0.5).then_inc(step, 1)

        @block.tensor
        def _(pe):
            pe.wait_ge(step, 8)
            for g in range(8):
                for b in range(4):
                    mm = pe.transpose(PS[:, g, b * P:(b + 1) * P], tm[:, (g % 2) * 4 + b, g // 2 * P:(g // 2 + 1) * P],
                                      c.ident[:, :])
                mm.then_inc(turned, 1)


def build(nc, inputs, out, blocks=(1, 2, 3), upto=99):
    with ExitStack() as ctx:
        c = Core(nc, ctx, inputs, out)
        c.rms_eps = ctx.enter_context(nc.sbuf_tensor("rms_eps", [P, 1], F32))
        c.ln_eps = ctx.enter_context(nc.sbuf_tensor("ln_eps", [P, 1], F32))
        c.x_landed = ctx.enter_context(nc.semaphore("x_landed"))
        c.ctx_landed = ctx.enter_context(nc.semaphore("ctx_landed"))
        c.par_landed = ctx.enter_context(nc.semaphore("params_landed"))
        stored = [ctx.enter_context(nc.semaphore(f"stored_{i}")) for i in range(3)]
        with c.stage("memsets", "tables") as (block, memsets, tables):
            @block.sync
            def _(sp):
                if blocks[0] == 1:
                    c.load(sp, 0, "w_in", 0)
                sp.dma_start(c.X[:, :, :], inputs["x"]).then_inc(c.x_landed, 16)
                if blocks[0] == 1:
                    c.load(sp, 1, "w_in", 1)
                sp.dma_start(c.par[:, :], inputs["params"]).then_inc(c.par_landed, 16)
                if blocks[0] == 3:
                    for slot in range(4):
                        c.load(sp, slot, "w_ada_3", slot)
                sp.wait_ge(c.x_landed, 16)
                sp.wait_ge(c.par_landed, 16)

            @block.scalar
            def _(act):
                act.dma_start(c.ident[:, :], inputs["ident"]).then_inc(tables, 16)
                act.dma_start(c.masks[:, :, :], inputs["masks"]).then_inc(tables, 16)
                act.dma_start(c.group_ones[:, :], inputs["group_ones"]).then_inc(tables, 16)
                act.dma_start(c.row_par[:, :], inputs["row_params"]).then_inc(tables, 16)
                act.wait_ge(tables, 64)

            @block.vector
            def _(dve):
                dve.memset(c.ones[:, :], 1.0)
                dve.memset(c.ones_d[:, :], 1.0 / D)
                dve.memset(c.rms_eps[:, :], RMS_EPS)
                dve.memset(c.ln_eps[:, :], LN_EPS)
                dve.memset(c.ones_h[:, :], 1.0 / 512)
                dve.wait_ge(tables, 64)
                dve.tensor_scalar(c.masks[:, LEVELS:, :], c.masks[:, LEVELS:, :], 1.0, 1e30, ALU.subtract,
                                  ALU.mult).then_inc(memsets, 1)
        X, H, XR, MR, HR = [tile_of(b) for b in (c.X, c.H, c.XR, c.MR, c.HR)]
        g = lambda name: lambda k: c.vec(name, k)
        scaled_copy = lambda eng, k, n: eng.tensor_scalar(X(k, n), H(k, n), ALPHA, None, ALU.mult)
        ones_d, ln_eps, rms_eps = c.ones_d[:, :], c.ln_eps[:, :], c.rms_eps[:, :]
        pre = ((0, "w_in_2", 0), (1, "w_in_2", 1))
        plan = [
            (1, lambda f: block1_project(c)),
            (1, lambda f: block1_hgrn(c, f(((0, "w_out", 0), (1, "w_out", 1))))),
            (1, lambda f: w_out_stage(c, "out1", "w_out", (), ALPHA)),
            (1, lambda f: layer_norm_stage(c, X, H, KT, ones_d, ln_eps, g("ln1_g"), g("ln1_b"), copies=scaled_copy, hi=MR, lo=HR,
                                           prefetch=f(((0, "w_up", 0), (1, "w_down", 0))))),
            (1, lambda f: ffn_stage(c, "ffn1", "w_up", "w_down", 22, conv=True)),
            (1, lambda f: layer_norm_stage(c, X, X, KT, ones_d, ln_eps, g("ln2_g"), g("ln2_b"))),
            (2, lambda f: layer_norm_stage(c, X, H, KT, ones_d, rms_eps, g("norm_mix_g_2"), centre=False,
                                           hi=XR, lo=HR, spill=True,
                                           prefetch=f(pre))),
            (2, lambda f: block2_project(c)),
            (2, lambda f: layer_norm_stage(c, tile_of(c.M), tile_of(c.M), 4, c.ones_h[:, :], rms_eps,
                                           g("conv_ln_g_2"), g("conv_ln_b_2"), func=ACT.Silu,
                                           prefetch=f(((0, "w_pw_2", 0),)))),
            (2, lambda f: block2_pointwise(c, ())),
            (2, lambda f: block2_attention(c, f(((0, "w_out_2", 0), (1, "w_out_2", 1))))),
            (2, lambda f: w_out_stage(c, "out2", "w_out_2", (), 1.0)),
            (2, lambda f: layer_norm_stage(c, X, H, KT, ones_d, rms_eps, g("norm_ffn_g_2"), centre=False, hi=MR, lo=HR,
                                           prefetch=f(((0, "w_up_2", 0), (1, "w_down_2", 0))))),
            (2, lambda f: ffn_stage(c, "ffn2", "w_up_2", "w_down_2", 16)),
            (2, lambda f: layer_norm_stage(c, X, X, KT, ones_d, rms_eps, g("norm_final_g_2"), centre=False,
                                           prefetch=f(tuple((i, "w_ada_3", i) for i in range(4))))),
        ]
        ada = lambda first, of=0: lambda k: c.ada[:, 2 * (first + k) + of:2 * (first + k) + of + 1]
        ctx_tile = lambda k, n: c.T[:, k // 4, (k % 4) * CTX:(k % 4 + 1) * CTX]
        next_x = lambda eng, k, n: eng.tensor_scalar(X(k, n), X(k, n), ALPHA, c.gate_bias[:, k:k + 1], ALU.mult, ALU.add)
        plan += [
            (3, lambda f: block3_ada(c, f(((0, "w_k_3", 0), (1, "w_gates_3", 0), (2, "w_in_vv_3", 0))))),
            (3, lambda f: layer_norm_stage(c, ctx_tile, ctx_tile, KT, ones_d, ln_eps, ada(8, 1), ada(0, 1),
                                           halves=1, width=CTX, arrive=c.ctx_landed, scratch=False)),
            (3, lambda f: block3_context(c, ())),
            (3, lambda f: layer_norm_stage(c, X, H, KT, ones_d, ln_eps, ada(8), ada(0), scratch=False,
                                           hi=XR, lo=HR, spill=True,
                                           prefetch=f(((0, "w_in_3", 0), (1, "w_in_3", 1))))),
            (3, lambda f: block3_project(c)),
            (3, lambda f: block3_gates(c, ())),
            (3, lambda f: block3_mlstm(c, ())),
            (3, lambda f: block3_head_norm(c, f(((0, "w_out_3", 0), (1, "w_out_3", 1))))),
            (3, lambda f: w_out_stage(c, "out3", "w_out_3", (), None, gate=32)),
            (3, lambda f: layer_norm_stage(c, X, X, KT, ones_d, ln_eps, g("ln1_g_3"), g("ln1_b_3"),
                                           prefetch=f(((0, "w1_3", 0), (1, "w2_3", 0))))),
            (3, lambda f: layer_norm_stage(c, X, H, KT, ones_d, ln_eps, ada(32), ada(24), copies=next_x, hi=MR, lo=HR)),
            (3, lambda f: ffn_stage(c, "ffn3", "w1_3", "w2_3", 16, bias="b1_3", gate=ada(40))),
            (3, lambda f: layer_norm_stage(c, X, X, KT, ones_d, ln_eps, g("ln2_g_3"), g("ln2_b_3"),
                                           store=stored)),
        ]
        todo = [s for b, s in plan if b in blocks][:upto]
        for n, s in enumerate(todo):
            s(lambda loads, n=n: loads if n + 1 < len(todo) else ())


def slabs(w):
    n = w.shape[1] // 256
    return w.reshape(KT, P, n, 256).transpose(2, 1, 0, 3).reshape(n * P, SLAB)


def wide_slab(w):
    return w.reshape(KT, P, HALF).transpose(1, 0, 2).reshape(P, KT * HALF)


def down_slabs(w):
    n = w.shape[0] // 256
    return w.reshape(n, 2, P, D).transpose(0, 2, 1, 3).reshape(n * P, SLAB)


def layouts(a):
    w_in, w2 = a["w_in"][0], a["w_in_2"][0]
    rows = np.zeros((P, 4), np.float32)
    rows[0:8, 0] = a["b_forget_2"][0]
    w3, gates = a["w_in_3"][0], np.zeros((D, P), np.float32)
    for j in range(4):
        rows[32 * j:32 * j + 4, 1] = a["b_gates_3"][0, 4 * j:4 * j + 4]
        gates[:, 32 * j:32 * j + 4] = w3[:, 2560 + 4 * j:2564 + 4 * j]
    sel, sel2 = np.zeros((ROWS, 8, P), np.float32), np.zeros((ROWS, 4, P), np.float32)
    for j in range(8):
        row = 32 * (j // 4) + j % 4
        sel[row, j] = 1.0
        sel2[row, j // 2, 64 * (j % 2):64 * (j % 2) + 64] = 1.0
    cols = []
    for name, n in param_spec():
        cols.append(a[name].reshape(n, P).T)
    s, t = np.arange(P)[:, None], np.arange(P)[None, :]
    masks = []
    for r in range(LEVELS):
        m = 64 >> r
        masks.append((s // (2 * m) == t // (2 * m)) & (s % (2 * m) < m) & (t % (2 * m) >= m))
    masks += [s <= t, s >= t]
    inv = np.stack([1.0 / np.minimum(np.arange(1, 17), 2 ** (g + 1)) for g in range(4)]).reshape(1, 64)
    return {
        "x": a["x"][0].T.reshape(KT, P, T).transpose(1, 0, 2),
        "params": np.concatenate(cols, axis=1),
        "ident": np.eye(P, dtype=np.float32),
        "masks": np.stack(masks, axis=1).astype(np.float32),
        "inv_count": np.repeat(inv, P, axis=0).astype(np.float32),
        "pool_w": a["pool_w"][0].transpose(1, 0, 2).reshape(P, 512),
        "w_in": slabs(np.concatenate([w_in[:, 0:1536], w_in[:, 2048:2560], w_in[:, 1536:2048]], axis=1)),
        "w_out": slabs(a["w_out"][0]),
        "w_up": slabs(np.concatenate([a["w_up"][0].reshape(D, 2, 22, P)[:, s, c] for c in range(22) for s in range(2)], axis=1)),
        "w_down": a["w_down"][0],
        "group_ones": np.kron(np.eye(2), np.full((64, 64), 1.0 / 64)).astype(np.float32),
        "row_params": rows,
        "w_in_2": slabs(np.concatenate([w2[:, 2560:2568], np.zeros((D, 248), np.float32), w2[:, 1536:2560], w2[:, 0:1536]],
                                       axis=1)),
        "w_pw_2": a["w_conv_pw_2"][0].reshape(4, P, 512).transpose(1, 0, 2).reshape(P, SLAB),
        "w_out_2": slabs(a["w_out_2"][0]),
        "w_up_2": slabs(a["w_ffn_up_2"][0]),
        "w_down_2": down_slabs(a["w_ffn_down_2"][0]),
        "w_ada_3": slabs(a["w_ada_3"][0]),
        "ctx": a["ctx_3"][0].T.reshape(KT, P, CTX).transpose(1, 0, 2).reshape(P, KT * CTX),
        "w_k_3": slabs(w3[:, 1280:1536]),
        "w_gates_3": gates.reshape(KT, P, P).transpose(1, 0, 2).reshape(P, KT * P),
        "w_in_3": slabs(np.concatenate([w3[:, 512:1024], w3[:, 0:512], w3[:, 1024:1536], w3[:, 2048:2560],
                                        w3[:, 1536:2048], gates, np.zeros((D, P), np.float32)], axis=1)),
        "w_in_vv_3": wide_slab(w3[:, 1536:2048]),
        "ln_v_rows": np.broadcast_to(np.concatenate([a["ln_v_g_3"][0], a["ln_v_b_3"][0]]), (P, 1024)),
        "w_s_3": a["w_s_3"][0].transpose(2, 0, 1).reshape(P, 512),
        "b_s_3": a["b_s_3"][0].reshape(1, 512),
        "sel": sel.reshape(ROWS, 8 * P),
        "sel2": sel2.reshape(ROWS, 4 * P),
        "w_out_3": slabs(a["w_out_3"][0]),
        "w1_3": slabs(a["w1_3"][0]),
        "w2_3": down_slabs(a["w2_3"][0]),
    }


def kernel(**inputs):
    import concourse.bacc as bacc
    from concourse.bass_utils import run_bass_kernel_spmd

    arrays = layouts({k: np.asarray(v) for k, v in inputs.items()})
    arrays = {k: np.ascontiguousarray(v) for k, v in arrays.items()}
    nc = bacc.Bacc("TRN2", target_bir_lowering=False, num_devices=1)
    aps = {k: nc.dram_tensor(f"in_{k}", v.shape, F32, kind="ExternalInput").ap() for k, v in arrays.items()}
    out = nc.dram_tensor("out", (P, KT, T), F32, kind="ExternalOutput").ap()
    build(nc, aps, out)
    r = run_bass_kernel_spmd(nc, [{f"in_{k}": v for k, v in arrays.items()}], core_ids=[0])
    return r.results[0]["out"].transpose(1, 0, 2).reshape(1, D, T).transpose(0, 2, 1)
```
